# Optimizing a Trainium2 kernel written in Bass

```python
import jax, jax.numpy as jnp
from jax import lax
import numpy as np
import math

D_MODEL = 1024
BATCH = 1
SEQ = 512
DEPTH = 1

NSA_HEADS = 8
NSA_KV_GROUPS = 2
NSA_HEAD_DIM = 64
CMP_LEN = 32
CMP_STRIDE = 16
CMP_HIDDEN = 256
SEL_BLOCK = 64
SEL_TOPK = 16
WINDOW = 512
MLA_HEADS = 8
MLA_NOPE = 64
MLA_ROPE = 32
MLA_V = 64
MLA_Q_RANK = 384
MLA_KV_RANK = 256
ROPE_THETA = 10000.0
D_FF = 4 * D_MODEL
Q_BLOCK = 128
EPS = 1e-6
FORCE_BONUS = 1000.0

NSA_HG = NSA_HEADS // NSA_KV_GROUPS
NSA_Q_DIM = NSA_HEADS * NSA_HEAD_DIM
NSA_KV_DIM = NSA_KV_GROUPS * NSA_HEAD_DIM
IN_SPLITS = (NSA_Q_DIM, NSA_KV_DIM, NSA_KV_DIM, NSA_KV_DIM, NSA_KV_DIM, NSA_KV_DIM, NSA_KV_DIM,
             3 * NSA_HEADS, MLA_Q_RANK, MLA_KV_RANK, MLA_ROPE, D_MODEL, D_MODEL)
IN_DIM = sum(IN_SPLITS)


def rmsnorm(x, g):
    xf = x.astype(jnp.float32)
    y = xf * lax.rsqrt(jnp.mean(xf * xf, axis=-1, keepdims=True) + EPS)
    return (y * g.astype(jnp.float32)).astype(x.dtype)

def modulate(h, shift, scale):
    return h * (1.0 + scale[:, None, :]) + shift[:, None, :]

def masked_softmax(s, mask):
    s = jnp.where(mask, s, -jnp.inf)
    m = jnp.max(s, axis=-1, keepdims=True)
    m = jnp.where(jnp.isfinite(m), m, 0.0)
    e = jnp.exp(s - m)
    return e / jnp.maximum(jnp.sum(e, axis=-1, keepdims=True), 1e-30)

def alibi_slopes(n):
    return 2.0 ** (-8.0 * jnp.arange(1, n + 1, dtype=jnp.float32) / n)

def rope(x, cos, sin):
    half = x.shape[-1] // 2
    x1, x2 = x[..., :half], x[..., half:]
    return jnp.concatenate([x1 * cos - x2 * sin, x2 * cos + x1 * sin], axis=-1).astype(x.dtype)

def compress(kv, pe, w1, w2):
    B, S, G, dh = kv.shape
    r = CMP_LEN // CMP_STRIDE
    n_chunks = S // CMP_STRIDE
    nc = n_chunks - r + 1
    chunks = kv.reshape(B, n_chunks, CMP_STRIDE, G, dh)
    blocks = jnp.concatenate([chunks[:, i:i + nc] for i in range(r)], axis=2)
    blocks = blocks + pe[None, None, :, None, :]
    flat = blocks.transpose(0, 3, 1, 2, 4).reshape(B, G, nc, CMP_LEN * dh)
    return jax.nn.silu(flat @ w1) @ w2

def nsa_attention(q, kc, vc, ks, vs, kw, vw, gates):
    B, G, Hg, S, dh = q.shape
    nc = kc.shape[2]
    ns = S // SEL_BLOCK
    n_sel = min(SEL_TOPK, ns)
    n_key_sel = n_sel * SEL_BLOCK
    scale = dh ** -0.5
    slopes = alibi_slopes(G * Hg).reshape(1, G, Hg, 1, 1)
    c_start = jnp.arange(nc) * CMP_STRIDE
    c_end = c_start + CMP_LEN - 1
    s_start = jnp.arange(ns) * SEL_BLOCK
    overlap = ((c_start[:, None] < s_start[None, :] + SEL_BLOCK)
               & (c_end[:, None] >= s_start[None, :])).astype(jnp.float32)
    ks_blocks = ks.reshape(B, G, ns, SEL_BLOCK, dh)
    vs_blocks = vs.reshape(B, G, ns, SEL_BLOCK, dh)
    kw_pad = jnp.pad(kw, ((0, 0), (0, 0), (WINDOW, 0), (0, 0)))
    vw_pad = jnp.pad(vw, ((0, 0), (0, 0), (WINDOW, 0), (0, 0)))
    blk = jnp.arange(ns)
    in_blk = jnp.arange(SEL_BLOCK)
    win_off = jnp.arange(Q_BLOCK + WINDOW) - WINDOW
    gather = jax.vmap(jax.vmap(lambda kb, ix: kb[ix]))

    def block(qb):
        t0 = qb * Q_BLOCK
        t = t0 + jnp.arange(Q_BLOCK)
        qq = lax.dynamic_slice_in_dim(q, t0, Q_BLOCK, axis=3)
        g = lax.dynamic_slice_in_dim(gates, t0, Q_BLOCK, axis=4)
        dist_c = (t[:, None] - c_end[None, :]).astype(jnp.float32)
        s = jnp.einsum('bghqd,bgkd->bghqk', qq, kc).astype(jnp.float32) * scale - slopes * dist_c
        p_cmp = masked_softmax(s, dist_c >= 0)
        o_cmp = jnp.einsum('bghqk,bgkd->bghqd', p_cmp.astype(vc.dtype), vc)
        p_slc = jnp.einsum('bghqk,ks->bgqs', p_cmp, overlap)
        cur = t // SEL_BLOCK
        valid = blk[None, :] <= cur[:, None]
        forced = (blk[None, :] == 0) | (blk[None, :] >= cur[:, None] - 1)
        score = jnp.where(valid, p_slc + FORCE_BONUS * forced.astype(jnp.float32), -jnp.inf)
        _, idx = lax.top_k(score, n_sel)
        spos = idx[..., None] * SEL_BLOCK + in_blk
        smask = (spos <= t[:, None, None]).reshape(B, G, Q_BLOCK, n_key_sel)
        dist_s = (t[:, None, None] - spos).reshape(B, G, Q_BLOCK, n_key_sel).astype(jnp.float32)
        k_sel = gather(ks_blocks, idx).reshape(B, G, Q_BLOCK, n_key_sel, dh)
        v_sel = gather(vs_blocks, idx).reshape(B, G, Q_BLOCK, n_key_sel, dh)
        s = jnp.einsum('bghqd,bgqkd->bghqk', qq, k_sel).astype(jnp.float32) * scale - slopes * dist_s[:, :, None]
        p = masked_softmax(s, smask[:, :, None])
        o_sel = jnp.einsum('bghqk,bgqkd->bghqd', p.astype(vs.dtype), v_sel)
        k_win = lax.dynamic_slice_in_dim(kw_pad, t0, Q_BLOCK + WINDOW, axis=2)
        v_win = lax.dynamic_slice_in_dim(vw_pad, t0, Q_BLOCK + WINDOW, axis=2)
        wpos = t0 + win_off
        dist_w = t[:, None] - wpos[None, :]
        wmask = (dist_w >= 0) & (dist_w < WINDOW) & (wpos[None, :] >= 0)
        s = jnp.einsum('bghqd,bgkd->bghqk', qq, k_win).astype(jnp.float32) * scale - slopes * dist_w.astype(jnp.float32)
        p = masked_softmax(s, wmask)
        o_win = jnp.einsum('bghqk,bgkd->bghqd', p.astype(vw.dtype), v_win)
        o = g[0] * o_cmp + g[1] * o_sel + g[2] * o_win
        return o.transpose(0, 3, 1, 2, 4).reshape(B, Q_BLOCK, G * Hg * dh)

    out = lax.map(block, jnp.arange(S // Q_BLOCK))
    return out.transpose(1, 0, 2, 3).reshape(B, S, G * Hg * dh)

def mla_attention(q, k, v):
    B, H, S, dqk = q.shape
    dv = v.shape[-1]
    scale = dqk ** -0.5
    kpos = jnp.arange(S)

    def block(qb):
        t0 = qb * Q_BLOCK
        t = t0 + jnp.arange(Q_BLOCK)
        qq = lax.dynamic_slice_in_dim(q, t0, Q_BLOCK, axis=2)
        s = jnp.einsum('bhqd,bhkd->bhqk', qq, k).astype(jnp.float32) * scale
        p = masked_softmax(s, kpos[None, :] <= t[:, None])
        o = jnp.einsum('bhqk,bhkd->bhqd', p.astype(v.dtype), v)
        return o.transpose(0, 2, 1, 3).reshape(B, Q_BLOCK, H * dv)

    out = lax.map(block, jnp.arange(S // Q_BLOCK))
    return out.transpose(1, 0, 2, 3).reshape(B, S, H * dv)

def first_inputs(seed: int = 0) -> dict:
    key = jax.random.key(seed)
    ks = jax.random.split(key, 24)
    f32 = jnp.float32

    def nrm(k, shape, scale):
        return jax.random.normal(k, (DEPTH,) + shape, f32) * scale

    def gain(k, n):
        return 1.0 + 0.05 * jax.random.normal(k, (DEPTH, n), f32)

    dqk = MLA_NOPE + MLA_ROPE
    return {
        'x': jax.random.normal(ks[0], (BATCH, SEQ, D_MODEL), f32),
        'c': jax.random.normal(ks[1], (BATCH, D_MODEL), f32),
        'w_ada': nrm(ks[2], (D_MODEL, 6 * D_MODEL), 0.5 * D_MODEL ** -0.5),
        'b_ada': nrm(ks[3], (6 * D_MODEL,), 0.01),
        'g_mix': gain(ks[4], D_MODEL),
        'w_in': nrm(ks[5], (D_MODEL, IN_DIM), D_MODEL ** -0.5),
        'pe_ck': nrm(ks[6], (CMP_LEN, NSA_HEAD_DIM), 0.1),
        'w_ck1': nrm(ks[7], (CMP_LEN * NSA_HEAD_DIM, CMP_HIDDEN), (CMP_LEN * NSA_HEAD_DIM) ** -0.5),
        'w_ck2': nrm(ks[8], (CMP_HIDDEN, NSA_HEAD_DIM), CMP_HIDDEN ** -0.5),
        'pe_cv': nrm(ks[9], (CMP_LEN, NSA_HEAD_DIM), 0.1),
        'w_cv1': nrm(ks[10], (CMP_LEN * NSA_HEAD_DIM, CMP_HIDDEN), (CMP_LEN * NSA_HEAD_DIM) ** -0.5),
        'w_cv2': nrm(ks[11], (CMP_HIDDEN, NSA_HEAD_DIM), CMP_HIDDEN ** -0.5),
        'g_cq': gain(ks[12], MLA_Q_RANK),
        'w_uq': nrm(ks[13], (MLA_Q_RANK, MLA_HEADS * dqk), MLA_Q_RANK ** -0.5),
        'g_ckv': gain(ks[14], MLA_KV_RANK),
        'w_uk': nrm(ks[15], (MLA_KV_RANK, MLA_HEADS * MLA_NOPE), MLA_KV_RANK ** -0.5),
        'w_uv': nrm(ks[16], (MLA_KV_RANK, MLA_HEADS * MLA_V), MLA_KV_RANK ** -0.5),
        'w_o_nsa': nrm(ks[17], (NSA_Q_DIM, D_MODEL), NSA_Q_DIM ** -0.5),
        'w_o_mla': nrm(ks[18], (MLA_HEADS * MLA_V, D_MODEL), (MLA_HEADS * MLA_V) ** -0.5),
        'w_out': nrm(ks[19], (D_MODEL, D_MODEL), D_MODEL ** -0.5),
        'g_mlp': gain(ks[20], D_MODEL),
        'w_fc1': nrm(ks[21], (D_MODEL, D_FF), D_MODEL ** -0.5),
        'w_fc2': nrm(ks[22], (D_FF, D_MODEL), D_FF ** -0.5),
        'g_final': 1.0 + 0.05 * jax.random.normal(ks[23], (D_MODEL,), f32),
    }

def first_block(x, c, w_ada, b_ada, g_mix, w_in, pe_ck, w_ck1, w_ck2, pe_cv, w_cv1, w_cv2,
              g_cq, w_uq, g_ckv, w_uk, w_uv, w_o_nsa, w_o_mla, w_out, g_mlp, w_fc1, w_fc2, g_final):
    B, S, _ = x.shape
    G, Hg, dh = NSA_KV_GROUPS, NSA_HG, NSA_HEAD_DIM
    split_points = np.cumsum(IN_SPLITS)[:-1].tolist()
    half = MLA_ROPE // 2
    pos = jnp.arange(S, dtype=jnp.float32)
    inv_freq = ROPE_THETA ** (-jnp.arange(half, dtype=jnp.float32) / half)
    ang = pos[:, None] * inv_freq[None, :]
    cos, sin = jnp.cos(ang), jnp.sin(ang)

    def kv_groups(t):
        return t.reshape(B, S, G, dh)

    for layer in range(DEPTH):
        mod = c @ w_ada[layer] + b_ada[layer]
        sh_a, sc_a, gt_a, sh_m, sc_m, gt_m = jnp.split(mod, 6, axis=-1)

        h = modulate(rmsnorm(x, g_mix[layer]), sh_a, sc_a)
        z = h @ w_in[layer]
        (zq, zkc, zvc, zks, zvs, zkw, zvw, zg, zqd, zkvd, zkr, zga, zgb) = jnp.split(z, split_points, axis=-1)

        q_nsa = zq.reshape(B, S, G, Hg, dh).transpose(0, 2, 3, 1, 4)
        kc = compress(kv_groups(zkc), pe_ck[layer], w_ck1[layer], w_ck2[layer])
        vc = compress(kv_groups(zvc), pe_cv[layer], w_cv1[layer], w_cv2[layer])
        k_s = kv_groups(zks).transpose(0, 2, 1, 3)
        v_s = kv_groups(zvs).transpose(0, 2, 1, 3)
        k_w = kv_groups(zkw).transpose(0, 2, 1, 3)
        v_w = kv_groups(zvw).transpose(0, 2, 1, 3)
        nsa_gates = jax.nn.sigmoid(zg).reshape(B, S, 3, G, Hg).transpose(2, 0, 3, 4, 1)[..., None]
        o_nsa = nsa_attention(q_nsa, kc, vc, k_s, v_s, k_w, v_w, nsa_gates)

        cq = rmsnorm(zqd, g_cq[layer])
        qm = (cq @ w_uq[layer]).reshape(B, S, MLA_HEADS, MLA_NOPE + MLA_ROPE)
        q_rot = rope(qm[..., MLA_NOPE:], cos[:, None, :], sin[:, None, :])
        q_mla = jnp.concatenate([qm[..., :MLA_NOPE], q_rot], axis=-1)
        ckv = rmsnorm(zkvd, g_ckv[layer])
        k_nope = (ckv @ w_uk[layer]).reshape(B, S, MLA_HEADS, MLA_NOPE)
        v_mla = (ckv @ w_uv[layer]).reshape(B, S, MLA_HEADS, MLA_V)
        k_rot = rope(zkr, cos, sin)
        k_mla = jnp.concatenate(
            [k_nope, jnp.broadcast_to(k_rot[:, :, None, :], (B, S, MLA_HEADS, MLA_ROPE))], axis=-1)
        o_mla = mla_attention(q_mla.transpose(0, 2, 1, 3), k_mla.transpose(0, 2, 1, 3),
                              v_mla.transpose(0, 2, 1, 3))

        y = jax.nn.sigmoid(zga) * (o_nsa @ w_o_nsa[layer]) + jax.nn.sigmoid(zgb) * (o_mla @ w_o_mla[layer])
        x = x + gt_a[:, None, :] * (y @ w_out[layer])

        h = modulate(rmsnorm(x, g_mlp[layer]), sh_m, sc_m)
        x = x + gt_m[:, None, :] * (jnp.square(jax.nn.relu(h @ w_fc1[layer])) @ w_fc2[layer])

    return rmsnorm(x, g_final)


MIX_WIDTH = D_MODEL
M_HEADS = 4
M_HEAD_DIM = (MIX_WIDTH // 2) // M_HEADS
M_WIDTH = M_HEADS * M_HEAD_DIM
CONV_WIDTH = 4
CHUNK = 64
D_HEADS = 4
D_HEAD_DIM = (MIX_WIDTH // 2) // (2 * D_HEADS)
D_WIDTH = D_HEADS * 2 * D_HEAD_DIM
P_HEADS = 8
N_KEYS = 128
N_EXPERTS = N_KEYS * N_KEYS
P_TOPK = 16
P_QUERY_DIM = 256
P_HALF = P_QUERY_DIM // 2
TOKEN_BLOCK = 128

NEG = -1e30


def rmsnorm_2(x, g):
    xf = x.astype(jnp.float32)
    y = xf * lax.rsqrt(jnp.mean(xf * xf, axis=-1, keepdims=True) + EPS)
    return (y * g.astype(jnp.float32)).astype(x.dtype)

def causal_dwconv(u, w, b):
    C = u.shape[-1]
    y = lax.conv_general_dilated(
        u, w[:, None, :].astype(u.dtype), window_strides=(1,),
        padding=[(CONV_WIDTH - 1, 0)],
        dimension_numbers=("NWC", "WIO", "NWC"),
        feature_group_count=C)
    return y + b.astype(u.dtype)

def mlstm_chunkwise(q, k, v, ig, lf):
    Bb, H, S, d = q.shape
    nc = S // CHUNK

    def to_chunks(a):
        a = a.reshape(a.shape[:2] + (nc, CHUNK) + a.shape[3:])
        return jnp.moveaxis(a, 2, 0)

    qc, kc, vc, ic, fc = (to_chunks(a) for a in (q, k, v, ig, lf))
    causal = jnp.tril(jnp.ones((CHUNK, CHUNK), dtype=bool))

    def step(carry, inp):
        C, n, m = carry
        qb, kb, vb, ib, fb = inp
        b = jnp.cumsum(fb, axis=-1)
        logD = jnp.where(causal, b[..., :, None] - b[..., None, :] + ib[..., None, :], -jnp.inf)
        m_t = jnp.maximum(b + m[..., None], jnp.max(logD, axis=-1))
        Dw = jnp.exp(logD - m_t[..., None])
        inter = jnp.exp(b + m[..., None] - m_t)
        sqk = jnp.einsum('bhtd,bhsd->bhts', qb, kb) * Dw
        num = (jnp.einsum('bhts,bhsv->bhtv', sqk, vb)
               + inter[..., None] * jnp.einsum('bhtd,bhdv->bhtv', qb, C))
        den = jnp.sum(sqk, axis=-1) + inter * jnp.einsum('bhtd,bhd->bht', qb, n)
        h = num / jnp.maximum(jnp.abs(den), jnp.exp(-m_t))[..., None]
        bL = b[..., -1]
        logw = bL[..., None] - b + ib
        m_new = jnp.maximum(bL + m, jnp.max(logw, axis=-1))
        w = jnp.exp(logw - m_new[..., None])
        decay = jnp.exp(bL + m - m_new)
        C_new = decay[..., None, None] * C + jnp.einsum('bhs,bhsd,bhsv->bhdv', w, kb, vb)
        n_new = decay[..., None] * n + jnp.einsum('bhs,bhsd->bhd', w, kb)
        return (C_new, n_new, m_new), h

    init = (jnp.zeros((Bb, H, d, d), jnp.float32),
            jnp.zeros((Bb, H, d), jnp.float32),
            jnp.zeros((Bb, H), jnp.float32))
    _, hs = lax.scan(step, init, (qc, kc, vc, ic, fc))
    return jnp.moveaxis(hs, 0, 2).reshape(Bb, H, S, d)

def diff_attention(q, k, v, lam):
    Bb, H, _, S, dh = q.shape
    nb = S // Q_BLOCK
    kpos = jnp.arange(S)
    scale = D_HEAD_DIM ** -0.5

    def block(i):
        qb = lax.dynamic_slice_in_dim(q, i * Q_BLOCK, Q_BLOCK, axis=3)
        s = jnp.einsum('bhptd,bhpsd->bhpts', qb, k) * scale
        qpos = i * Q_BLOCK + jnp.arange(Q_BLOCK)
        mask = kpos[None, :] <= qpos[:, None]
        a = jax.nn.softmax(jnp.where(mask, s, NEG), axis=-1)
        att = a[:, :, 0] - lam * a[:, :, 1]
        return jnp.einsum('bhts,bhsv->bhtv', att, v)

    o = lax.map(block, jnp.arange(nb))
    return jnp.moveaxis(o, 0, 2).reshape(Bb, H, S, v.shape[-1])

def peer(h, w_query, sub_keys, u_tab, v_tab):
    Bb, S, D = h.shape
    xt = h.reshape(-1, TOKEN_BLOCK, D)

    def block(xb):
        q = (xb @ w_query).reshape(TOKEN_BLOCK, P_HEADS, 2, P_HALF)
        s = jnp.einsum('thpk,hpnk->thpn', q, sub_keys).astype(jnp.float32)
        sv, si = lax.top_k(s, P_TOPK)
        cand = (sv[:, :, 0, :, None] + sv[:, :, 1, None, :]).reshape(TOKEN_BLOCK, P_HEADS, P_TOPK * P_TOPK)
        cidx = (si[:, :, 0, :, None] * N_KEYS + si[:, :, 1, None, :]).reshape(TOKEN_BLOCK, P_HEADS, P_TOPK * P_TOPK)
        fv, fpos = lax.top_k(cand, P_TOPK)
        eidx = jnp.take_along_axis(cidx, fpos, axis=-1)
        g = jax.nn.softmax(fv, axis=-1)
        u = u_tab[eidx]
        act = jax.nn.gelu(jnp.einsum('td,thkd->thk', xb, u).astype(jnp.float32), approximate=False)
        return jnp.einsum('thk,thkd->td', (g * act).astype(xb.dtype), v_tab[eidx])

    return lax.map(block, xt).reshape(Bb, S, D)

def second_inputs(seed: int = 0) -> dict:
    key = jax.random.key(seed)
    ks = jax.random.split(key, 24)
    L, D = DEPTH, D_MODEL
    n_in = 4 * M_WIDTH + 2 * M_HEADS + 3 * D_WIDTH
    nrm = lambda k, shape, s: jax.random.normal(k, shape, jnp.float32) * s
    f_bias = jnp.linspace(3.0, 6.0, M_HEADS, dtype=jnp.float32)
    gate_b = jnp.concatenate([
        nrm(ks[7], (L, M_HEADS), 0.1),
        f_bias[None, :] + nrm(ks[8], (L, M_HEADS), 0.1)], axis=-1)
    return {
        "x": nrm(ks[0], (BATCH, SEQ, D), 1.0),
        "c": nrm(ks[1], (BATCH, D), 1.0),
        "ada_w": nrm(ks[2], (L, D, 6 * D), 0.5 * D ** -0.5),
        "ada_b": nrm(ks[3], (L, 6 * D), 0.02),
        "norm1_g": 1.0 + nrm(ks[4], (L, D), 0.02),
        "w_in": nrm(ks[5], (L, D, n_in), D ** -0.5),
        "conv_w": nrm(ks[6], (L, CONV_WIDTH, 2 * M_WIDTH), CONV_WIDTH ** -0.5),
        "conv_b": nrm(ks[9], (L, 2 * M_WIDTH), 0.02),
        "mlstm_gate_b": gate_b,
        "mlstm_norm_g": 1.0 + nrm(ks[10], (L, M_WIDTH), 0.02),
        "lambda_q1": nrm(ks[11], (L, D_HEAD_DIM), 0.1),
        "lambda_k1": nrm(ks[12], (L, D_HEAD_DIM), 0.1),
        "lambda_q2": nrm(ks[13], (L, D_HEAD_DIM), 0.1),
        "lambda_k2": nrm(ks[14], (L, D_HEAD_DIM), 0.1),
        "diff_norm_g": 1.0 + nrm(ks[15], (L, 2 * D_HEAD_DIM), 0.02),
        "w_out": nrm(ks[16], (L, MIX_WIDTH, D), MIX_WIDTH ** -0.5),
        "norm2_g": 1.0 + nrm(ks[17], (L, D), 0.02),
        "peer_w_query": nrm(ks[18], (L, D, P_HEADS * P_QUERY_DIM), D ** -0.5),
        "peer_sub_keys": nrm(ks[19], (L, P_HEADS, 2, N_KEYS, P_HALF), P_HALF ** -0.5),
        "peer_u": nrm(ks[20], (L, N_EXPERTS, D), D ** -0.5),
        "peer_v": nrm(ks[21], (L, N_EXPERTS, D), 0.1),
        "final_g": 1.0 + nrm(ks[22], (D,), 0.02),
    }

def second_block(x, c, ada_w, ada_b, norm1_g, w_in, conv_w, conv_b, mlstm_gate_b,
              mlstm_norm_g, lambda_q1, lambda_k1, lambda_q2, lambda_k2, diff_norm_g,
              w_out, norm2_g, peer_w_query, peer_sub_keys, peer_u, peer_v, final_g):
    Bb, S, D = x.shape
    split_pts = [M_WIDTH, 2 * M_WIDTH, 3 * M_WIDTH, 4 * M_WIDTH,
                 4 * M_WIDTH + M_HEADS, 4 * M_WIDTH + 2 * M_HEADS,
                 4 * M_WIDTH + 2 * M_HEADS + D_WIDTH,
                 4 * M_WIDTH + 2 * M_HEADS + 2 * D_WIDTH]
    for l in range(DEPTH):
        mod = jax.nn.silu(c) @ ada_w[l] + ada_b[l]
        sh1, sc1, g1, sh2, sc2, g2 = jnp.split(mod[:, None, :], 6, axis=-1)

        h = rmsnorm_2(x, norm1_g[l]) * (1.0 + sc1) + sh1
        p = h @ w_in[l]
        mq, mk, mv, mo, mi, mf, dq, dk, dv = jnp.split(p, split_pts, axis=-1)

        qk = jax.nn.silu(causal_dwconv(jnp.concatenate([mq, mk], axis=-1), conv_w[l], conv_b[l]))
        mq, mk = jnp.split(qk, 2, axis=-1)
        heads = lambda a: a.reshape(Bb, S, M_HEADS, M_HEAD_DIM).transpose(0, 2, 1, 3).astype(jnp.float32)
        q_m = heads(mq)
        k_m = heads(mk) * (M_HEAD_DIM ** -0.5)
        v_m = heads(mv)
        gb = mlstm_gate_b[l].astype(jnp.float32)
        ig = (mi.astype(jnp.float32) + gb[:M_HEADS]).transpose(0, 2, 1)
        lf = jax.nn.log_sigmoid(mf.astype(jnp.float32) + gb[M_HEADS:]).transpose(0, 2, 1)
        hm = mlstm_chunkwise(q_m, k_m, v_m, ig, lf).transpose(0, 2, 1, 3)
        hm = rmsnorm_2(hm, mlstm_norm_g[l].reshape(M_HEADS, M_HEAD_DIM)).reshape(Bb, S, M_WIDTH)
        hm = (hm * jax.nn.sigmoid(mo.astype(jnp.float32))).astype(x.dtype)

        lam_init = 0.8 - 0.6 * math.exp(-0.3 * l)
        lam = (jnp.exp(jnp.sum(lambda_q1[l].astype(jnp.float32) * lambda_k1[l].astype(jnp.float32)))
               - jnp.exp(jnp.sum(lambda_q2[l].astype(jnp.float32) * lambda_k2[l].astype(jnp.float32)))
               + lam_init)
        qk_heads = lambda a: a.reshape(Bb, S, D_HEADS, 2, D_HEAD_DIM).transpose(0, 2, 3, 1, 4).astype(jnp.float32)
        q_d, k_d = qk_heads(dq), qk_heads(dk)
        v_d = dv.reshape(Bb, S, D_HEADS, 2 * D_HEAD_DIM).transpose(0, 2, 1, 3).astype(jnp.float32)
        od = diff_attention(q_d, k_d, v_d, lam)
        od = rmsnorm_2(od, diff_norm_g[l]) * (1.0 - lam_init)
        od = od.transpose(0, 2, 1, 3).reshape(Bb, S, D_WIDTH).astype(x.dtype)

        y = jnp.concatenate([hm, od], axis=-1) @ w_out[l]
        x = x + g1 * y

        h2 = rmsnorm_2(x, norm2_g[l]) * (1.0 + sc2) + sh2
        x = x + g2 * peer(h2, peer_w_query[l], peer_sub_keys[l], peer_u[l], peer_v[l])

    return rmsnorm_2(x, final_g)


def setup_inputs(seed=0):
    out = dict(first_inputs(seed))
    for name, value in second_inputs(seed + 1).items():
        if name != "x":
            out[name + "_2"] = value
    return out


def reference(
    x, c, w_ada, b_ada, g_mix, w_in, pe_ck, w_ck1, w_ck2, pe_cv, w_cv1, w_cv2, g_cq, w_uq,
    g_ckv, w_uk, w_uv, w_o_nsa, w_o_mla, w_out, g_mlp, w_fc1, w_fc2, g_final, c_2, ada_w_2,
    ada_b_2, norm1_g_2, w_in_2, conv_w_2, conv_b_2, mlstm_gate_b_2, mlstm_norm_g_2, lambda_q1_2,
    lambda_k1_2, lambda_q2_2, lambda_k2_2, diff_norm_g_2, w_out_2, norm2_g_2, peer_w_query_2,
    peer_sub_keys_2, peer_u_2, peer_v_2, final_g_2,
):
    x = first_block(
        x, c, w_ada, b_ada, g_mix, w_in, pe_ck, w_ck1, w_ck2, pe_cv, w_cv1, w_cv2, g_cq, w_uq,
        g_ckv, w_uk, w_uv, w_o_nsa, w_o_mla, w_out, g_mlp, w_fc1, w_fc2, g_final,
    )
    return second_block(
        x, c_2, ada_w_2, ada_b_2, norm1_g_2, w_in_2, conv_w_2, conv_b_2, mlstm_gate_b_2,
        mlstm_norm_g_2, lambda_q1_2, lambda_k1_2, lambda_q2_2, lambda_k2_2, diff_norm_g_2,
        w_out_2, norm2_g_2, peer_w_query_2, peer_sub_keys_2, peer_u_2, peer_v_2, final_g_2,
    )


_drawn_inputs = setup_inputs


def setup_inputs(seed=0):
    import zlib

    import numpy as np

    out = dict(_drawn_inputs(seed))
    spreads = {}
    factors = {'b_ada': 3.286,
     'g_mix': 4.855,
     'pe_ck': 8.0,
     'w_ck1': 2.669,
     'pe_cv': 6.224,
     'g_cq': 8.0,
     'g_ckv': 8.0,
     'ada_b_2': 3.416,
     'norm1_g_2': 8.0,
     'conv_b_2': 25.184,
     'mlstm_norm_g_2': 8.0,
     'lambda_q1_2': 3.866,
     'lambda_k1_2': 3.61,
     'lambda_q2_2': 4.738,
     'lambda_k2_2': 4.072,
     'diff_norm_g_2': 8.0,
     'norm2_g_2': 8.0,
     'peer_w_query_2': 3.432,
     'peer_sub_keys_2': 3.425,
     'peer_u_2': 3.867,
     'peer_v_2': 3.453,
     'final_g_2': 8.416}
    for name, (base, spread) in spreads.items():
        noise = np.random.default_rng([zlib.crc32(name.encode()), seed]).standard_normal(out[name].shape)
        drawn = base * np.exp(spread * noise) if base else spread * noise
        out[name] = __import__('jax').numpy.asarray(drawn.astype(out[name].dtype))
    for name, factor in factors.items():
        out[name] = (out[name] * factor).astype(out[name].dtype)
    return out
```

```python
from contextlib import ExitStack

import numpy as np

import concourse.bass as bass
from concourse import mybir

ALU = mybir.AluOpType
ACT = mybir.ActivationFunctionType
AXX = mybir.AxisListType.X
F32 = mybir.dt.float32
U32 = mybir.dt.uint32

P = 128
D = 1024
S = 512
T = S // P
KD = D // P
FF = 4 * D
EPS = 1e-6
BIG = 1e30
NH, NG, HG, DH = 8, 2, 4, 64
NC = S // 16 - 1
CMP_END0, CMP_STRIDE = 31, 16
MLA_SCALE = 96.0 ** -0.5
NSA_SCALE = 64.0 ** -0.5
MH = 4
PH, PK, NKEY = 8, 16, 128
NEXP = NKEY * NKEY
NSLOT = PH * PK
GRP = 8
BLK = 4096

STREAM = [
    ("ada_a", [(1, 0)] * 4), ("in1", [(4, 4)] * 3 + [(6, 6)]), ("uq", [(8, 8)]), ("ukv", [(8, 8)]),
    ("ck", [(1, 0)]), ("cv", [(1, 0)]), ("gab", [(4, 4)] * 4), ("ada_b", [(1, 0)] * 8),
    ("on", [(8, 8)]), ("om", [(8, 8)]), ("out1", [(4, 4)] * 2), ("fc1", [(4, 4)] * 8),
    ("fc2", [(1, 1)] * 8), ("ada_c", [(1, 0)] * 12),
    ("in2", [(4, 4)] * 5 + [(1, 1)] + [(4, 4)] * 2), ("out2", [(4, 4)] * 2), ("pq", [(4, 4)] * 4),
    ("sk", [(T, 0)]),
]
BLOCK0, MM0, EV0, MM_THROUGH = {}, {}, {}, []
_b = _m = _e = 0
for _name, _blocks in STREAM:
    BLOCK0[_name], MM0[_name], EV0[_name] = _b, _m, _e
    for _mm, _ev in _blocks:
        _b, _m, _e = _b + 1, _m + _mm, _e + _ev
        MM_THROUGH.append(_m)
NBLK = _b

PARAMS = [("c", 8), ("b_ada", 48), ("g_mix", 8), ("g_mlp", 8), ("g_cq", 3), ("g_ckv", 2), ("c2", 8),
          ("ada_b2", 48), ("n1g", 8), ("n2g", 8), ("convw", 32), ("convb", 8), ("mng", 4), ("dng", 1),
          ("ck2", 128), ("cv2", 128), ("pek", 16), ("pev", 16), ("gb_i", 1), ("gb_f", 1), ("g_final", 8), ("lam", 256)]
PCOL, _o = {}, 0
for _n, _w in PARAMS:
    PCOL[_n] = _o
    _o += _w
NPRM = _o
CONSTS = [("ident", 128), ("mask", 512), ("rope", 512), ("sel", 512), ("iota", 16)]
CCOL, _o = {}, 0
for _n, _w in CONSTS:
    CCOL[_n] = _o
    _o += _w
NCST = _o

NORMS = [("x", 8), ("cq", 3), ("ckv", 2), ("mid", 8), ("fin", 8), ("n1", 8), ("n2", 8)]
NORM0, _o = {}, 0
for _i, (_n, _w) in enumerate(NORMS):
    NORM0[_n] = (_o, _i)
    _o += _w


def build(nc, ap, out):
    with ExitStack() as ctx:
        def sb(name, shape, dt=F32):
            return ctx.enter_context(nc.sbuf_tensor(name, shape, dt))

        def sem(name):
            return ctx.enter_context(nc.semaphore(name))

        PS = ctx.enter_context(nc.psum_tensor("PS", [P, 8, 512], F32))
        ring = [sb(f"ring{i}", [P, BLK]) for i in range(2)]
        xT = sb("xT", [P, KD, S])
        hT = sb("hT", [P, KD, S])
        prm = sb("prm", [P, NPRM])
        cst = sb("cst", [P, NCST])
        ones = sb("ones", [P, P])
        sq = sb("sq", [P, 2, S])
        rstd = sb("rstd", [P, S])
        modc = sb("modc", [P, 48])
        scl = sb("scl", [P, 16])
        smalls = sb("smalls", [P, 512])
        ARENA = 32100
        arena = sb("arena", [P, ARENA])

        def area(kib, *dims, parts=P):
            n = int(np.prod(dims))
            o = int(kib * 256)
            assert o + n <= ARENA, (kib, dims)
            a = arena[0:parts, o:o + n]
            if len(dims) == 2:
                return a.rearrange("p (a b) -> p a b", a=dims[0])
            if len(dims) == 3:
                return a.rearrange("p (a b c) -> p a b c", a=dims[0], b=dims[1])
            return a

        def prow(name, a=0, b=None, rows=slice(0, P)):
            w = dict(PARAMS)[name]
            return prm[rows, PCOL[name] + a:PCOL[name] + (w if b is None else b)]

        def const(name, rows=slice(0, P)):
            return cst[rows, CCOL[name]:CCOL[name] + dict(CONSTS)[name]]

        ident = const("ident")
        mask = const("mask")

        zT = area(0, 14, S)
        vtok = area(28, T, 256)
        qm = area(32, 8, S)
        km = area(48, 8, S)
        vm = area(64, T, S)
        alibi = area(72, 8, S)
        biasc = area(88, T, 8, NC)
        onT = area(92, 4, S)
        omT = area(100, 4, S)
        sneg = area(108, 2, S)
        prob = area(112, 2, S)
        probT = area(116, 2, S)
        otok = area(120, S)
        otmp = area(122, S)
        cqT = area(108, 3, S)
        ckvT = area(114, 2, S)
        rt = area(118, 2, S)
        stk = [area(108, 2, S), area(112, 2, S)]
        gT = area(0, 16, S)
        yT = area(32, 8, S)
        ytmp = area(48, 2, S)
        aT = area(0, 32, S)
        rbuf = area(64, 2, S)
        uT = area(0, 8, S + 3)
        qk2 = area(17, 8, S)
        mo = area(33, 4, S)
        dqk = area(41, 8, S)
        mv = area(57, T, S)
        dv = area(65, T, S)
        zG = area(73, S)
        grow = area(75, 8, S)
        abc = area(91, 4, S)
        abcm = area(99, 4, S)
        catT = hT
        pq = area(0, 16, S)
        sc = area(32, 16, NKEY)
        sc2 = area(40, 16, NKEY)
        cand = area(48, PH, PK * PK)
        cand2 = area(56, PH, PK * PK)
        oneh = area(64, NSLOT, PK)
        oneh2 = area(72, NSLOT, PK)
        xtok = area(80, T, D)
        h2tok = area(96, T, D)
        eidx = area(112, T, NSLOT).bitcast(U32)
        gate = area(114, T, NSLOT)
        dots = area(116, NSLOT)
        wexp = area(117, T, NSLOT)
        tkv = area(119, 16, PK)
        tki = area(120, 16, PK).bitcast(U32)
        tkf = area(121, 16, PK)
        fpos = area(122, NSLOT).bitcast(U32)
        fpi = area(122.5, NSLOT).bitcast(U32)
        fpf = area(123, NSLOT)
        fval = area(123.5, NSLOT)
        selv = area(124, 2, NSLOT)
        sm8 = area(125, 4, PH)
        ubuf = area(0, GRP, D)
        acc = area(32, 2, D)
        g2row = area(40, D)
        fgrow = area(44, D)

        def small(a, n, rows=slice(0, P)):
            return smalls[rows, a:a + n]

        hid = small(0, 124)
        hb = small(124, 2)
        kcT = small(126, NC)
        vcm = small(157, 128)
        gtok = small(285, 96)
        rs = small(381, 48)
        nmx = small(429, 2)
        coef = small(431, 24)
        tok8 = small(0, 32)
        lamc = small(32, 8)
        ss4 = small(40, 16)
        dots8 = small(60, 8)
        w8 = small(68, 8)
        idx8 = small(76, 8).bitcast(U32)
        ssf = small(84, 4)

        loaded = sem("loaded")
        ready = sem("constants_ready")
        w_loaded = [sem("w_loaded0"), sem("w_loaded1")]
        mm_done = sem("mm_done")
        evac = sem("evac")
        stage_done = sem("stage_done")
        act_own = sem("act_own")
        dve_own = sem("dve_own")
        nrm_sq, nrm_mm, nrm_ms, nrm_rt, nrm_h = (sem(n) for n in ("nrm_sq", "nrm_mm", "nrm_ms", "nrm_rt", "nrm_h"))
        stored = sem("stored")

        class Own:

            def __init__(self, eng, s):
                self.eng, self.s, self.n = eng, s, 0

            def __call__(self, ins):
                self.n += 1
                ins.then_inc(self.s, 1)
                self.eng.wait_ge(self.s, self.n)

            def mark(self, ins):
                self.n += 1
                ins.then_inc(self.s, 1)

            def wait(self):
                self.eng.wait_ge(self.s, self.n)

        fences = {}

        def fence(eng, name):
            k = fences[name] = fences.get(name, 0) + 1
            eng.drain().then_inc(stage_done, 1)
            eng.wait_ge(stage_done, 3 * k)

        def tile(i):
            return slice(i * P, (i + 1) * P)

        def bank(b, n=512, rows=slice(0, P)):
            return PS[rows, b, 0:n]

        def block_arrived(pe, n):
            pe.wait_ge(w_loaded[n % 2], 16 * (n // 2 + 1))

        def norm_act(act, name, src, n, dst=None, shift=None):
            b, k = NORM0[name]
            for c in range(n):
                if b + c >= 2:
                    act.wait_ge(nrm_mm, b + c - 1)
                act.activation(sq[:, c % 2, :], src(c), ACT.Square).then_inc(nrm_sq, 1)
            act.wait_ge(nrm_ms, k + 1)
            act.activation(rstd[:, :], rstd[:, :], ACT.Sqrt).then_inc(nrm_rt, 1)
            if shift is not None:
                for c in range(n):
                    act.wait_ge(nrm_h, b + c + 1)
                    act.activation(dst(c), dst(c), ACT.Identity, bias=shift(c))

        def norm_pe(pe, name, n):
            b, k = NORM0[name]
            if k:
                pe.wait_ge(nrm_ms, k)
            for c in range(n):
                pe.wait_ge(nrm_sq, b + c + 1)
                pe.matmul(bank(7), ones[:, :], sq[:, c % 2, :], start=(c == 0), stop=(c == n - 1)).then_inc(nrm_mm, 1)

        def norm_dve(dve, own, name, src, n, dst, gain):
            b, k = NORM0[name]
            dve.wait_ge(nrm_mm, b + n)
            if b:
                dve.wait_ge(nrm_h, b)
            dve.tensor_scalar(rstd[:, :], bank(7), 1.0 / (n * P), EPS, ALU.mult, ALU.add).then_inc(nrm_ms, 1)
            dve.wait_ge(nrm_rt, k + 1)
            own(dve.reciprocal(rstd[:, :], rstd[:, :]))
            for c in range(n):
                dve.scalar_tensor_tensor(out=dst(c), in0=src(c), scalar=gain(c), in1=rstd[:, :],
                                         op0=ALU.mult, op1=ALU.mult).then_inc(nrm_h, 1)

        def ada_pe(pe, name, nblk, col0, vec):
            for n in range(nblk):
                block_arrived(pe, BLOCK0[name] + n)
                w = ring[(BLOCK0[name] + n) % 2][:, :].rearrange("p (k m) -> p k m", k=KD)
                for m in range(4):
                    for k in range(KD):
                        ins = pe.matmul(PS[:, 6, col0 + 4 * n + m:col0 + 4 * n + m + 1], w[:, k, m * P:(m + 1) * P],
                                        vec(k), start=(k == 0), stop=(k == KD - 1))
                ins.then_inc(mm_done, 1)

        def ada_dve(dve, own, name, nblk, col0, bias):
            dve.wait_ge(mm_done, MM0[name] + nblk)
            c = slice(col0, col0 + 4 * nblk)
            own(dve.tensor_tensor(modc[:, c], PS[:, 6, c], bias[:, c], ALU.add))

        def chunk_pe(pe, name, j, lhs, rhs, dst=None, n=512):
            if j >= 2:
                pe.wait_ge(evac, EV0[name] + j - 1)
            o = bank(j % 2, n) if dst is None else dst
            for a, (l, r) in enumerate(zip(lhs, rhs)):
                ins = pe.matmul(o, l, r, start=(a == 0), stop=(a == len(lhs) - 1))
            ins.then_inc(mm_done, 1)

        def layer_pe(pe, name, nblk, kc, act_in):
            per = BLK // kc // P
            for n in range(nblk):
                g = BLOCK0[name] + n
                block_arrived(pe, g)
                w = ring[g % 2][:, :].rearrange("p (k m) -> p k m", k=kc)
                for m in range(per):
                    chunk_pe(pe, name, n * per + m, [w[:, k, m * P:(m + 1) * P] for k in range(kc)],
                             [act_in(k) for k in range(kc)])

        def layer_pe_loop(pe, name, nblk, kc, act_in):
            per = BLK // kc // P
            with pe.Fori(0, nblk // 2) as i:
                for s in range(2):
                    pe.wait_ge(w_loaded[s], i * 16 + 16 * (BLOCK0[name] // 2 + 1))
                    w = ring[s][:, :].rearrange("p (k m) -> p k m", k=kc)
                    for m in range(per):
                        j = s * per + m
                        pe.wait_ge(evac, i * (2 * per) + EV0[name] + j - 1)
                        for k in range(kc):
                            ins = pe.matmul(bank(j % 2), w[:, k, m * P:(m + 1) * P], act_in(k),
                                            start=(k == 0), stop=(k == kc - 1))
                        ins.then_inc(mm_done, 1)

        class Attention:

            def __init__(self, name, units, kind, n_tok_cols=512):
                self.units, self.kind, self.name = units, kind, name
                self.last = [u for u in range(len(units)) if u + 1 == len(units) or units[u + 1]["tile"] != units[u]["tile"]]
                self.scored = sem(f"{name}_scored")
                self.weighed = sem(f"{name}_weighed")
                self.exped = sem(f"{name}_exped")
                self.turned = sem(f"{name}_turned")
                self.copied = sem(f"{name}_copied")
                self.summed = sem(f"{name}_summed")
                self.banks_free = sem(f"{name}_banks_free")
                self.tok_ready = sem(f"{name}_tok_ready")
                self.tok_turned = sem(f"{name}_tok_turned")
                self.tok_out = sem(f"{name}_tok_out")
                self.ms_ready = sem(f"{name}_ms_ready")
                self.root_ready = sem(f"{name}_root_ready")

            def pe(self, pe):
                U = self.units
                for u in range(len(U) + 7):
                    if u < len(U):
                        x = U[u]
                        if u >= 2:
                            pe.wait_ge(self.weighed, u - 1)
                        for (l, r, o) in x["scores"](u % 2):
                            ins = pe.matmul(o, l, r, start=True, stop=True)
                        ins.then_inc(self.scored, 1)
                    v = u - 1
                    if 0 <= v < len(U):
                        pe.wait_ge(self.weighed if self.kind == "mlstm" else self.exped, v + 1)
                        if v >= 2:
                            pe.wait_ge(self.copied, v - 1)
                        for (o, i, n) in U[v]["turns"](v % 2):
                            ins = pe.transpose(o, i, ident[0:n, 0:n])
                        ins.then_inc(self.turned, 1)
                    v = u - 2
                    if 0 <= v < len(U):
                        pe.wait_ge(self.copied, v + 1)
                        t = U[v]["tile"]
                        if t > 0 and (v - 1) in self.last:
                            pe.wait_ge(self.banks_free, t)
                        for (o, pairs) in U[v]["values"](v % 2):
                            for a, (l, r) in enumerate(pairs):
                                ins = pe.matmul(o, l, r, start=(a == 0), stop=(a == len(pairs) - 1))
                        ins.then_inc(self.summed, 1)
                    v = u - 5
                    if v in self.last:
                        t = U[v]["tile"]
                        pe.wait_ge(self.tok_ready, t + 1)
                        if t > 0:
                            pe.wait_ge(self.tok_out, t)
                        for c in range(4):
                            ins = pe.transpose(PS[:, 7, tile(c)], otok[:, tile(c)], ident)
                        ins.then_inc(self.tok_turned, 1)

            def act(self, act):
                U = self.units
                for u in range(len(U) + 7):
                    if u < len(U):
                        x = U[u]
                        if self.kind == "mlstm":
                            if u >= 2:
                                act.wait_ge(self.weighed, u - 1)
                        else:
                            act.wait_ge(self.weighed, u + 1)
                            if u >= 2:
                                act.wait_ge(self.turned, u - 1)
                        ins = x["exp"](act, u % 2)
                        ins.then_inc(self.exped, 1)
                    v = u - 1
                    if 0 <= v < len(U):
                        act.wait_ge(self.turned, v + 1)
                        if v >= 2:
                            act.wait_ge(self.summed, v - 1)
                        n, r = U[v]["tcols"], U[v]["trows"]
                        act.activation(probT[0:r, v % 2, 0:n], PS[0:r, 2 + v % 2, 0:n], ACT.Copy).then_inc(self.copied, 1)
                    if u - 3 in self.last and self.root is not None:
                        t = U[u - 3]["tile"]
                        act.wait_ge(self.ms_ready, t + 1)
                        act.activation(self.root, self.root, ACT.Sqrt).then_inc(self.root_ready, 1)
                    if u - 6 in self.last and self.out_act is not None:
                        t = U[u - 6]["tile"]
                        act.wait_ge(self.tok_turned, t + 1)
                        act.activation(self.out_act[:, :, tile(t)], bank(7).rearrange("p (c t) -> p c t", c=4),
                                       ACT.Copy).then_inc(self.tok_out, 1)

            def dve(self, dve, own):
                U = self.units
                for u in range(len(U) + 7):
                    if u < len(U):
                        dve.wait_ge(self.scored, u + 1)
                        if self.kind == "mlstm":
                            dve.wait_ge(self.exped, u + 1)
                            if u >= 2:
                                dve.wait_ge(self.turned, u - 1)
                        elif u >= 2:
                            dve.wait_ge(self.exped, u - 1)
                        U[u]["weigh"](dve, own, u % 2).then_inc(self.weighed, 1)
                    if 0 <= u - 1 < len(U) and U[u - 1].get("rowsum"):
                        dve.wait_ge(self.exped, u)
                        U[u - 1]["rowsum"](dve, own, (u - 1) % 2)
                    if u - 2 in self.last:
                        t = U[u - 2]["tile"]
                        dve.wait_ge(self.summed, u - 1)
                        if t > 0:
                            dve.wait_ge(self.tok_turned, t)
                        self.finish_a(dve, own, t)
                    if u - 4 in self.last and self.finish_b is not None:
                        t = U[u - 4]["tile"]
                        dve.wait_ge(self.root_ready, t + 1)
                        self.finish_b(dve, own, t)
                    if u - 6 in self.last and self.out_dve is not None:
                        t = U[u - 6]["tile"]
                        dve.wait_ge(self.tok_turned, t + 1)
                        self.out_dve(dve, own, t).then_inc(self.tok_out, 1)

            root = out_act = finish_b = out_dve = None

        def softmax_unit(t, q, k, bias, scale, v, o, rsum):
            n = (t + 1) * P
            return dict(
                tile=t, tcols=n, trows=P,
                scores=lambda b: [(q, k, PS[:, b, 0:n])],
                weigh=lambda dve, own, b: dve.tensor_tensor_reduce(
                    sneg[:, b, 0:n], PS[:, b, 0:n], bias, -scale, BIG, ALU.add, ALU.min, nmx[:, b:b + 1]),
                exp=lambda act, b: act.activation(prob[:, b, 0:n], sneg[:, b, 0:n], ACT.Exp, scale=-1.0,
                                                  bias=nmx[:, b:b + 1], accum_out=rsum),
                turns=lambda b: [(PS[:, 2 + b, tile(kb)], prob[:, b, tile(kb)], P) for kb in range(t + 1)],
                values=lambda b: [(o, [(probT[:, b, tile(kb)], v(kb)) for kb in range(t + 1)])])

        def nsa_units():
            U = []
            for t in range(T):
                def q(h):
                    g = h // HG
                    return zT[g * DH:(g + 1) * DH, h % HG, tile(t)]
                for g in range(NG):
                    kc = kcT[g * DH:(g + 1) * DH, :]

                    def weigh(dve, own, b, g=g, t=t):
                        s3 = sneg[:, b, 0:P].rearrange("p (h j) -> p h j", h=HG)[:, :, 0:NC]
                        p3 = PS[:, b, 0:P].rearrange("p (h j) -> p h j", h=HG)[:, :, 0:NC]
                        own(dve.tensor_tensor(s3, p3, biasc[:, t, g * HG:(g + 1) * HG, :], ALU.add))
                        own(dve.tensor_reduce(ssf, s3, AXX, ALU.max))
                        own(dve.tensor_scalar(ssf, ssf, -1e20, None, ALU.max))
                        return dve.tensor_tensor(s3, s3, ssf.unsqueeze(2).to_broadcast([P, HG, NC]), ALU.subtract)

                    U.append(dict(
                        tile=t, tcols=512, trows=NC,
                        scores=lambda b, g=g, kc=kc, t=t: [
                            (zT[g * DH:(g + 1) * DH, a, tile(t)], kc, PS[:, b, 32 * a:32 * a + NC]) for a in range(HG)],
                        weigh=weigh,
                        exp=lambda act, b: act.activation(
                            prob[:, b, 0:P].rearrange("p (h j) -> p h j", h=HG)[:, :, 0:NC],
                            sneg[:, b, 0:P].rearrange("p (h j) -> p h j", h=HG)[:, :, 0:NC], ACT.Exp, scale=NSA_SCALE),
                        rowsum=lambda dve, own, b, g=g, t=t: own(dve.tensor_reduce(
                            rs[:, 24 * (t % 2) + g * HG:24 * (t % 2) + (g + 1) * HG],
                            prob[:, b, 0:P].rearrange("p (h j) -> p h j", h=HG)[:, :, 0:NC], AXX, ALU.add)),
                        turns=lambda b: [(PS[0:NC, 2 + b, tile(a)], prob[:, b, 32 * a:32 * a + NC], P) for a in range(HG)],
                        values=lambda b, g=g: [(PS[:, 4, (g * HG + a) * DH:(g * HG + a + 1) * DH],
                                                [(probT[0:NC, b, tile(a)], vcm[0:NC, g * DH:(g + 1) * DH])])
                                               for a in range(HG)]))
                for br in range(2):
                    for h in range(NH):
                        g = h // HG
                        r = 24 * (t % 2) + 8 * (br + 1) + h
                        U.append(softmax_unit(
                            t, q(h), zT[g * DH:(g + 1) * DH, 4 + br, 0:(t + 1) * P],
                            alibi[:, h, (T - 1 - t) * P:S], NSA_SCALE,
                            lambda kb, br=br, g=g: vtok[:, kb, br * P + g * DH:br * P + (g + 1) * DH],
                            PS[:, 5 + br, h * DH:(h + 1) * DH], rs[:, r:r + 1]))
            return U

        def mla_units():
            U = []
            for t in range(T):
                for h in range(NH):
                    r = 24 * (t % 2) + h
                    U.append(softmax_unit(
                        t, qm[0:96, h, tile(t)], km[0:96, h, 0:(t + 1) * P], mask[:, (T - 1 - t) * P:S], MLA_SCALE,
                        lambda kb, h=h: vm[:, kb, h * DH:(h + 1) * DH],
                        PS[:, 4, h * DH:(h + 1) * DH], rs[:, r:r + 1]))
            return U

        def diff_units():
            U = []
            for t in range(T):
                for p in range(2):
                    for h in range(MH):
                        r = 24 * (t % 2) + MH * p + h
                        U.append(softmax_unit(
                            t, dqk[p * DH:(p + 1) * DH, h, tile(t)], dqk[p * DH:(p + 1) * DH, 4 + h, 0:(t + 1) * P],
                            mask[:, (T - 1 - t) * P:S], NSA_SCALE,
                            lambda kb, h=h: dv[:, kb, tile(h)],
                            PS[:, 4 + p, tile(h)], rs[:, r:r + 1]))
            return U

        def mlstm_units():
            U = []
            for t in range(T):
                for h in range(MH):
                    n = (t + 1) * P
                    r = 24 * (t % 2) + h

                    def decay(act, b, h=h, t=t):
                        nm = tok8[:, 8 * t + h:8 * t + h + 1]
                        if t > 0:
                            act.activation(sneg[:, b, 0:t * P], abc[:, h, 0:t * P], ACT.Exp, bias=nm)
                        return act.activation(sneg[:, b, tile(t)], abcm[:, h, tile(t)], ACT.Exp, bias=nm)

                    U.append(dict(
                        tile=t, tcols=n, trows=P,
                        scores=lambda b, h=h, t=t, n=n: [(qk2[:, h, tile(t)], qk2[:, 4 + h, 0:n], PS[:, b, 0:n])],
                        exp=decay,
                        weigh=lambda dve, own, b, n=n, r=r: dve.tensor_tensor_reduce(
                            prob[:, b, 0:n], PS[:, b, 0:n], sneg[:, b, 0:n], float(P) ** -0.5, 0.0,
                            ALU.mult, ALU.add, rs[:, r:r + 1]),
                        turns=lambda b, t=t: [(PS[:, 2 + b, tile(kb)], prob[:, b, tile(kb)], P) for kb in range(t + 1)],
                        values=lambda b, h=h, t=t: [(PS[:, 4, tile(h)],
                                                     [(probT[:, b, tile(kb)], mv[:, kb, tile(h)]) for kb in range(t + 1)])]))
            return U

        def per_head(a, n, w):
            return a.unsqueeze(2).to_broadcast([P, n, w])

        def heads(a, n):
            return a.rearrange("p (h d) -> p h d", h=n)

        nsa = Attention("nsa", nsa_units(), "softmax")
        mla = Attention("mla", mla_units(), "softmax")
        mls = Attention("mls", mlstm_units(), "mlstm")
        dif = Attention("dif", diff_units(), "softmax")

        def nsa_finish(dve, own, t):
            r = rs[:, 24 * (t % 2):24 * (t % 2) + 24]
            own(dve.tensor_scalar(coef, r, 1e-30, None, ALU.max))
            own(dve.reciprocal(coef, coef))
            own(dve.tensor_tensor(coef, coef, gtok[:, 24 * t:24 * t + 24], ALU.mult))
            own(dve.tensor_tensor(heads(otok, NH), heads(bank(4), NH), per_head(coef[:, 0:8], NH, DH), ALU.mult))
            own(dve.tensor_tensor(heads(otmp, NH), heads(bank(5), NH), per_head(coef[:, 8:16], NH, DH), ALU.mult))
            own(dve.tensor_tensor(otok, otok, otmp, ALU.add))
            ins = dve.tensor_tensor(heads(otmp, NH), heads(bank(6), NH), per_head(coef[:, 16:24], NH, DH), ALU.mult)
            ins.then_inc(nsa.banks_free, 1)
            dve.wait_ge(nsa.banks_free, t + 1)
            dve.tensor_tensor(otok, otok, otmp, ALU.add).then_inc(nsa.tok_ready, 1)

        def mla_finish(dve, own, t):
            r = rs[:, 24 * (t % 2):24 * (t % 2) + 8]
            own(dve.tensor_scalar(coef[:, 0:8], r, 1e-30, None, ALU.max))
            own(dve.reciprocal(coef[:, 0:8], coef[:, 0:8]))
            ins = dve.tensor_tensor(heads(otok, NH), heads(bank(4), NH), per_head(coef[:, 0:8], NH, DH), ALU.mult)
            ins.then_inc(mla.banks_free, 1)

        def head_ms(dve, own, att):
            own(dve.tensor_tensor(otmp, otok, otok, ALU.mult))
            own(dve.tensor_reduce(ss4[:, 0:4], heads(otmp, MH), AXX, ALU.add))
            dve.tensor_scalar(ss4[:, 0:4], ss4[:, 0:4], 1.0 / P, EPS, ALU.mult, ALU.add).then_inc(att.ms_ready, 1)

        def mls_finish(dve, own, t):
            den = rs[:, 24 * (t % 2):24 * (t % 2) + 4]
            own(dve.tensor_scalar(coef[:, 0:4], den, -1.0, None, ALU.mult))
            own(dve.tensor_tensor(coef[:, 0:4], coef[:, 0:4], den, ALU.max))
            own(dve.tensor_tensor(coef[:, 0:4], coef[:, 0:4], tok8[:, 8 * t + 4:8 * t + 8], ALU.max))
            own(dve.reciprocal(coef[:, 0:4], coef[:, 0:4]))
            ins = dve.tensor_tensor(heads(otok, MH), heads(bank(4), MH), per_head(coef[:, 0:4], MH, P), ALU.mult)
            ins.then_inc(mls.banks_free, 1)
            dve.wait_ge(mls.banks_free, t + 1)
            head_ms(dve, own, mls)

        def dif_finish(dve, own, t):
            r = rs[:, 24 * (t % 2):24 * (t % 2) + 8]
            own(dve.reciprocal(coef[:, 0:8], r))
            own(dve.tensor_scalar(coef[:, 4:8], coef[:, 4:8], lamc[:, 4:5], None, ALU.mult))
            own(dve.tensor_tensor(heads(otok, MH), heads(bank(4), MH), per_head(coef[:, 0:4], MH, P), ALU.mult))
            ins = dve.tensor_tensor(heads(otmp, MH), heads(bank(5), MH), per_head(coef[:, 4:8], MH, P), ALU.mult)
            ins.then_inc(dif.banks_free, 1)
            dve.wait_ge(dif.banks_free, t + 1)
            own(dve.tensor_tensor(otok, otok, otmp, ALU.subtract))
            head_ms(dve, own, dif)

        def head_norm(att):
            def finish(dve, own, t):
                own(dve.reciprocal(ss4[:, 0:4], ss4[:, 0:4]))
                dve.tensor_tensor(heads(otok, MH), heads(otok, MH), per_head(ss4[:, 0:4], MH, P), ALU.mult)\
                   .then_inc(att.tok_ready, 1)
            return finish

        def mls_out(dve, own, t):
            for h in range(MH):
                ins = dve.scalar_tensor_tensor(out=catT[:, h, tile(t)], in0=PS[:, 7, tile(h)], scalar=prow("mng", h, h + 1),
                                               in1=mo[:, h, tile(t)], op0=ALU.mult, op1=ALU.mult)
            return ins

        def dif_out(dve, own, t):
            return dve.tensor_scalar(catT[:, MH:2 * MH, tile(t)], bank(7).rearrange("p (c t) -> p c t", c=4),
                                     prow("dng"), 1.0 - 0.2, ALU.mult, ALU.mult)

        nsa.finish_a, nsa.out_act = nsa_finish, onT
        mla.finish_a, mla.out_act = mla_finish, omT
        mla.tok_ready = mla.banks_free
        mls.finish_a, mls.finish_b, mls.root, mls.out_dve = mls_finish, head_norm(mls), ss4[:, 0:4], mls_out
        dif.finish_a, dif.finish_b, dif.root, dif.out_dve = dif_finish, head_norm(dif), ss4[:, 0:4], dif_out

        g_sig, g_turn = sem("gates_sigmoid"), sem("gates_turned")
        c_stk, c_mm, c_pe, c_hid, c_out = (sem(n) for n in ("cmp_stacked", "cmp_hidden", "cmp_bias", "cmp_silu", "cmp_out"))
        y_tmp = sem("y_tmp")
        fc_sq = sem("fc_squared")
        cv_sum = sem("conv_summed")
        gr, gr_x = sem("gate_rows"), sem("gate_rows_abs")
        dot_cp, w_cp = sem("dots_copied"), sem("weights_copied")
        gr_act = sem("gate_rows_act")
        gr_pe = sem("gate_rows_pe")
        lam_s, lam_e = sem("lam_sums"), sem("lam_exps")
        silu_c = sem("silu_c")
        tt_pe, tt_ev = sem("token_turned"), sem("token_copied")
        pk_ev, pk_top = sem("peer_scores_copied"), sem("peer_scores_used")
        pk_mx, pk_ex = sem("peer_gate_max"), sem("peer_gate_exp")
        u_land = [sem(f"landed{j}") for j in range(GRP)]
        u_used = sem("slots_used")
        idx_cp, pool_step = sem("idx_copied"), sem("pool_step")
        top_done = sem("top_done")
        gl_done, fin_ms, fin_rt, fin_ok = (sem(n) for n in (
            "gelu_done", "final_ms", "final_root", "final_ready"))
        g2_pe, g2_ev = sem("g2_pe"), sem("g2_ev")

        block = ctx.enter_context(nc.Block())

        @block.sync
        def _(sp):
            for n in range(NBLK):
                if n >= 2:
                    sp.wait_ge(mm_done, MM_THROUGH[n - 2])
                sp.dma_start(ring[n % 2][:, :], ap["wstream"][n]).then_inc(w_loaded[n % 2], 16)
            for t in range(T):
                sp.wait_ge(fin_ok, t + 1)
                sp.dma_start(out[t * P:(t + 1) * P, :], acc[:, 0, :]).then_inc(stored, 16)
            sp.wait_ge(stored, 16 * T)

        @block.tensor
        def _(pe):
            pe.wait_ge(loaded, 80)
            pe.wait_ge(ready, 1)
            norm_pe(pe, "x", KD)
            ada_pe(pe, "ada_a", 4, 0, lambda k: prow("c", k, k + 1))
            fence(pe, "pe")
            name = "in1"
            for n in range(4):
                g = BLOCK0[name] + n
                block_arrived(pe, g)
                w = ring[g % 2][:, :].rearrange("p (k m) -> p k m", k=KD)
                for m in range(4 if n < 3 else 2):
                    chunk_pe(pe, name, 4 * n + m, [w[:, k, tile(m)] for k in range(KD)], [hT[:, k, :] for k in range(KD)])
            for t in range(T):
                chunk_pe(pe, name, 14 + t, [hT[:, k, tile(t)] for k in range(KD)],
                         [w[:, k, 256:512] for k in range(KD)], n=256)
            fence(pe, "pe")
            norm_pe(pe, "cq", 3)
            norm_pe(pe, "ckv", 2)
            pe.wait_ge(g_sig, 1)
            for t in range(T):
                ins = pe.transpose(PS[:, 6, 24 * t:24 * t + 24], sq[0:24, 0, tile(t)], ident[0:24, 0:24])
            ins.then_inc(g_turn, 1)
            fence(pe, "pe")
            block_arrived(pe, BLOCK0["uq"])
            w = ring[BLOCK0["uq"] % 2][:, 0:3 * D].rearrange("p (k m) -> p k m", k=3)
            for h in range(NH):
                chunk_pe(pe, "uq", h, [w[:, k, tile(h)] for k in range(3)], [cqT[:, k, :] for k in range(3)])
            block_arrived(pe, BLOCK0["ukv"])
            w = ring[BLOCK0["ukv"] % 2][:, 0:2 * D].rearrange("p (k m) -> p k m", k=2)
            for c in range(4):
                chunk_pe(pe, "uq", 8 + c, [w[:, k, tile(c)] for k in range(2)], [ckvT[:, k, :] for k in range(2)])
            for t in range(T):
                chunk_pe(pe, "uq", 12 + t, [ckvT[:, k, tile(t)] for k in range(2)], [w[:, k, 512:1024] for k in range(2)])
            fence(pe, "pe")
            for r in range(2):
                n = BLOCK0["ck"] + r
                block_arrived(pe, n)
                w = ring[n % 2][:, :].rearrange("p (l m) -> p l m", l=16)
                pev = prow("pek" if r == 0 else "pev")
                if r == 0:
                    pe.wait_ge(c_stk, 8)
                for hc in range(2):
                    for l in range(16):
                        rhs = stk[r][:, :, 2 * l:2 * l + 16 * (NC - 1) + 1:16]
                        pe.matmul(PS[:, 2 * r + hc, 0:2 * NC].rearrange("p (g j) -> p g j", g=2), w[:, l, tile(hc)], rhs,
                                  start=(l == 0), stop=(l == 15))
                    for l in range(16):
                        ins = pe.matmul(PS[:, 4 + 2 * r + hc, 0:1], w[:, l, tile(hc)], pev[:, l:l + 1],
                                        start=(l == 0), stop=(l == 15))
                ins.then_inc(mm_done, 1)
                pe.wait_ge(c_hid, 2 * r + 2)
                if r == 0:
                    for g in range(NG):
                        for hc in range(2):
                            ins = pe.matmul(PS[g * DH:(g + 1) * DH, 0, 128:128 + NC], prow("ck2", hc * DH, (hc + 1) * DH),
                                            hid[:, hc * 62 + g * NC:hc * 62 + (g + 1) * NC], start=(hc == 0), stop=(hc == 1))
                    ins.then_inc(c_mm, 1)
                else:
                    for g in range(NG):
                        for hc in range(2):
                            ins = pe.matmul(PS[0:NC, 1, 128 + g * DH:128 + (g + 1) * DH],
                                            hid[:, hc * 62 + g * NC:hc * 62 + (g + 1) * NC],
                                            prow("cv2", hc * DH, (hc + 1) * DH), start=(hc == 0), stop=(hc == 1))
                    ins.then_inc(c_mm, 1)
            fence(pe, "pe")
            nsa.pe(pe)
            fence(pe, "pe")
            mla.pe(pe)
            fence(pe, "pe")
            layer_pe_loop(pe, "gab", 4, KD, lambda k: hT[:, k, :])
            ada_pe(pe, "ada_b", 8, 16, lambda k: prow("c", k, k + 1))
            fence(pe, "pe")
            layer_pe(pe, "on", 1, 4, lambda k: onT[:, k, :])
            block_arrived(pe, BLOCK0["om"])
            w = ring[BLOCK0["om"] % 2][:, :].rearrange("p (k m) -> p k m", k=4)
            for m in range(8):
                chunk_pe(pe, "on", 8 + m, [w[:, k, tile(m)] for k in range(4)], [omT[:, k, :] for k in range(4)])
            fence(pe, "pe")
            layer_pe(pe, "out1", 2, KD, lambda k: yT[:, k, :])
            fence(pe, "pe")
            norm_pe(pe, "mid", KD)
            fence(pe, "pe")
            layer_pe_loop(pe, "fc1", 8, KD, lambda k: hT[:, k, :])
            fence(pe, "pe")
            layer_pe_loop(pe, "fc2", 8, 32, lambda k: aT[:, k, :])
            fence(pe, "pe")
            norm_pe(pe, "fin", KD)
            fence(pe, "pe")
            norm_pe(pe, "n1", KD)
            pe.wait_ge(silu_c, 1)
            ada_pe(pe, "ada_c", 12, 0, lambda k: scl[:, 8 + k:9 + k])
            fence(pe, "pe")
            name = "in2"
            for n in range(8):
                g = BLOCK0[name] + n
                block_arrived(pe, g)
                w = ring[g % 2][:, :].rearrange("p (k m) -> p k m", k=KD)
                if n < 5:
                    for m in range(4):
                        chunk_pe(pe, name, 4 * n + m, [w[:, k, tile(m)] for k in range(KD)], [hT[:, k, :] for k in range(KD)])
                elif n == 5:
                    chunk_pe(pe, name, 20, [w[:, k, 0:P] for k in range(KD)], [hT[:, k, :] for k in range(KD)])
                else:
                    for t in range(T):
                        chunk_pe(pe, name, 21 + 4 * (n - 6) + t, [hT[:, k, tile(t)] for k in range(KD)],
                                 [w[:, k, :] for k in range(KD)])
            fence(pe, "pe")
            pe.wait_ge(gr, 1)
            for h in range(MH):
                ins = pe.matmul(PS[:, h, :], const("sel", slice(0, 4))[:, tile(h)], grow[0:4, 4, :], start=True, stop=True)
            ins.then_inc(gr_pe, 1)
            pe.wait_ge(gr_act, 3)
            for t in range(T):
                pe.transpose(PS[:, 4, 8 * t:8 * t + 4], grow[0:4, 6, tile(t)], ident[0:4, 0:4])
                ins = pe.transpose(PS[:, 4, 8 * t + 4:8 * t + 8], grow[0:4, 7, tile(t)], ident[0:4, 0:4])
            ins.then_inc(gr_pe, 1)
            fence(pe, "pe")
            mls.pe(pe)
            fence(pe, "pe")
            dif.pe(pe)
            fence(pe, "pe")
            layer_pe(pe, "out2", 2, KD, lambda k: catT[:, k, :])
            fence(pe, "pe")
            norm_pe(pe, "n2", KD)
            fence(pe, "pe")
            layer_pe_loop(pe, "pq", 4, KD, lambda k: hT[:, k, :])
            fence(pe, "pe")
            for b in range(16):
                src = xT if b < 8 else hT
                t, half = (b % 8) // 2, b % 2
                if b >= 4:
                    pe.wait_ge(tt_ev, b - 3)
                for c in range(4):
                    ins = pe.transpose(PS[:, b % 4, tile(c)], src[:, 4 * half + c, tile(t)], ident)
                ins.then_inc(tt_pe, 1)
            for k in range(KD):
                ins = pe.matmul(PS[:, 4 + k // 4, tile(k % 4)], modc[:, 40 + k:41 + k].to_broadcast([P, P]), ident,
                                start=True, stop=True)
            ins.then_inc(g2_pe, 1)
            fence(pe, "pe")
            block_arrived(pe, BLOCK0["sk"])
            w = ring[BLOCK0["sk"] % 2][:, 0:16 * NKEY].rearrange("p (c n) -> p c n", c=16)
            for t in range(T):
                if t > 0:
                    pe.wait_ge(pk_ev, t)
                for c in range(16):
                    ins = pe.matmul(PS[:, c // 4, tile(c % 4)], pq[:, c, tile(t)], w[:, c, :], start=True, stop=True)
                ins.then_inc(mm_done, 1)

        @block.scalar
        def _(act):
            own = Own(act, act_own)
            for dst, src in ((prm[:, :], ap["params"]), (cst[:, :], ap["consts"]), (xT[:, :, :], ap["xT"]),
                             (alibi, ap["alibi"]), (biasc, ap["biasc"])):
                act.dma_start(dst, src).then_inc(loaded, 16)
            act.wait_ge(loaded, 80)
            norm_act(act, "x", lambda c: xT[:, c, :], KD, lambda c: hT[:, c, :], lambda c: modc[:, c:c + 1])
            fence(act, "act")
            n = "in1"
            for j in range(18):
                act.wait_ge(mm_done, MM0[n] + j + 1)
                if j < 14:
                    act.activation(zT[:, j, :], bank(j % 2), ACT.Copy).then_inc(evac, 1)
                else:
                    act.activation(vtok[:, j - 14, :], bank(j % 2, 256), ACT.Copy).then_inc(evac, 1)
            fence(act, "act")
            norm_act(act, "cq", lambda c: zT[:, 8 + c, :], 3)
            norm_act(act, "ckv", lambda c: zT[:, 11 + c, :], 2)
            act.wait_ge(nrm_mm, NORM0["mid"][0])
            act.activation(sq[0:24, 0, :], zT[0:24, 13, :], ACT.Sigmoid).then_inc(g_sig, 1)
            act.wait_ge(g_turn, 1)
            act.activation(gtok, PS[:, 6, 0:96], ACT.Copy)
            fence(act, "act")
            fence(act, "act")
            for r in range(2):
                act.wait_ge(c_pe, 1 + r)
                act.wait_ge(c_mm, r) if r else None
                for hc in range(2):
                    act.activation(hid[:, hc * 62:(hc + 1) * 62], PS[:, 2 * r + hc, 0:2 * NC], ACT.Silu,
                                   bias=hb[:, hc:hc + 1]).then_inc(c_hid, 1)
            fence(act, "act")
            nsa.act(act)
            fence(act, "act")
            mla.act(act)
            fence(act, "act")
            with act.Fori(0, 2) as i:
                for j in range(8):
                    act.wait_ge(mm_done, i * 8 + (MM0["gab"] + j + 1))
                    act.activation(gT[:, bass.ds(i * 8 + j, 1), :].rearrange("p a n -> p (a n)"), bank(j % 2),
                                   ACT.Sigmoid).then_inc(evac, 1)
            fence(act, "act")
            fence(act, "act")
            fence(act, "act")
            norm_act(act, "mid", lambda c: xT[:, c, :], KD, lambda c: hT[:, c, :], lambda c: modc[:, 24 + c:25 + c])
            fence(act, "act")
            with act.Fori(0, 4) as i:
                for j in range(8):
                    act.wait_ge(evac, i * 8 + (EV0["fc1"] + j + 1))
                    act.activation(aT[:, bass.ds(i * 8 + j, 1), :].rearrange("p a n -> p (a n)"), rbuf[:, j % 2, :],
                                   ACT.Square).then_inc(fc_sq, 1)
            fence(act, "act")
            fence(act, "act")
            norm_act(act, "fin", lambda c: xT[:, c, :], KD)
            fence(act, "act")
            act.activation(scl[:, 8:16], prow("c2"), ACT.Silu).then_inc(silu_c, 1)
            norm_act(act, "n1", lambda c: xT[:, c, :], KD, lambda c: hT[:, c, :], lambda c: modc[:, c:c + 1])
            fence(act, "act")
            n = "in2"
            for j in range(29):
                act.wait_ge(mm_done, MM0[n] + j + 1)
                if j < 8:
                    ins = act.activation(uT[:, j, 3:S + 3], bank(j % 2), ACT.Copy)
                elif j < 12:
                    ins = act.activation(mo[:, j - 8, :], bank(j % 2), ACT.Sigmoid)
                elif j < 20:
                    ins = act.activation(dqk[:, j - 12, :], bank(j % 2), ACT.Copy)
                elif j == 20:
                    ins = act.activation(zG, bank(j % 2), ACT.Copy)
                elif j < 25:
                    ins = act.activation(mv[:, j - 21, :], bank(j % 2), ACT.Copy)
                else:
                    ins = act.activation(dv[:, j - 25, :], bank(j % 2), ACT.Copy)
                ins.then_inc(evac, 1)
            for c in range(8):
                act.wait_ge(cv_sum, c + 1)
                act.activation(qk2[:, c, :], qk2[:, c, :], ACT.Silu, bias=prow("convb", c, c + 1))
            fence(act, "act")
            act.wait_ge(gr_x, 1)
            own(act.activation(grow[32:36, 1, :], grow[32:36, 1, :], ACT.Exp))
            act.activation(grow[32:36, 1, :], grow[32:36, 1, :], ACT.Ln, bias=1.0).then_inc(gr_act, 1)
            act.wait_ge(gr, 1)
            act.activation(grow[0:4, 6, :], grow[0:4, 5, :], ACT.Copy, scale=-1.0).then_inc(gr_act, 1)
            act.activation(grow[0:4, 7, :], grow[0:4, 3, :], ACT.Exp, scale=-1.0).then_inc(gr_act, 1)
            act.wait_ge(gr_pe, 1)
            act.activation(abc, PS[:, 0:4, :], ACT.Copy).then_inc(gr_act, 1)
            act.wait_ge(gr_pe, 2)
            act.activation(tok8, PS[:, 4, 0:32], ACT.Copy)
            act.wait_ge(lam_s, 1)
            act.activation(lamc[:, 2:4], lamc[:, 0:2], ACT.Exp).then_inc(lam_e, 1)
            fence(act, "act")
            mls.act(act)
            fence(act, "act")
            dif.act(act)
            fence(act, "act")
            fence(act, "act")
            norm_act(act, "n2", lambda c: xT[:, c, :], KD, lambda c: hT[:, c, :], lambda c: modc[:, 24 + c:25 + c])
            fence(act, "act")
            with act.Fori(0, 2) as i:
                for j in range(8):
                    act.wait_ge(mm_done, i * 8 + (MM0["pq"] + j + 1))
                    act.activation(pq[:, bass.ds(i * 8 + j, 1), :].rearrange("p a n -> p (a n)"), bank(j % 2),
                                   ACT.Copy).then_inc(evac, 1)
            fence(act, "act")
            for b in range(16):
                act.wait_ge(tt_pe, b + 1)
                dst = xtok if b < 8 else h2tok
                act.activation(dst[:, (b % 8) // 2, (b % 2) * 512:(b % 2 + 1) * 512], bank(b % 4), ACT.Copy).then_inc(tt_ev, 1)
            fence(act, "act")
            for t in range(T):
                act.wait_ge(mm_done, MM0["sk"] + t + 1)
                if t > 0:
                    act.wait_ge(pk_top, t)
                act.activation(sc.rearrange("p (a b) n -> p a (b n)", a=4), PS[:, 0:4, :], ACT.Copy).then_inc(pk_ev, 1)
                act.wait_ge(pk_mx, t + 1)
                act.activation(gate[:, t, :], gate[:, t, :], ACT.Exp).then_inc(pk_ex, 1)
            act.wait_ge(g2_pe, 1)
            act.wait_ge(top_done, T)
            act.activation(g2row.rearrange("p (a b) -> p a b", a=2), PS[:, 4:6, :], ACT.Copy).then_inc(g2_ev, 1)
            act.dma_start(fgrow, ap["fgrow"]).then_inc(g2_ev, 16)
            for t in range(T):
                act.wait_ge(dot_cp, NSLOT // GRP * (t + 1) + 1)
                act.activation(dots, dots, ACT.Gelu).then_inc(gl_done, 1)
                act.wait_ge(fin_ms, t + 1)
                act.activation(ssf[:, 0:1], ssf[:, 0:1], ACT.Sqrt).then_inc(fin_rt, 1)

        @block.vector
        def _(dve):
            own = Own(dve, dve_own)
            dve.memset(ones[:, :], 1.0).then_inc(ready, 1)
            dve.wait_ge(loaded, 80)
            ada_dve(dve, own, "ada_a", 4, 0, prow("b_ada"))
            own(dve.scalar_tensor_tensor(out=scl[:, 0:8], in0=modc[:, 8:16], scalar=1.0, in1=prow("g_mix"),
                                         op0=ALU.add, op1=ALU.mult))
            norm_dve(dve, own, "x", lambda c: xT[:, c, :], KD, lambda c: hT[:, c, :], lambda c: scl[:, c:c + 1])
            fence(dve, "dve")
            fence(dve, "dve")
            norm_dve(dve, own, "cq", lambda c: zT[:, 8 + c, :], 3, lambda c: cqT[:, c, :], lambda c: prow("g_cq", c, c + 1))
            norm_dve(dve, own, "ckv", lambda c: zT[:, 11 + c, :], 2, lambda c: ckvT[:, c, :], lambda c: prow("g_ckv", c, c + 1))
            fence(dve, "dve")
            rope_k, rope_s = slice(64, 96), slice(96, 128)

            def rotate(src, dst):
                own(dve.tensor_tensor(rt[rope_k, 0, :], src[rope_k, :], const("rope", rope_k), ALU.mult))
                own(dve.tensor_tensor(rt[rope_k, 1, :], src[rope_s, :], const("rope", rope_s), ALU.mult))
                return dve.tensor_tensor(dst, rt[rope_k, 0, :], rt[rope_k, 1, :], ALU.add)

            own(rotate(zT[:, 13, :], km[rope_k, 0, :]))
            own(dve.tensor_copy(km[rope_k, 1:8, :], km[rope_k, 0:1, :].to_broadcast([32, 7, S])))
            for j in range(16):
                dve.wait_ge(mm_done, MM0["uq"] + j + 1)
                b = bank(j % 2)
                if j < 8:
                    own(dve.tensor_copy(qm[0:64, j, :], b[0:64, :]))
                    ins = rotate(b, qm[rope_k, j, :])
                elif j < 12:
                    own(dve.tensor_copy(km[0:64, 2 * (j - 8), :], b[0:64, :]))
                    ins = dve.tensor_copy(km[0:64, 2 * (j - 8) + 1, :], b[64:128, :])
                else:
                    ins = dve.tensor_copy(vm[:, j - 12, :], b)
                ins.then_inc(evac, 1)
            fence(dve, "dve")
            for r in range(2):
                src = zT[:, 6 + r, :]
                for g in range(NG):
                    dve.tensor_copy(stk[r][0:64, g, :], src[g * DH:(g + 1) * DH, :]).then_inc(c_stk, 1)
                    dve.tensor_copy(stk[r][64:128, g, 0:S - 1], src[g * DH:(g + 1) * DH, 1:S]).then_inc(c_stk, 1)
            for r in range(2):
                dve.wait_ge(mm_done, MM0["ck"] + r + 1)
                if r:
                    dve.wait_ge(c_hid, 2)
                dve.tensor_copy(hb[:, 0:1], PS[:, 4 + 2 * r, 0:1])
                dve.tensor_copy(hb[:, 1:2], PS[:, 5 + 2 * r, 0:1]).then_inc(c_pe, 1)
                dve.wait_ge(c_mm, r + 1)
                if r == 0:
                    own(dve.tensor_copy(kcT, PS[:, 0, 128:128 + NC]))
                else:
                    own(dve.tensor_copy(vcm[0:NC, :], PS[0:NC, 1, 128:256]))
            fence(dve, "dve")
            nsa.dve(dve, own)
            fence(dve, "dve")
            mla.dve(dve, own)
            fence(dve, "dve")
            ada_dve(dve, own, "ada_b", 8, 16, prow("b_ada"))
            fence(dve, "dve")
            for j in range(16):
                dve.wait_ge(mm_done, MM0["on"] + j + 1)
                if j < 8:
                    dve.tensor_tensor(yT[:, j, :], gT[:, j, :], bank(j % 2), ALU.mult).then_inc(evac, 1)
                else:
                    if j == 8:
                        dve.wait_ge(evac, EV0["on"] + 8)
                    if j >= 10:
                        dve.wait_ge(y_tmp, j - 9)
                    dve.tensor_tensor(ytmp[:, j % 2, :], gT[:, j, :], bank(j % 2), ALU.mult).then_inc(evac, 1)
                    dve.wait_ge(evac, EV0["on"] + j + 1)
                    dve.tensor_tensor(yT[:, j - 8, :], yT[:, j - 8, :], ytmp[:, j % 2, :], ALU.add).then_inc(y_tmp, 1)
            fence(dve, "dve")

            def residual(name, gcol):
                for j in range(8):
                    dve.wait_ge(mm_done, MM0[name] + j + 1)
                    dve.scalar_tensor_tensor(out=xT[:, j, :], in0=bank(j % 2), scalar=modc[:, gcol + j:gcol + j + 1],
                                             in1=xT[:, j, :], op0=ALU.mult, op1=ALU.add).then_inc(evac, 1)

            residual("out1", 16)
            fence(dve, "dve")
            own(dve.scalar_tensor_tensor(out=scl[:, 0:8], in0=modc[:, 32:40], scalar=1.0, in1=prow("g_mlp"),
                                         op0=ALU.add, op1=ALU.mult))
            norm_dve(dve, own, "mid", lambda c: xT[:, c, :], KD, lambda c: hT[:, c, :], lambda c: scl[:, c:c + 1])
            fence(dve, "dve")
            for j in range(2):
                dve.memset(rbuf[:, j, :], 0.0).then_inc(fc_sq, 1)
            dve.wait_ge(fc_sq, 2)
            with dve.Fori(0, 4) as i:
                for j in range(8):
                    dve.wait_ge(mm_done, i * 8 + (MM0["fc1"] + j + 1))
                    dve.wait_ge(fc_sq, i * 8 + (j + 1))
                    dve.tensor_scalar(rbuf[:, j % 2, :], bank(j % 2), 0.0, None, ALU.max).then_inc(evac, 1)
            fence(dve, "dve")
            residual("fc2", 40)
            fence(dve, "dve")
            norm_dve(dve, own, "fin", lambda c: xT[:, c, :], KD, lambda c: xT[:, c, :], lambda c: prow("g_final", c, c + 1))
            fence(dve, "dve")
            ada_dve(dve, own, "ada_c", 12, 0, prow("ada_b2"))
            own(dve.scalar_tensor_tensor(out=scl[:, 0:8], in0=modc[:, 8:16], scalar=1.0, in1=prow("n1g"),
                                         op0=ALU.add, op1=ALU.mult))
            norm_dve(dve, own, "n1", lambda c: xT[:, c, :], KD, lambda c: hT[:, c, :], lambda c: scl[:, c:c + 1])
            fence(dve, "dve")
            own(dve.memset(uT[:, :, 0:3], 0.0))
            for c in range(8):
                dve.wait_ge(evac, EV0["in2"] + c + 1)
                for j in range(4):
                    wj = prow("convw", 4 * c + j, 4 * c + j + 1)
                    src = uT[:, c, j:j + S]
                    if j == 0:
                        own(dve.tensor_scalar(qk2[:, c, :], src, wj, None, ALU.mult))
                    else:
                        ins = dve.scalar_tensor_tensor(out=qk2[:, c, :], in0=src, scalar=wj, in1=qk2[:, c, :],
                                                       op0=ALU.mult, op1=ALU.add)
                        if j < 3:
                            own(ins)
                ins.then_inc(cv_sum, 1)
            fence(dve, "dve")
            f = slice(32, 36)
            own(dve.tensor_scalar(grow[f, 0, :], zG[f, :], prow("gb_f", rows=f), None, ALU.add))
            own(dve.tensor_scalar(grow[f, 1, :], grow[f, 0, :], -1.0, None, ALU.mult))
            own(dve.tensor_scalar(grow[f, 2, :], grow[f, 0, :], 0.0, None, ALU.min))
            dve.tensor_tensor(grow[f, 1, :], grow[f, 1, :], grow[f, 0, :], ALU.min).then_inc(gr_x, 1)
            dve.wait_ge(gr_act, 1)
            r4 = slice(0, 4)
            own(dve.tensor_tensor(grow[r4, 0, :], grow[f, 2, :], grow[f, 1, :], ALU.subtract))
            own(dve.memset(grow[r4, 1, :], 1.0))
            own(dve.tensor_tensor_scan(grow[r4, 2, :], grow[r4, 1, :], grow[r4, 0, :], 0.0, ALU.mult, ALU.add))
            own(dve.scalar_tensor_tensor(out=grow[r4, 4, :], in0=zG[r4, :], scalar=prow("gb_i", rows=r4), in1=grow[r4, 2, :],
                                         op0=ALU.add, op1=ALU.subtract))
            own(dve.memset(grow[r4, 1, :], 0.0))
            own(dve.tensor_tensor_scan(grow[r4, 5, :], grow[r4, 4, :], grow[r4, 1, :], 0.0, ALU.max, ALU.add))
            dve.tensor_tensor(grow[r4, 3, :], grow[r4, 2, :], grow[r4, 5, :], ALU.add).then_inc(gr, 1)
            for a in range(2):
                own(dve.tensor_tensor_reduce(otmp[:, 0:64], prow("lam", 128 * a, 128 * a + 64), prow("lam", 128 * a + 64, 128 * a + 128),
                                             1.0, 0.0, ALU.mult, ALU.add, lamc[:, a:a + 1]))
            dve.tensor_scalar(lamc[:, 5:6], lamc[:, 0:1], 1.0, None, ALU.mult).then_inc(lam_s, 1)
            dve.wait_ge(lam_e, 1)
            own(dve.tensor_tensor(lamc[:, 6:7], lamc[:, 2:3], lamc[:, 3:4], ALU.subtract))
            own(dve.tensor_scalar(lamc[:, 4:5], lamc[:, 6:7], 0.2, None, ALU.add))
            dve.wait_ge(gr_act, 4)
            for h in range(MH):
                own(dve.tensor_tensor(abcm[:, h, :].rearrange("p (t s) -> p t s", t=T), abc[:, h, :].rearrange("p (t s) -> p t s", t=T),
                                      mask[:, 3 * P:].unsqueeze(1).to_broadcast([P, T, P]), ALU.add))
            fence(dve, "dve")
            mls.dve(dve, own)
            fence(dve, "dve")
            dif.dve(dve, own)
            fence(dve, "dve")
            residual("out2", 16)
            fence(dve, "dve")
            own(dve.scalar_tensor_tensor(out=scl[:, 0:8], in0=modc[:, 32:40], scalar=1.0, in1=prow("n2g"),
                                         op0=ALU.add, op1=ALU.mult))
            norm_dve(dve, own, "n2", lambda c: xT[:, c, :], KD, lambda c: hT[:, c, :], lambda c: scl[:, c:c + 1])
            fence(dve, "dve")
            fence(dve, "dve")
            fence(dve, "dve")

            def top16(src, src2, val, idx):
                own(dve.max(val[:, 0:8], src))
                own(dve.max_index(idx[:, 0:8], val[:, 0:8], src))
                own(dve.match_replace(src2, val[:, 0:8], src, -3e38))
                own(dve.max(val[:, 8:16], src2))
                own(dve.max_index(idx[:, 8:16], val[:, 8:16], src2))

            for t in range(T):
                dve.wait_ge(pk_ev, t + 1)
                for c in range(16):
                    top16(sc[:, c, :], sc2[:, c, :], tkv[:, c, :], tki[:, c, :])
                dve.tensor_copy(tkf, tki).then_inc(pk_top, 1)
                dve.wait_ge(pk_top, t + 1)
                for h in range(PH):
                    own(dve.tensor_tensor(cand[:, h, :].rearrange("p (a b) -> p a b", a=PK),
                                          tkv[:, 2 * h, :].unsqueeze(2).to_broadcast([P, PK, PK]),
                                          tkv[:, 2 * h + 1, :].unsqueeze(1).to_broadcast([P, PK, PK]), ALU.add))
                    top16(cand[:, h, :], cand2[:, h, :], fval[:, PK * h:PK * h + PK], fpos[:, PK * h:PK * h + PK])
                for half in range(2):
                    if half == 0:
                        own(dve.tensor_scalar(fpi, fpos, 4, None, ALU.logical_shift_right))
                    else:
                        own(dve.tensor_scalar(fpi, fpos, 15, None, ALU.bitwise_and))
                    own(dve.tensor_copy(fpf, fpi))
                    own(dve.tensor_tensor(oneh, fpf.unsqueeze(2).to_broadcast([P, NSLOT, PK]),
                                          const("iota").unsqueeze(1).to_broadcast([P, NSLOT, PK]), ALU.is_equal))
                    keys = tkf.rearrange("p (h a) k -> p h a k", a=2)[:, :, half, :]
                    for h in range(PH):
                        own(dve.tensor_tensor(oneh2[:, PK * h:PK * h + PK, :], oneh[:, PK * h:PK * h + PK, :],
                                              keys[:, h, :].unsqueeze(1).to_broadcast([P, PK, PK]), ALU.mult))
                    own(dve.tensor_reduce(selv[:, half, :], oneh2, AXX, ALU.add))
                own(dve.scalar_tensor_tensor(out=fpf, in0=selv[:, 0, :], scalar=float(NKEY), in1=selv[:, 1, :],
                                             op0=ALU.mult, op1=ALU.add))
                own(dve.tensor_copy(eidx[:, t, :], fpf))
                f3 = fval.rearrange("p (h k) -> p h k", h=PH)
                g3 = gate[:, t, :].rearrange("p (h k) -> p h k", h=PH)
                dve.tensor_tensor(g3, f3, f3[:, :, 0:1].to_broadcast([P, PH, PK]), ALU.subtract).then_inc(pk_mx, 1)
                dve.wait_ge(pk_ex, t + 1)
                own(dve.tensor_reduce(sm8[:, 0, :], g3, AXX, ALU.add))
                own(dve.reciprocal(sm8[:, 1, :], sm8[:, 0, :]))
                dve.tensor_tensor(g3, g3, sm8[:, 1, :].unsqueeze(2).to_broadcast([P, PH, PK]), ALU.mult).then_inc(top_done, 1)
                dve.wait_ge(top_done, t + 1)
            NI = NSLOT // GRP
            dve.sem_inc(u_used, GRP)
            dve.sem_inc(dot_cp, 1)
            for t in range(T):
                base = 2 * t * NI
                with dve.Fori(0, NI) as i:
                    for j in range(GRP):
                        dve.wait_ge(u_land[j], i * 16 + 16 * (base + 1))
                        if j == 0:
                            dve.wait_ge(dot_cp, i + (NI * t + 1))
                        dve.tensor_tensor_reduce(ubuf[:, j, :], ubuf[:, j, :], h2tok[:, t, :], 1.0, 0.0,
                                                 ALU.mult, ALU.add, dots8[:, j:j + 1]).then_inc(u_used, 1)
                    dve.wait_ge(u_used, i * GRP + GRP * (base + 2))
                    dve.tensor_copy(dots[:, bass.ds(i * GRP, GRP)], dots8).then_inc(dot_cp, 1)
                dve.wait_ge(gl_done, t + 1)
                own(dve.tensor_tensor(wexp[:, t, :], dots, gate[:, t, :], ALU.mult))
                if t > 0:
                    dve.wait_ge(stored, 16 * t)
                own(dve.memset(acc, 0.0))
                vb = base + NI
                with dve.Fori(0, NI) as i:
                    dve.wait_ge(u_used, i * GRP + GRP * (vb + 1))
                    dve.tensor_copy(w8, wexp[:, t, bass.ds(i * GRP, GRP)]).then_inc(w_cp, 1)
                    dve.wait_ge(w_cp, i + (NI * t + 1))
                    for j in range(GRP):
                        dve.wait_ge(u_land[j], i * 16 + 16 * (vb + 1))
                        if j >= 2:
                            dve.wait_ge(u_used, i * GRP + (GRP * (vb + 1) + j - 1))
                        dve.scalar_tensor_tensor(out=acc[:, j % 2, :], in0=ubuf[:, j, :], scalar=w8[:, j:j + 1],
                                                 in1=acc[:, j % 2, :], op0=ALU.mult, op1=ALU.add).then_inc(u_used, 1)
                dve.wait_ge(u_used, GRP * (vb + NI + 1))
                if t == 0:
                    dve.wait_ge(g2_ev, 17)
                a0, a1, x = acc[:, 0, :], acc[:, 1, :], xtok[:, t, :]
                own(dve.tensor_tensor(a0, a0, a1, ALU.add))
                own(dve.tensor_tensor(a0, a0, g2row, ALU.mult))
                own(dve.tensor_tensor(a0, a0, x, ALU.add))
                own(dve.tensor_tensor_reduce(a1, a0, a0, 1.0, 0.0, ALU.mult, ALU.add, ssf[:, 1:2]))
                dve.tensor_scalar(ssf[:, 0:1], ssf[:, 1:2], 1.0 / D, EPS, ALU.mult, ALU.add).then_inc(fin_ms, 1)
                dve.wait_ge(fin_rt, t + 1)
                own(dve.reciprocal(ssf[:, 2:3], ssf[:, 0:1]))
                dve.scalar_tensor_tensor(out=a0, in0=a0, scalar=ssf[:, 2:3], in1=fgrow, op0=ALU.mult, op1=ALU.mult)\
                   .then_inc(fin_ok, 1)

        @block.gpsimd
        def _(pool):
            NI = NSLOT // GRP
            pool.wait_ge(top_done, T)
            for ph in range(2 * T):
                t, table = ph // 2, ap["peer_u"] if ph % 2 == 0 else ap["peer_v"]
                with pool.Fori(0, NI) as i:
                    for half in range(2):
                        a, b = half * GRP // 2, (half + 1) * GRP // 2
                        pool.wait_ge(u_used, i * GRP + (GRP * NI * ph + b))
                        pool.sem_inc(pool_step, 1)
                        pool.tensor_copy(idx8[:, a:b], eidx[:, t, bass.ds(i * GRP + a, b - a)]).then_inc(idx_cp, 1)
                        pool.wait_ge(idx_cp, i * 2 + (2 * NI * ph + half + 1))
                        pool.sem_inc(pool_step, 1)
                        for j in range(a, b):
                            pool.indirect_dma_start(ubuf[:, j, :], None, table,
                                                    bass.IndirectOffsetOnAxis(ap=idx8[:, j:j + 1], axis=0))\
                                .then_inc(u_land[j], 16)


def lay_out(inp):
    f32 = np.float32
    w = {k: np.asarray(v) for k, v in inp.items()}
    w = {k: (v[0] if k not in ("g_final", "final_g_2") else v) for k, v in w.items()}

    def kparts(m, k):
        return m.reshape(k, P, m.shape[1]).transpose(1, 0, 2)

    def block(m, k):
        b = np.zeros((P, BLK), f32)
        b[:, :k * m.shape[1]] = kparts(m, k).reshape(P, -1)
        return b

    def blocks(m, k, width):
        return [block(m[:, i:i + width], k) for i in range(0, m.shape[1], width)]

    def swap(m):
        return np.concatenate([m[:, 16:32], m[:, 0:16]], axis=1)

    wi = w["w_in"]
    q, kc, vc, ks, vs, kw, vw, zg, qd, kvd, kr, ga, gb = np.split(
        wi, np.cumsum([512, 128, 128, 128, 128, 128, 128, 24, 384, 256, 32, D]).tolist(), axis=1)
    qch = [q[:, h * DH:(h + 1) * DH] for c in range(HG) for h in (c, HG + c)]
    in1 = np.concatenate(qch + [ks, kw, kc, vc, qd, kvd, zg, np.zeros((D, 40), f32), kr, swap(kr), vs, vw], axis=1)
    uq = w["w_uq"]
    uqh = []
    for h in range(8):
        m = uq[:, h * 96:(h + 1) * 96]
        uqh += [m, swap(m[:, 64:96])]
    mq, mk, mv, mo, mi, mf, dq, dk, dv = np.split(
        w["w_in_2"], np.cumsum([512, 512, 512, 512, 4, 4, 512, 512]).tolist(), axis=1)
    gates = np.concatenate([mi, np.zeros((D, 28), f32), mf, np.zeros((D, 476), f32)], axis=1)
    keys = w["peer_sub_keys_2"].transpose(3, 0, 1, 2).reshape(P, 16 * NKEY)
    ada = blocks(w["w_ada"], KD, 512)
    stream = (
        ada[:4] + blocks(in1, KD, 512) + [block(np.concatenate(uqh, axis=1), 3)]
        + [block(np.concatenate([w["w_uk"], w["w_uv"]], axis=1), 2)]
        + [block(w["w_ck1"], 16), block(w["w_cv1"], 16)]
        + blocks(np.concatenate([ga, gb], axis=1), KD, 512) + ada[4:]
        + [block(w["w_o_nsa"], 4), block(w["w_o_mla"], 4)] + blocks(w["w_out"], KD, 512)
        + blocks(w["w_fc1"], KD, 512) + blocks(w["w_fc2"], 32, P)
        + blocks(w["ada_w_2"], KD, 512)
        + [block(m, KD) for m in (mq, mk, mo, dq, dk, gates, mv, dv)] + blocks(w["w_out_2"], KD, 512)
        + blocks(w["peer_w_query_2"], KD, 512) + [np.concatenate([keys, np.zeros((P, BLK - 16 * NKEY), f32)], axis=1)])
    assert len(stream) == NBLK

    def cols(v):
        return v.reshape(-1, P).T

    def rows(v, at):
        a = np.zeros((P, 1), f32)
        a[at:at + len(v), 0] = v
        return a

    lam = np.concatenate([w["lambda_q1_2"], w["lambda_k1_2"], w["lambda_q2_2"], w["lambda_k2_2"]])
    params = dict(
        c=cols(w["c"]), b_ada=cols(w["b_ada"]), g_mix=cols(w["g_mix"]), g_mlp=cols(w["g_mlp"]), g_cq=cols(w["g_cq"]),
        g_ckv=cols(w["g_ckv"]), c2=cols(w["c_2"]), ada_b2=cols(w["ada_b_2"]), n1g=cols(w["norm1_g_2"]),
        n2g=cols(w["norm2_g_2"]), convw=w["conv_w_2"].reshape(4, 8, P).transpose(2, 1, 0).reshape(P, 32),
        convb=cols(w["conv_b_2"]), mng=cols(w["mlstm_norm_g_2"]), dng=cols(w["diff_norm_g_2"]),
        ck2=kparts(w["w_ck2"], 2).reshape(P, 128), cv2=kparts(w["w_cv2"], 2).reshape(P, 128),
        pek=w["pe_ck"].reshape(16, P).T, pev=w["pe_cv"].reshape(16, P).T,
        gb_i=rows(w["mlstm_gate_b_2"][:4], 0), gb_f=rows(w["mlstm_gate_b_2"][4:], 32),
        g_final=cols(w["g_final"]), lam=np.broadcast_to(lam, (P, 256)))
    return {
        "wstream": np.stack(stream), "params": np.concatenate([params[n] for n, _ in PARAMS], axis=1),
        "xT": w["x"].T.reshape(KD, P, S).transpose(1, 0, 2), "fgrow": np.broadcast_to(w["final_g_2"], (P, D)),
        "peer_u": w["peer_u_2"], "peer_v": w["peer_v_2"],
    }


def shape_tables():
    f32 = np.float32
    p = np.arange(P)[:, None]
    back = p - (np.arange(S)[None, :] - (S - P))
    mask = np.where(back >= 0, 0.0, -BIG)
    slope = 2.0 ** -(np.arange(NH) + 1.0)
    alibi = np.where(back[:, None, :] >= 0, -8.0 * slope[None, :, None] * back[:, None, :], -BIG)
    t = np.arange(T)[None, :, None] * P + p[:, :, None]
    far = t - (np.arange(NC) * CMP_STRIDE + CMP_END0)[None, None, :]
    biasc = np.where(far[:, :, None, :] >= 0, -8.0 * slope[None, None, :, None] * far[:, :, None, :], -BIG)
    inv = (f32(10000.0) ** (-np.arange(16, dtype=f32) / f32(16))).astype(f32)
    ang = (np.arange(S, dtype=f32)[None, :] * inv[:, None]).astype(f32)
    rope = np.zeros((P, S))
    rope[64:80], rope[80:96] = np.cos(ang), np.cos(ang)
    rope[96:112], rope[112:128] = -np.sin(ang), np.sin(ang)
    sel = np.zeros((P, S))
    for h in range(4):
        sel[h, h * P:(h + 1) * P] = 1.0
    tab = dict(ident=np.eye(P), mask=mask, rope=rope, sel=sel, iota=np.broadcast_to(np.arange(PK), (P, PK)))
    return {"consts": np.concatenate([tab[n] for n, _ in CONSTS], axis=1).astype(f32), "alibi": alibi.astype(f32),
            "biasc": biasc.astype(f32)}


def kernel(**inputs):
    import concourse.bacc as bacc
    from concourse.bass_utils import run_bass_kernel_spmd

    nc = bacc.Bacc("TRN2", target_bir_lowering=False, num_devices=1)
    arrays = {k: np.ascontiguousarray(v) for k, v in {**lay_out(inputs), **shape_tables()}.items()}
    ap = {n: nc.dram_tensor("in_" + n, a.shape, mybir.dt.from_np(a.dtype), kind="ExternalInput").ap() for n, a in arrays.items()}
    out = nc.dram_tensor("result", (S, D), F32, kind="ExternalOutput").ap()
    build(nc, ap, out)
    r = run_bass_kernel_spmd(nc, [{"in_" + n: a for n, a in arrays.items()}], core_ids=[0])
    return r.results[0]["result"].reshape(1, S, D)
```

```python
from contextlib import ExitStack

import numpy as np

import concourse.bass as bass
from concourse import mybir

ALU = mybir.AluOpType
ACT = mybir.ActivationFunctionType
AXX = mybir.AxisListType.X
F32 = mybir.dt.float32
U32 = mybir.dt.uint32

P = 128
D = 1024
S = 512
T = S // P
KD = D // P
FF = 4 * D
EPS = 1e-6
BIG = 1e30
NH, NG, HG, DH = 8, 2, 4, 64
NC = S // 16 - 1
CMP_END0, CMP_STRIDE = 31, 16
MLA_SCALE = 96.0 ** -0.5
NSA_SCALE = 64.0 ** -0.5
MH = 4
PH, PK, NKEY = 8, 16, 128
NEXP = NKEY * NKEY
NSLOT = PH * PK
GRP = 8
BLK = 4096
MLA_FENCE = 7

STREAM = [
    ("in1", [(4, 4)] * 3 + [(6, 6)]), ("uq", [(8, 8)]), ("ukv", [(8, 8)]),
    ("ck", [(1, 0)]), ("cv", [(1, 0)]), ("gab", [(4, 4)] * 4), ("on", [(8, 8)]), ("om", [(8, 8)]), ("out1", [(4, 4)] * 2), ("fc1", [(4, 4)] * 8),
    ("fc2", [(1, 1)] * 8), ("in2", [(4, 4)] * 5 + [(1, 1)] + [(4, 4)] * 2), ("out2", [(4, 4)] * 2),
    ("pqa", [(4, 4)] * 4), ("pqb", [(4, 4)] * 4),
]
BLOCK0, MM0, EV0, MM_THROUGH = {}, {}, {}, []
_b = _m = _e = 0
for _name, _blocks in STREAM:
    BLOCK0[_name], MM0[_name], EV0[_name] = _b, _m, _e
    for _mm, _ev in _blocks:
        _b, _m, _e = _b + 1, _m + _mm, _e + _ev
        MM_THROUGH.append(_m)
NBLK = _b

PARAMS = [("c", 8), ("b_ada", 48), ("g_mix", 8), ("g_mlp", 8), ("g_cq", 3), ("g_ckv", 2), ("c2", 8),
          ("ada_b2", 48), ("n1g", 8), ("n2g", 8), ("convw", 32), ("convb", 8), ("mng", 4), ("dng", 1),
          ("ck2", 128), ("cv2", 128), ("pek", 16), ("pev", 16), ("gb_i", 1), ("gb_f", 1), ("g_final", 8), ("lam", 256)]
PCOL, _o = {}, 0
for _n, _w in PARAMS:
    PCOL[_n] = _o
    _o += _w
NPRM = _o
CONSTS = [("ident", 128), ("mask", 512), ("rope", 512), ("sel", 512), ("iota", 16)]
CCOL, _o = {}, 0
for _n, _w in CONSTS:
    CCOL[_n] = _o
    _o += _w
NCST = _o

NORMS = [("x", 8), ("cq", 3), ("ckv", 2), ("mid", 8), ("fin", 8), ("n1", 8), ("n2", 8)]
NORM0, _o = {}, 0
for _i, (_n, _w) in enumerate(NORMS):
    NORM0[_n] = (_o, _i)
    _o += _w


def build(nc, ap, out):
    with ExitStack() as ctx:
        def sb(name, shape, dt=F32):
            return ctx.enter_context(nc.sbuf_tensor(name, shape, dt))

        def sem(name):
            return ctx.enter_context(nc.semaphore(name))

        PS = ctx.enter_context(nc.psum_tensor("PS", [P, 8, 512], F32))
        ring = [sb(f"ring{i}", [P, BLK]) for i in range(2)]
        xT = sb("xT", [P, KD, S])
        hT = sb("hT", [P, KD, S])
        prm = sb("prm", [P, NPRM])
        cst = sb("cst", [P, NCST])
        ones = sb("ones", [P, P])
        sq = sb("sq", [P, 2, S])
        rstd = sb("rstd", [P, S])
        modc = sb("modc", [P, 48])
        modc2 = sb("modc2", [P, 48])
        scl = sb("scl", [P, 16])
        smalls = sb("smalls", [P, 512])
        ARENA = 32100
        arena = sb("arena", [P, ARENA])

        def area(kib, *dims, parts=P):
            n = int(np.prod(dims))
            o = int(kib * 256)
            assert o + n <= ARENA, (kib, dims)
            a = arena[0:parts, o:o + n]
            if len(dims) == 2:
                return a.rearrange("p (a b) -> p a b", a=dims[0])
            if len(dims) == 3:
                return a.rearrange("p (a b c) -> p a b c", a=dims[0], b=dims[1])
            return a

        def prow(name, a=0, b=None, rows=slice(0, P)):
            w = dict(PARAMS)[name]
            return prm[rows, PCOL[name] + a:PCOL[name] + (w if b is None else b)]

        def const(name, rows=slice(0, P)):
            return cst[rows, CCOL[name]:CCOL[name] + dict(CONSTS)[name]]

        ident = const("ident")
        mask = const("mask")

        zT = area(0, 14, S)
        vtok = area(28, T, 256)
        qm = area(32, 8, S)
        km = area(48, 8, S)
        vm = area(64, T, S)
        alibi = area(72, 8, S)
        biasc = area(88, T, 8, NC)
        onT = area(92, 4, S)
        omT = area(100, 4, S)
        sneg = area(108, 2, S)
        prob = area(112, 2, S)
        probT = area(116, 2, S)
        otok = area(120, S)
        otmp = area(122, S)
        cqT = area(108, 3, S)
        ckvT = area(114, 2, S)
        rt = area(118, 2, S)
        stk = [area(108, 3, S), area(114, 3, S)]
        adaw = [area(32, BLK), area(48, BLK)]
        adas = area(64, 2, S)
        gT = area(0, 16, S)
        yT = area(32, 8, S)
        ytmp = area(48, 2, S)
        aT = area(0, 32, S)
        rbuf = area(64, 2, S)
        uT = area(0, 8, S + 3)
        qk2 = area(17, 8, S)
        mo = area(33, 4, S)
        dqk = area(41, 8, S)
        mv = area(57, T, S)
        dv = area(65, T, S)
        zG = area(73, S)
        grow = area(75, 8, S)
        abc = area(91, 4, S)
        abcm = area(99, 4, S)
        catT = hT
        pqt = area(0, 16, S)
        skw = area(32, 16, NKEY)
        sc = area(40, 16, NKEY)
        cand = area(48, PH, PK * PK)
        oneh = area(48, NSLOT, PK)
        h2tok = area(56, 2, D)
        ubuf = area(64, GRP, D)
        acc = area(96, 2, D)
        diag = area(104, GRP, P)
        fgrow = area(108, D)
        eidx = area(112, T, NSLOT).bitcast(U32)
        gate = area(114, T, NSLOT)
        dots = area(116, NSLOT)
        wexp = area(117, T, NSLOT)
        tkv = area(119, 16, PK)
        tki = area(120, 16, PK).bitcast(U32)
        tkf = area(121, 16, PK)
        fpos = area(122, NSLOT).bitcast(U32)
        fpi = area(122.5, NSLOT).bitcast(U32)
        fpf = area(123, NSLOT)
        fval = area(123.5, NSLOT)
        selv = area(124, 2, NSLOT)
        sm8 = area(125, 4, PH)
        g2row = sq
        zeros = rstd[:, 0:P]

        def small(a, n, rows=slice(0, P)):
            return smalls[rows, a:a + n]

        hid = small(0, 124)
        hb = small(124, 2)
        kcT = small(126, NC)
        vcm = small(157, 128)
        gtok = small(285, 96)
        rs = small(381, 48)
        nmx = small(429, 2)
        coef = small(431, 24)
        tok8 = small(0, 32)
        lamc = small(32, 8)
        ss4 = small(40, 16)
        dots8 = small(60, 8)
        w8 = small(68, 8)
        idx8 = small(76, 8).bitcast(U32)
        ssf = small(84, 4)

        loaded = sem("loaded")
        ready = sem("constants_ready")
        w_loaded = [sem("w_loaded0"), sem("w_loaded1")]
        mm_done = sem("mm_done")
        evac = sem("evac")
        tables = sem("tables_loaded")
        ada_loaded = [sem("ada_loaded0"), sem("ada_loaded1")]
        ada_summed, ada_taken = sem("ada_summed"), sem("ada_taken")
        stage_done = sem("stage_done")
        act_own = sem("act_own")
        dve_own = sem("dve_own")
        nrm_sq, nrm_mm, nrm_ms, nrm_rt, nrm_h = (sem(n) for n in ("nrm_sq", "nrm_mm", "nrm_ms", "nrm_rt", "nrm_h"))
        stored = sem("stored")

        class Own:

            def __init__(self, eng, s):
                self.eng, self.s, self.n = eng, s, 0

            def __call__(self, ins):
                self.n += 1
                ins.then_inc(self.s, 1)
                self.eng.wait_ge(self.s, self.n)

            def mark(self, ins):
                self.n += 1
                ins.then_inc(self.s, 1)

            def wait(self):
                self.eng.wait_ge(self.s, self.n)

        fences = {}

        def fence(eng, name):
            k = fences[name] = fences.get(name, 0) + 1
            eng.drain().then_inc(stage_done, 1)
            eng.wait_ge(stage_done, 3 * k)

        def tile(i):
            return slice(i * P, (i + 1) * P)

        def bank(b, n=512, rows=slice(0, P)):
            return PS[rows, b, 0:n]

        def block_arrived(pe, n):
            pe.wait_ge(w_loaded[n % 2], 16 * (n // 2 + 1))

        def norm_act(act, name, src, n, dst=None, shift=None):
            b, k = NORM0[name]
            for c in range(n):
                if b + c >= 2:
                    act.wait_ge(nrm_mm, b + c - 1)
                act.activation(sq[:, c % 2, :], src(c), ACT.Square).then_inc(nrm_sq, 1)
            act.wait_ge(nrm_ms, k + 1)
            act.activation(rstd[:, :], rstd[:, :], ACT.Sqrt).then_inc(nrm_rt, 1)
            if shift is not None:
                for c in range(n):
                    act.wait_ge(nrm_h, b + c + 1)
                    act.activation(dst(c), dst(c), ACT.Identity, bias=shift(c))

        def norm_pe(pe, name, n):
            b, k = NORM0[name]
            if k:
                pe.wait_ge(nrm_ms, k)
            for c in range(n):
                pe.wait_ge(nrm_sq, b + c + 1)
                pe.matmul(bank(7), ones[:, :], sq[:, c % 2, :], start=(c == 0), stop=(c == n - 1)).then_inc(nrm_mm, 1)

        def norm_dve(dve, own, name, src, n, dst, gain):
            b, k = NORM0[name]
            dve.wait_ge(nrm_mm, b + n)
            if b:
                dve.wait_ge(nrm_h, b)
            dve.tensor_scalar(rstd[:, :], bank(7), 1.0 / (n * P), EPS, ALU.mult, ALU.add).then_inc(nrm_ms, 1)
            dve.wait_ge(nrm_rt, k + 1)
            own(dve.reciprocal(rstd[:, :], rstd[:, :]))
            for c in range(n):
                dve.scalar_tensor_tensor(out=dst(c), in0=src(c), scalar=gain(c), in1=rstd[:, :],
                                         op0=ALU.mult, op1=ALU.mult).then_inc(nrm_h, 1)

        def ada_sum(dve, own, n, vec):
            dve.wait_ge(ada_loaded[n % 2], 16 * (n // 2 + 1))
            if n >= 2:
                dve.wait_ge(ada_taken, n - 1)
            w = adaw[n % 2].rearrange("p (k m) -> p k m", k=KD)
            own(dve.tensor_scalar(adas[:, n % 2, :], w[:, 0, :], vec(0), None, ALU.mult))
            for k in range(1, KD):
                ins = dve.scalar_tensor_tensor(out=adas[:, n % 2, :], in0=w[:, k, :], scalar=vec(k), in1=adas[:, n % 2, :],
                                               op0=ALU.mult, op1=ALU.add)
                if k < KD - 1:
                    own(ins)
            ins.then_inc(ada_summed, 1)

        def ada_take(pe, n):
            pe.wait_ge(ada_summed, n + 1)
            for m in range(4):
                ins = pe.matmul(PS[:, 6, 4 * n + m:4 * n + m + 1], adas[:, n % 2, tile(m)], ones[:, 0:1],
                                start=True, stop=True)
            ins.then_inc(ada_taken, 1)

        def ada_bias(dve, own, dst, n0, n1, bias):
            dve.wait_ge(ada_taken, n1)
            c = slice(4 * n0 % 48, 4 * n0 % 48 + 4 * (n1 - n0))
            own(dve.tensor_tensor(dst[:, c], PS[:, 6, 4 * n0:4 * n1], bias[:, c], ALU.add))

        def chunk_pe(pe, name, j, lhs, rhs, dst=None, n=512):
            if j >= 2:
                pe.wait_ge(evac, EV0[name] + j - 1)
            o = bank(j % 2, n) if dst is None else dst
            for a, (l, r) in enumerate(zip(lhs, rhs)):
                ins = pe.matmul(o, l, r, start=(a == 0), stop=(a == len(lhs) - 1))
            ins.then_inc(mm_done, 1)

        def layer_pe(pe, name, nblk, kc, act_in):
            per = BLK // kc // P
            for n in range(nblk):
                g = BLOCK0[name] + n
                block_arrived(pe, g)
                w = ring[g % 2][:, :].rearrange("p (k m) -> p k m", k=kc)
                for m in range(per):
                    chunk_pe(pe, name, n * per + m, [w[:, k, m * P:(m + 1) * P] for k in range(kc)],
                             [act_in(k) for k in range(kc)])

        def layer_pe_loop(pe, name, nblk, kc, act_in, n=512):
            per = BLK // kc // P
            with pe.Fori(0, nblk // 2) as i:
                for s in range(2):
                    pe.wait_ge(w_loaded[s], i * 16 + 16 * (BLOCK0[name] // 2 + 1))
                    w = ring[s][:, :].rearrange("p (k m) -> p k m", k=kc)
                    for m in range(per):
                        j = s * per + m
                        pe.wait_ge(evac, i * (2 * per) + EV0[name] + j - 1)
                        for k in range(kc):
                            ins = pe.matmul(bank(j % 2, n), w[:, k, m * P:(m + 1) * P], act_in(k),
                                            start=(k == 0), stop=(k == kc - 1))
                        ins.then_inc(mm_done, 1)

        class Attention:

            def __init__(self, name, units, kind, n_tok_cols=512):
                self.units, self.kind, self.name = units, kind, name
                self.last = [u for u in range(len(units)) if u + 1 == len(units) or units[u + 1]["tile"] != units[u]["tile"]]
                self.scored = sem(f"{name}_scored")
                self.weighed = sem(f"{name}_weighed")
                self.exped = sem(f"{name}_exped")
                self.turned = sem(f"{name}_turned")
                self.copied = sem(f"{name}_copied")
                self.summed = sem(f"{name}_summed")
                self.banks_free = sem(f"{name}_banks_free")
                self.tok_ready = sem(f"{name}_tok_ready")
                self.tok_turned = sem(f"{name}_tok_turned")
                self.tok_out = sem(f"{name}_tok_out")
                self.ms_ready = sem(f"{name}_ms_ready")
                self.root_ready = sem(f"{name}_root_ready")

            def pe(self, pe):
                U = self.units
                for u in range(len(U) + 7):
                    if u < len(U):
                        x = U[u]
                        if u >= 2:
                            pe.wait_ge(self.weighed, u - 1)
                        for (l, r, o) in x["scores"](u % 2):
                            ins = pe.matmul(o, l, r, start=True, stop=True)
                        ins.then_inc(self.scored, 1)
                    v = u - 1
                    if 0 <= v < len(U):
                        pe.wait_ge(self.weighed if self.kind == "mlstm" else self.exped, v + 1)
                        if v >= 2:
                            pe.wait_ge(self.copied, v - 1)
                        for (o, i, n) in U[v]["turns"](v % 2):
                            ins = pe.transpose(o, i, ident[0:n, 0:n])
                        ins.then_inc(self.turned, 1)
                    v = u - 2
                    if 0 <= v < len(U):
                        pe.wait_ge(self.copied, v + 1)
                        t = U[v]["tile"]
                        if t > 0 and (v - 1) in self.last:
                            pe.wait_ge(self.banks_free, t)
                        for (o, pairs) in U[v]["values"](v % 2):
                            for a, (l, r) in enumerate(pairs):
                                ins = pe.matmul(o, l, r, start=(a == 0), stop=(a == len(pairs) - 1))
                        ins.then_inc(self.summed, 1)
                    v = u - 5
                    if v in self.last:
                        t = U[v]["tile"]
                        pe.wait_ge(self.tok_ready, t + 1)
                        if t > 0:
                            pe.wait_ge(self.tok_out, t)
                        for c in range(4):
                            ins = pe.transpose(PS[:, 7, tile(c)], otok[:, tile(c)], ident)
                        ins.then_inc(self.tok_turned, 1)

            def act(self, act):
                U = self.units
                for u in range(len(U) + 7):
                    if u < len(U):
                        x = U[u]
                        if self.kind == "mlstm":
                            if u >= 2:
                                act.wait_ge(self.weighed, u - 1)
                        else:
                            act.wait_ge(self.weighed, u + 1)
                            if u >= 2:
                                act.wait_ge(self.turned, u - 1)
                        ins = x["exp"](act, u % 2)
                        ins.then_inc(self.exped, 1)
                    v = u - 1
                    if 0 <= v < len(U):
                        act.wait_ge(self.turned, v + 1)
                        if v >= 2:
                            act.wait_ge(self.summed, v - 1)
                        n, r = U[v]["tcols"], U[v]["trows"]
                        act.activation(probT[0:r, v % 2, 0:n], PS[0:r, 2 + v % 2, 0:n], ACT.Copy).then_inc(self.copied, 1)
                    if u - 3 in self.last and self.root is not None:
                        t = U[u - 3]["tile"]
                        act.wait_ge(self.ms_ready, t + 1)
                        act.activation(self.root, self.root, ACT.Sqrt).then_inc(self.root_ready, 1)
                    if u - 6 in self.last and self.out_act is not None:
                        t = U[u - 6]["tile"]
                        act.wait_ge(self.tok_turned, t + 1)
                        act.activation(self.out_act[:, :, tile(t)], bank(7).rearrange("p (c t) -> p c t", c=4),
                                       ACT.Copy).then_inc(self.tok_out, 1)

            def dve(self, dve, own):
                U = self.units
                for u in range(len(U) + 7):
                    if u < len(U):
                        dve.wait_ge(self.scored, u + 1)
                        if self.kind == "mlstm":
                            dve.wait_ge(self.exped, u + 1)
                            if u >= 2:
                                dve.wait_ge(self.turned, u - 1)
                        elif u >= 2:
                            dve.wait_ge(self.exped, u - 1)
                        U[u]["weigh"](dve, own, u % 2).then_inc(self.weighed, 1)
                    if 0 <= u - 1 < len(U) and U[u - 1].get("rowsum"):
                        dve.wait_ge(self.exped, u)
                        U[u - 1]["rowsum"](dve, own, (u - 1) % 2)
                    if u - 2 in self.last:
                        t = U[u - 2]["tile"]
                        dve.wait_ge(self.summed, u - 1)
                        if t > 0:
                            dve.wait_ge(self.tok_turned, t)
                        self.finish_a(dve, own, t)
                    if u - 4 in self.last and self.finish_b is not None:
                        t = U[u - 4]["tile"]
                        dve.wait_ge(self.root_ready, t + 1)
                        self.finish_b(dve, own, t)
                    if u - 6 in self.last and self.out_dve is not None:
                        t = U[u - 6]["tile"]
                        dve.wait_ge(self.tok_turned, t + 1)
                        self.out_dve(dve, own, t).then_inc(self.tok_out, 1)

            root = out_act = finish_b = out_dve = None

        def softmax_unit(t, q, k, bias, scale, v, o, rsum):
            n = (t + 1) * P
            return dict(
                tile=t, tcols=n, trows=P,
                scores=lambda b: [(q, k, PS[:, b, 0:n])],
                weigh=lambda dve, own, b: dve.tensor_tensor_reduce(
                    sneg[:, b, 0:n], PS[:, b, 0:n], bias, -scale, BIG, ALU.add, ALU.min, nmx[:, b:b + 1]),
                exp=lambda act, b: act.activation(prob[:, b, 0:n], sneg[:, b, 0:n], ACT.Exp, scale=-1.0,
                                                  bias=nmx[:, b:b + 1], accum_out=rsum),
                turns=lambda b: [(PS[:, 2 + b, tile(kb)], prob[:, b, tile(kb)], P) for kb in range(t + 1)],
                values=lambda b: [(o, [(probT[:, b, tile(kb)], v(kb)) for kb in range(t + 1)])])

        def nsa_units():
            U = []
            for t in range(T):
                def q(h):
                    g = h // HG
                    return zT[g * DH:(g + 1) * DH, h % HG, tile(t)]
                for g in range(NG):
                    kc = kcT[g * DH:(g + 1) * DH, :]

                    def weigh(dve, own, b, g=g, t=t):
                        s3 = sneg[:, b, 0:P].rearrange("p (h j) -> p h j", h=HG)[:, :, 0:NC]
                        p3 = PS[:, b, 0:P].rearrange("p (h j) -> p h j", h=HG)[:, :, 0:NC]
                        own(dve.tensor_tensor(s3, p3, biasc[:, t, g * HG:(g + 1) * HG, :], ALU.add))
                        own(dve.tensor_reduce(ssf, s3, AXX, ALU.max))
                        own(dve.tensor_scalar(ssf, ssf, -1e20, None, ALU.max))
                        return dve.tensor_tensor(s3, s3, ssf.unsqueeze(2).to_broadcast([P, HG, NC]), ALU.subtract)

                    U.append(dict(
                        tile=t, tcols=512, trows=NC,
                        scores=lambda b, g=g, kc=kc, t=t: [
                            (zT[g * DH:(g + 1) * DH, a, tile(t)], kc, PS[:, b, 32 * a:32 * a + NC]) for a in range(HG)],
                        weigh=weigh,
                        exp=lambda act, b: act.activation(
                            prob[:, b, 0:P].rearrange("p (h j) -> p h j", h=HG)[:, :, 0:NC],
                            sneg[:, b, 0:P].rearrange("p (h j) -> p h j", h=HG)[:, :, 0:NC], ACT.Exp, scale=NSA_SCALE),
                        rowsum=lambda dve, own, b, g=g, t=t: own(dve.tensor_reduce(
                            rs[:, 24 * (t % 2) + g * HG:24 * (t % 2) + (g + 1) * HG],
                            prob[:, b, 0:P].rearrange("p (h j) -> p h j", h=HG)[:, :, 0:NC], AXX, ALU.add)),
                        turns=lambda b: [(PS[0:NC, 2 + b, tile(a)], prob[:, b, 32 * a:32 * a + NC], P) for a in range(HG)],
                        values=lambda b, g=g: [(PS[:, 4, (g * HG + a) * DH:(g * HG + a + 1) * DH],
                                                [(probT[0:NC, b, tile(a)], vcm[0:NC, g * DH:(g + 1) * DH])])
                                               for a in range(HG)]))
                for br in range(2):
                    for h in range(NH):
                        g = h // HG
                        r = 24 * (t % 2) + 8 * (br + 1) + h
                        U.append(softmax_unit(
                            t, q(h), zT[g * DH:(g + 1) * DH, 4 + br, 0:(t + 1) * P],
                            alibi[:, h, (T - 1 - t) * P:S], NSA_SCALE,
                            lambda kb, br=br, g=g: vtok[:, kb, br * P + g * DH:br * P + (g + 1) * DH],
                            PS[:, 5 + br, h * DH:(h + 1) * DH], rs[:, r:r + 1]))
            return U

        def mla_units():
            U = []
            for t in range(T):
                for h in range(NH):
                    r = 24 * (t % 2) + h
                    U.append(softmax_unit(
                        t, qm[0:96, h, tile(t)], km[0:96, h, 0:(t + 1) * P], mask[:, (T - 1 - t) * P:S], MLA_SCALE,
                        lambda kb, h=h: vm[:, kb, h * DH:(h + 1) * DH],
                        PS[:, 4, h * DH:(h + 1) * DH], rs[:, r:r + 1]))
            return U

        def diff_units():
            U = []
            for t in range(T):
                for p in range(2):
                    for h in range(MH):
                        r = 24 * (t % 2) + MH * p + h
                        U.append(softmax_unit(
                            t, dqk[p * DH:(p + 1) * DH, h, tile(t)], dqk[p * DH:(p + 1) * DH, 4 + h, 0:(t + 1) * P],
                            mask[:, (T - 1 - t) * P:S], NSA_SCALE,
                            lambda kb, h=h: dv[:, kb, tile(h)],
                            PS[:, 4 + p, tile(h)], rs[:, r:r + 1]))
            return U

        def mlstm_units():
            U = []
            for t in range(T):
                for h in range(MH):
                    n = (t + 1) * P
                    r = 24 * (t % 2) + h

                    def decay(act, b, h=h, t=t):
                        nm = tok8[:, 8 * t + h:8 * t + h + 1]
                        if t > 0:
                            act.activation(sneg[:, b, 0:t * P], abc[:, h, 0:t * P], ACT.Exp, bias=nm)
                        return act.activation(sneg[:, b, tile(t)], abcm[:, h, tile(t)], ACT.Exp, bias=nm)

                    U.append(dict(
                        tile=t, tcols=n, trows=P,
                        scores=lambda b, h=h, t=t, n=n: [(qk2[:, h, tile(t)], qk2[:, 4 + h, 0:n], PS[:, b, 0:n])],
                        exp=decay,
                        weigh=lambda dve, own, b, n=n, r=r: dve.tensor_tensor_reduce(
                            prob[:, b, 0:n], PS[:, b, 0:n], sneg[:, b, 0:n], float(P) ** -0.5, 0.0,
                            ALU.mult, ALU.add, rs[:, r:r + 1]),
                        turns=lambda b, t=t: [(PS[:, 2 + b, tile(kb)], prob[:, b, tile(kb)], P) for kb in range(t + 1)],
                        values=lambda b, h=h, t=t: [(PS[:, 4, tile(h)],
                                                     [(probT[:, b, tile(kb)], mv[:, kb, tile(h)]) for kb in range(t + 1)])]))
            return U

        def per_head(a, n, w):
            return a.unsqueeze(2).to_broadcast([P, n, w])

        def heads(a, n):
            return a.rearrange("p (h d) -> p h d", h=n)

        nsa = Attention("nsa", nsa_units(), "softmax")
        mla = Attention("mla", mla_units(), "softmax")
        mls = Attention("mls", mlstm_units(), "mlstm")
        dif = Attention("dif", diff_units(), "softmax")

        def nsa_finish(dve, own, t):
            r = rs[:, 24 * (t % 2):24 * (t % 2) + 24]
            own(dve.tensor_scalar(coef, r, 1e-30, None, ALU.max))
            own(dve.reciprocal(coef, coef))
            own(dve.tensor_tensor(coef, coef, gtok[:, 24 * t:24 * t + 24], ALU.mult))
            own(dve.tensor_tensor(heads(otok, NH), heads(bank(4), NH), per_head(coef[:, 0:8], NH, DH), ALU.mult))
            own(dve.tensor_tensor(heads(otmp, NH), heads(bank(5), NH), per_head(coef[:, 8:16], NH, DH), ALU.mult))
            own(dve.tensor_tensor(otok, otok, otmp, ALU.add))
            ins = dve.tensor_tensor(heads(otmp, NH), heads(bank(6), NH), per_head(coef[:, 16:24], NH, DH), ALU.mult)
            ins.then_inc(nsa.banks_free, 1)
            dve.wait_ge(nsa.banks_free, t + 1)
            dve.tensor_tensor(otok, otok, otmp, ALU.add).then_inc(nsa.tok_ready, 1)

        def mla_finish(dve, own, t):
            r = rs[:, 24 * (t % 2):24 * (t % 2) + 8]
            own(dve.tensor_scalar(coef[:, 0:8], r, 1e-30, None, ALU.max))
            own(dve.reciprocal(coef[:, 0:8], coef[:, 0:8]))
            ins = dve.tensor_tensor(heads(otok, NH), heads(bank(4), NH), per_head(coef[:, 0:8], NH, DH), ALU.mult)
            ins.then_inc(mla.banks_free, 1)

        def head_ms(dve, own, att):
            own(dve.tensor_tensor(otmp, otok, otok, ALU.mult))
            own(dve.tensor_reduce(ss4[:, 0:4], heads(otmp, MH), AXX, ALU.add))
            dve.tensor_scalar(ss4[:, 0:4], ss4[:, 0:4], 1.0 / P, EPS, ALU.mult, ALU.add).then_inc(att.ms_ready, 1)

        def mls_finish(dve, own, t):
            den = rs[:, 24 * (t % 2):24 * (t % 2) + 4]
            own(dve.tensor_scalar(coef[:, 0:4], den, -1.0, None, ALU.mult))
            own(dve.tensor_tensor(coef[:, 0:4], coef[:, 0:4], den, ALU.max))
            own(dve.tensor_tensor(coef[:, 0:4], coef[:, 0:4], tok8[:, 8 * t + 4:8 * t + 8], ALU.max))
            own(dve.reciprocal(coef[:, 0:4], coef[:, 0:4]))
            ins = dve.tensor_tensor(heads(otok, MH), heads(bank(4), MH), per_head(coef[:, 0:4], MH, P), ALU.mult)
            ins.then_inc(mls.banks_free, 1)
            dve.wait_ge(mls.banks_free, t + 1)
            head_ms(dve, own, mls)

        def dif_finish(dve, own, t):
            r = rs[:, 24 * (t % 2):24 * (t % 2) + 8]
            own(dve.reciprocal(coef[:, 0:8], r))
            own(dve.tensor_scalar(coef[:, 4:8], coef[:, 4:8], lamc[:, 4:5], None, ALU.mult))
            own(dve.tensor_tensor(heads(otok, MH), heads(bank(4), MH), per_head(coef[:, 0:4], MH, P), ALU.mult))
            ins = dve.tensor_tensor(heads(otmp, MH), heads(bank(5), MH), per_head(coef[:, 4:8], MH, P), ALU.mult)
            ins.then_inc(dif.banks_free, 1)
            dve.wait_ge(dif.banks_free, t + 1)
            own(dve.tensor_tensor(otok, otok, otmp, ALU.subtract))
            head_ms(dve, own, dif)

        def head_norm(att):
            def finish(dve, own, t):
                own(dve.reciprocal(ss4[:, 0:4], ss4[:, 0:4]))
                dve.tensor_tensor(heads(otok, MH), heads(otok, MH), per_head(ss4[:, 0:4], MH, P), ALU.mult)\
                   .then_inc(att.tok_ready, 1)
            return finish

        def mls_out(dve, own, t):
            for h in range(MH):
                ins = dve.scalar_tensor_tensor(out=catT[:, h, tile(t)], in0=PS[:, 7, tile(h)], scalar=prow("mng", h, h + 1),
                                               in1=mo[:, h, tile(t)], op0=ALU.mult, op1=ALU.mult)
            return ins

        def dif_out(dve, own, t):
            return dve.tensor_scalar(catT[:, MH:2 * MH, tile(t)], bank(7).rearrange("p (c t) -> p c t", c=4),
                                     prow("dng"), 1.0 - 0.2, ALU.mult, ALU.mult)

        nsa.finish_a, nsa.out_act = nsa_finish, onT
        mla.finish_a, mla.out_act = mla_finish, omT
        mla.tok_ready = mla.banks_free
        mls.finish_a, mls.finish_b, mls.root, mls.out_dve = mls_finish, head_norm(mls), ss4[:, 0:4], mls_out
        dif.finish_a, dif.finish_b, dif.root, dif.out_dve = dif_finish, head_norm(dif), ss4[:, 0:4], dif_out

        g_sig, g_turn = sem("gates_sigmoid"), sem("gates_turned")
        c_stk, c_mm, c_pe, c_hid, c_out = (sem(n) for n in ("cmp_stacked", "cmp_hidden", "cmp_bias", "cmp_silu", "cmp_out"))
        y_tmp = sem("y_tmp")
        fc_sq = sem("fc_squared")
        cv_sum = sem("conv_summed")
        gr, gr_x = sem("gate_rows"), sem("gate_rows_abs")
        dot_cp = sem("dots_copied")
        sk_loaded, sk_done = sem("subkeys_loaded"), sem("subkey_scores")
        wexp_ok, diag_ok, pe_used = sem("expert_weights"), sem("diagonals"), sem("slots_used_pe")
        v_sum, x_turned, tile_read = sem("v_summed"), sem("x_turned"), sem("tile_read")
        zero_ok = sem("zeros_ready")
        gr_act = sem("gate_rows_act")
        gr_pe = sem("gate_rows_pe")
        lam_s, lam_e = sem("lam_sums"), sem("lam_exps")
        silu_c = sem("silu_c")
        tt_pe, tt_ev = sem("token_turned"), sem("token_copied")
        pk_ev, pk_top = sem("peer_scores_copied"), sem("peer_scores_used")
        pk_mx, pk_ex = sem("peer_gate_max"), sem("peer_gate_exp")
        u_land = [sem(f"landed{j}") for j in range(GRP)]
        u_used = sem("slots_used")
        idx_cp, pool_step = sem("idx_copied"), sem("pool_step")
        top_done = sem("top_done")
        gl_done, fin_ms, fin_rt, fin_ok = (sem(n) for n in (
            "gelu_done", "final_ms", "final_root", "final_ready"))
        g2_pe, g2_ev = sem("g2_pe"), sem("g2_ev")

        block = ctx.enter_context(nc.Block())

        @block.sync
        def _(sp):
            for n in range(NBLK):
                if n >= 2:
                    sp.wait_ge(mm_done, MM_THROUGH[n - 2])
                src = n if n < BLOCK0["pqb"] else n - 4
                sp.dma_start(ring[n % 2][:, :], ap["wstream"][src]).then_inc(w_loaded[n % 2], 16)
            for t in range(T):
                sp.wait_ge(fin_ok, t + 1)
                sp.dma_start(out[t * P:(t + 1) * P, :], acc[:, 0, :]).then_inc(stored, 16)
            sp.wait_ge(stored, 16 * T)

        @block.tensor
        def _(pe):
            pe.wait_ge(loaded, 48)
            pe.wait_ge(ready, 1)
            norm_pe(pe, "x", KD)
            for n in range(4):
                ada_take(pe, n)
            fence(pe, "pe")
            name = "in1"
            for n in range(4):
                g = BLOCK0[name] + n
                block_arrived(pe, g)
                w = ring[g % 2][:, :].rearrange("p (k m) -> p k m", k=KD)
                for m in range(4 if n < 3 else 2):
                    chunk_pe(pe, name, 4 * n + m, [w[:, k, tile(m)] for k in range(KD)], [hT[:, k, :] for k in range(KD)])
                    if 4 * n + m >= 6:
                        ada_take(pe, 4 + 4 * n + m - 6)
            for t in range(T):
                chunk_pe(pe, name, 14 + t, [hT[:, k, tile(t)] for k in range(KD)],
                         [w[:, k, 256:512] for k in range(KD)], n=256)
            fence(pe, "pe")
            norm_pe(pe, "cq", 3)
            norm_pe(pe, "ckv", 2)
            pe.wait_ge(g_sig, 1)
            for t in range(T):
                ins = pe.transpose(PS[:, 6, 24 * t:24 * t + 24], sq[0:24, 0, tile(t)], ident[0:24, 0:24])
            ins.then_inc(g_turn, 1)
            fence(pe, "pe")
            block_arrived(pe, BLOCK0["uq"])
            w = ring[BLOCK0["uq"] % 2][:, 0:3 * D].rearrange("p (k m) -> p k m", k=3)
            for h in range(NH):
                chunk_pe(pe, "uq", h, [w[:, k, tile(h)] for k in range(3)], [cqT[:, k, :] for k in range(3)])
            block_arrived(pe, BLOCK0["ukv"])
            w = ring[BLOCK0["ukv"] % 2][:, 0:2 * D].rearrange("p (k m) -> p k m", k=2)
            for c in range(4):
                chunk_pe(pe, "uq", 8 + c, [w[:, k, tile(c)] for k in range(2)], [ckvT[:, k, :] for k in range(2)])
            for t in range(T):
                chunk_pe(pe, "uq", 12 + t, [ckvT[:, k, tile(t)] for k in range(2)], [w[:, k, 512:1024] for k in range(2)])
            fence(pe, "pe")
            for r in range(2):
                n = BLOCK0["ck"] + r
                block_arrived(pe, n)
                w = ring[n % 2][:, :].rearrange("p (l m) -> p l m", l=16)
                if r == 0:
                    pe.wait_ge(c_stk, 10)
                for hc in range(2):
                    for l in range(16):
                        rhs = stk[r][:, :, 2 * l:2 * l + 16 * (NC - 1) + 1:16]
                        ins = pe.matmul(PS[:, 2 * r + hc, 0:3 * NC].rearrange("p (g j) -> p g j", g=3), w[:, l, tile(hc)],
                                        rhs, start=(l == 0), stop=(l == 15))
                ins.then_inc(mm_done, 1)
                pe.wait_ge(c_hid, 2 * r + 2)
                if r == 0:
                    for g in range(NG):
                        for hc in range(2):
                            ins = pe.matmul(PS[g * DH:(g + 1) * DH, 0, 128:128 + NC], prow("ck2", hc * DH, (hc + 1) * DH),
                                            hid[:, hc * 62 + g * NC:hc * 62 + (g + 1) * NC], start=(hc == 0), stop=(hc == 1))
                    ins.then_inc(c_mm, 1)
                else:
                    for g in range(NG):
                        for hc in range(2):
                            ins = pe.matmul(PS[0:NC, 1, 128 + g * DH:128 + (g + 1) * DH],
                                            hid[:, hc * 62 + g * NC:hc * 62 + (g + 1) * NC],
                                            prow("cv2", hc * DH, (hc + 1) * DH), start=(hc == 0), stop=(hc == 1))
                    ins.then_inc(c_mm, 1)
            fence(pe, "pe")
            nsa.pe(pe)
            fence(pe, "pe")
            mla.pe(pe)
            fence(pe, "pe")
            for n in range(4):
                g = BLOCK0["gab"] + n
                block_arrived(pe, g)
                w = ring[g % 2][:, :].rearrange("p (k m) -> p k m", k=KD)
                for m in range(4):
                    chunk_pe(pe, "gab", 4 * n + m, [w[:, k, tile(m)] for k in range(KD)], [hT[:, k, :] for k in range(KD)])
                    if 4 * n + m >= 4:
                        ada_take(pe, 12 + 4 * n + m - 4)
            fence(pe, "pe")
            layer_pe(pe, "on", 1, 4, lambda k: onT[:, k, :])
            block_arrived(pe, BLOCK0["om"])
            w = ring[BLOCK0["om"] % 2][:, :].rearrange("p (k m) -> p k m", k=4)
            for m in range(8):
                chunk_pe(pe, "on", 8 + m, [w[:, k, tile(m)] for k in range(4)], [omT[:, k, :] for k in range(4)])
            fence(pe, "pe")
            layer_pe(pe, "out1", 2, KD, lambda k: yT[:, k, :])
            fence(pe, "pe")
            norm_pe(pe, "mid", KD)
            fence(pe, "pe")
            layer_pe_loop(pe, "fc1", 8, KD, lambda k: hT[:, k, :])
            fence(pe, "pe")
            layer_pe_loop(pe, "fc2", 8, 32, lambda k: aT[:, k, :])
            fence(pe, "pe")
            norm_pe(pe, "fin", KD)
            fence(pe, "pe")
            norm_pe(pe, "n1", KD)
            fence(pe, "pe")
            name = "in2"
            for n in range(8):
                g = BLOCK0[name] + n
                block_arrived(pe, g)
                w = ring[g % 2][:, :].rearrange("p (k m) -> p k m", k=KD)
                if n < 5:
                    for m in range(4):
                        chunk_pe(pe, name, 4 * n + m, [w[:, k, tile(m)] for k in range(KD)], [hT[:, k, :] for k in range(KD)])
                elif n == 5:
                    chunk_pe(pe, name, 20, [w[:, k, 0:P] for k in range(KD)], [hT[:, k, :] for k in range(KD)])
                else:
                    for t in range(T):
                        chunk_pe(pe, name, 21 + 4 * (n - 6) + t, [hT[:, k, tile(t)] for k in range(KD)],
                                 [w[:, k, :] for k in range(KD)])
            fence(pe, "pe")
            pe.wait_ge(gr, 1)
            for h in range(MH):
                ins = pe.matmul(PS[:, h, :], const("sel", slice(0, 4))[:, tile(h)], grow[0:4, 4, :], start=True, stop=True)
            ins.then_inc(gr_pe, 1)
            pe.wait_ge(gr_act, 3)
            for t in range(T):
                pe.transpose(PS[:, 4, 8 * t:8 * t + 4], grow[0:4, 6, tile(t)], ident[0:4, 0:4])
                ins = pe.transpose(PS[:, 4, 8 * t + 4:8 * t + 8], grow[0:4, 7, tile(t)], ident[0:4, 0:4])
            ins.then_inc(gr_pe, 1)
            fence(pe, "pe")
            mls.pe(pe)
            fence(pe, "pe")
            dif.pe(pe)
            fence(pe, "pe")
            layer_pe(pe, "out2", 2, KD, lambda k: catT[:, k, :])
            fence(pe, "pe")
            norm_pe(pe, "n2", KD)
            fence(pe, "pe")
            pe.wait_ge(sk_loaded, 16)

            def sub_scores(t, c):
                h = c // 2
                o = PS[:, 2 + h % 4, tile(2 * (h // 4) + c % 2)]
                return pe.matmul(o, pqt[:, c, tile(t)], skw[:, c, :], start=True, stop=True)

            def turn(src, t, half, b):
                for c in range(4):
                    ins = pe.transpose(PS[:, b, tile(c)], src[:, 4 * half + c, tile(t)], ident)
                return ins

            for j in range(20):
                n, m = j // 4, j % 4
                if j < 16:
                    g = BLOCK0["pqa"] + n
                    if m == 0:
                        block_arrived(pe, g)
                        w = ring[g % 2][:, :].rearrange("p (k m) -> p k m", k=KD)
                    chunk_pe(pe, "pqa", j, [w[:, k, tile(m)] for k in range(KD)], [hT[:, k, 0:256] for k in range(KD)], n=256)
                if 3 <= j < 19 and j % 2 == 1:
                    pe.wait_ge(evac, EV0["pqa"] + j - 1)
                    sub_scores(0, j - 3)
                    sub_scores(0, j - 2).then_inc(sk_done, 1)
            for b in range(4):
                if b >= 2:
                    pe.wait_ge(tt_ev, b - 1)
                turn(hT, b // 2, b % 2, 6 + b % 2).then_inc(tt_pe, 1)
            pe.wait_ge(tt_ev, 4)
            for k in range(KD):
                ins = pe.matmul(PS[:, 6 + k // 4, tile(k % 4)], modc2[:, 40 + k:41 + k].to_broadcast([P, P]), ident,
                                start=True, stop=True)
            ins.then_inc(g2_pe, 1)

            def scores_of(t):
                pe.wait_ge(pk_ev, PH - 1 + t)
                for c in range(16):
                    ins = sub_scores(t, c)
                ins.then_inc(sk_done, 1)

            scores_of(1)
            layer_pe_loop(pe, "pqb", 4, KD, lambda k: hT[:, k, 256:512], n=256)
            pe.wait_ge(evac, EV0["pqb"] + 16)
            scores_of(2)
            for t in range(T):
                if t > 0:
                    pe.wait_ge(tile_read, t)
                    if t + 1 < T:
                        for half in range(2):
                            ins = turn(hT, t + 1, half, half)
                        ins.then_inc(tt_pe, 1)
                        pe.wait_ge(tt_ev, 4 + t)
                for half in range(2):
                    ins = turn(xT, t, half, half)
                ins.then_inc(x_turned, 1)
                if t == 0:
                    pe.wait_ge(g2_ev, 1)
                    pe.wait_ge(zero_ok, 1)
                for b in range(2):
                    pe.matmul(bank(6 + b), zeros, xT[:, b, :], start=True, stop=False)
                for r in range(NSLOT // GRP):
                    for q in range(GRP // 2):
                        n = (t * (NSLOT // GRP) + r) * (GRP // 2) + q
                        pe.wait_ge(diag_ok, n + 1)
                        pe.wait_ge(u_land[2 * q + 1], 16 * ((2 * t + 1) * (NSLOT // GRP) + r + 1))
                        for b in range(2):
                            ins = pe.matmul(bank(6 + b), diag[:, n % GRP, :], ubuf[:, 2 * q + 1, b * 512:(b + 1) * 512],
                                            start=False, stop=False)
                        ins.then_inc(pe_used, 2)
                for b in range(2):
                    ins = pe.matmul(bank(6 + b), zeros, xT[:, b, :], start=False, stop=True)
                ins.then_inc(v_sum, 1)
                if t == 0:
                    scores_of(3)

        @block.scalar
        def _(act):
            own = Own(act, act_own)
            for dst, src in ((prm[:, :], ap["params"]), (xT[:, :, :], ap["xT"]), (cst[:, :], ap["consts"])):
                act.dma_start(dst, src).then_inc(loaded, 16)
            for dst, src in ((alibi, ap["alibi"]), (biasc, ap["biasc"])):
                act.dma_start(dst, src).then_inc(tables, 16)
            act.wait_ge(loaded, 48)
            act.activation(scl[:, 8:16], prow("c2"), ACT.Silu).then_inc(silu_c, 1)
            norm_act(act, "x", lambda c: xT[:, c, :], KD, lambda c: hT[:, c, :], lambda c: modc[:, c:c + 1])
            fence(act, "act")
            n = "in1"
            for j in range(18):
                act.wait_ge(mm_done, MM0[n] + j + 1)
                if j < 14:
                    act.activation(zT[:, j, :], bank(j % 2), ACT.Copy).then_inc(evac, 1)
                else:
                    act.activation(vtok[:, j - 14, :], bank(j % 2, 256), ACT.Copy).then_inc(evac, 1)
            fence(act, "act")
            norm_act(act, "cq", lambda c: zT[:, 8 + c, :], 3)
            norm_act(act, "ckv", lambda c: zT[:, 11 + c, :], 2)
            act.wait_ge(nrm_mm, NORM0["mid"][0])
            act.activation(sq[0:24, 0, :], zT[0:24, 13, :], ACT.Sigmoid).then_inc(g_sig, 1)
            act.wait_ge(g_turn, 1)
            act.activation(gtok, PS[:, 6, 0:96], ACT.Copy)
            fence(act, "act")
            fence(act, "act")
            for r in range(2):
                act.wait_ge(c_pe, 1 + r)
                act.wait_ge(c_mm, r) if r else None
                for hc in range(2):
                    act.activation(hid[:, hc * 62:(hc + 1) * 62], PS[:, 2 * r + hc, 0:2 * NC], ACT.Silu,
                                   bias=hb[:, hc:hc + 1]).then_inc(c_hid, 1)
            fence(act, "act")
            nsa.act(act)
            fence(act, "act")
            mla.act(act)
            fence(act, "act")
            with act.Fori(0, 2) as i:
                for j in range(8):
                    act.wait_ge(mm_done, i * 8 + (MM0["gab"] + j + 1))
                    act.activation(gT[:, bass.ds(i * 8 + j, 1), :].rearrange("p a n -> p (a n)"), bank(j % 2),
                                   ACT.Sigmoid).then_inc(evac, 1)
            fence(act, "act")
            fence(act, "act")
            fence(act, "act")
            norm_act(act, "mid", lambda c: xT[:, c, :], KD, lambda c: hT[:, c, :], lambda c: modc[:, 24 + c:25 + c])
            fence(act, "act")
            with act.Fori(0, 4) as i:
                for j in range(8):
                    act.wait_ge(evac, i * 8 + (EV0["fc1"] + j + 1))
                    act.activation(aT[:, bass.ds(i * 8 + j, 1), :].rearrange("p a n -> p (a n)"), rbuf[:, j % 2, :],
                                   ACT.Square).then_inc(fc_sq, 1)
            fence(act, "act")
            fence(act, "act")
            norm_act(act, "fin", lambda c: xT[:, c, :], KD)
            fence(act, "act")
            norm_act(act, "n1", lambda c: xT[:, c, :], KD, lambda c: hT[:, c, :], lambda c: modc2[:, c:c + 1])
            fence(act, "act")
            n = "in2"
            for j in range(29):
                act.wait_ge(mm_done, MM0[n] + j + 1)
                if j < 8:
                    ins = act.activation(uT[:, j, 3:S + 3], bank(j % 2), ACT.Copy)
                elif j < 12:
                    ins = act.activation(mo[:, j - 8, :], bank(j % 2), ACT.Sigmoid)
                elif j < 20:
                    ins = act.activation(dqk[:, j - 12, :], bank(j % 2), ACT.Copy)
                elif j == 20:
                    ins = act.activation(zG, bank(j % 2), ACT.Copy)
                elif j < 25:
                    ins = act.activation(mv[:, j - 21, :], bank(j % 2), ACT.Copy)
                else:
                    ins = act.activation(dv[:, j - 25, :], bank(j % 2), ACT.Copy)
                ins.then_inc(evac, 1)
            for c in range(8):
                act.wait_ge(cv_sum, c + 1)
                act.activation(qk2[:, c, :], qk2[:, c, :], ACT.Silu, bias=prow("convb", c, c + 1))
            fence(act, "act")
            act.wait_ge(gr_x, 1)
            own(act.activation(grow[32:36, 1, :], grow[32:36, 1, :], ACT.Exp))
            act.activation(grow[32:36, 1, :], grow[32:36, 1, :], ACT.Ln, bias=1.0).then_inc(gr_act, 1)
            act.wait_ge(gr, 1)
            act.activation(grow[0:4, 6, :], grow[0:4, 5, :], ACT.Copy, scale=-1.0).then_inc(gr_act, 1)
            act.activation(grow[0:4, 7, :], grow[0:4, 3, :], ACT.Exp, scale=-1.0).then_inc(gr_act, 1)
            act.wait_ge(gr_pe, 1)
            act.activation(abc, PS[:, 0:4, :], ACT.Copy).then_inc(gr_act, 1)
            act.wait_ge(gr_pe, 2)
            act.activation(tok8, PS[:, 4, 0:32], ACT.Copy)
            act.wait_ge(lam_s, 1)
            act.activation(lamc[:, 2:4], lamc[:, 0:2], ACT.Exp).then_inc(lam_e, 1)
            fence(act, "act")
            mls.act(act)
            fence(act, "act")
            dif.act(act)
            fence(act, "act")
            act.dma_start(skw, ap["subkeys"]).then_inc(sk_loaded, 16)
            act.dma_start(fgrow, ap["fgrow"]).then_inc(g2_ev, 16)
            fence(act, "act")
            norm_act(act, "n2", lambda c: xT[:, c, :], KD, lambda c: hT[:, c, :], lambda c: modc2[:, 24 + c:25 + c])
            fence(act, "act")
            for j in range(20):
                if j < 16:
                    act.wait_ge(mm_done, MM0["pqa"] + j + 1)
                    act.activation(pqt[:, j, 0:256], bank(j % 2, 256), ACT.Copy).then_inc(evac, 1)
                if j >= 4 and j % 2 == 0:
                    h = (j - 4) // 2
                    act.wait_ge(sk_done, h + 1)
                    act.activation(sc[:, 2 * h:2 * h + 2, :].rearrange("p a n -> p (a n)"),
                                   PS[:, 2 + h % 4, (h // 4) * 256:(h // 4 + 1) * 256], ACT.Copy).then_inc(pk_ev, 1)
            for b in range(4):
                act.wait_ge(tt_pe, b + 1)
                act.activation(h2tok[:, b // 2, (b % 2) * 512:(b % 2 + 1) * 512], bank(6 + b % 2), ACT.Copy).then_inc(tt_ev, 1)
            act.wait_ge(g2_pe, 1)
            act.activation(g2row[:, :, :], PS[:, 6:8, :], ACT.Copy).then_inc(g2_ev, 1)
            act.wait_ge(pk_mx, 1)
            act.activation(gate[:, 0, :], gate[:, 0, :], ACT.Exp).then_inc(pk_ex, 1)

            def copy_scores(t):
                act.wait_ge(sk_done, PH + t)
                act.wait_ge(pk_top, t)
                act.activation(sc.rearrange("p (a b c) n -> p b a (c n)", a=2, b=4),
                               PS[:, 2:6, :].rearrange("p b (a n) -> p b a n", a=2), ACT.Copy).then_inc(pk_ev, 1)

            copy_scores(1)
            with act.Fori(0, 2) as i:
                for j in range(8):
                    act.wait_ge(mm_done, i * 8 + (MM0["pqb"] + j + 1))
                    act.activation(pqt[:, bass.ds(i * 8 + j, 1), 256:512].rearrange("p a n -> p (a n)"), bank(j % 2, 256),
                                   ACT.Copy).then_inc(evac, 1)
            for t in range(T):
                if 0 < t < T - 1:
                    act.wait_ge(tt_pe, 4 + t)
                    act.activation(h2tok[:, (t + 1) % 2, :].rearrange("p (a n) -> p a n", a=2), PS[:, 0:2, :],
                                   ACT.Copy).then_inc(tt_ev, 1)
                act.wait_ge(dot_cp, NSLOT // GRP * (t + 1) + 1)
                act.activation(dots, dots, ACT.Gelu).then_inc(gl_done, 1)
                act.wait_ge(wexp_ok, t + 1)
                for r in range(NSLOT // GRP):
                    for q in range(GRP // 2):
                        n = (t * (NSLOT // GRP) + r) * (GRP // 2) + q
                        if n >= GRP:
                            act.wait_ge(pe_used, GRP + 2 * (n - GRP + 1))
                        e = r * GRP + 2 * q + 1
                        act.activation(diag[:, n % GRP, :], ident, ACT.Copy, scale=wexp[:, t, e:e + 1]).then_inc(diag_ok, 1)
                    if r == 11 and t < T - 2:
                        copy_scores(t + 2)
                if t < T - 1:
                    act.wait_ge(pk_mx, t + 2)
                    act.activation(gate[:, t + 1, :], gate[:, t + 1, :], ACT.Exp).then_inc(pk_ex, 1)
                act.wait_ge(fin_ms, t + 1)
                act.activation(ssf[:, 0:1], ssf[:, 0:1], ACT.Sqrt).then_inc(fin_rt, 1)

        @block.vector
        def _(dve):
            own = Own(dve, dve_own)
            dve.memset(ones[:, :], 1.0).then_inc(ready, 1)
            dve.wait_ge(loaded, 48)
            for n in range(4):
                ada_sum(dve, own, n, lambda k: prow("c", k, k + 1))
            ada_bias(dve, own, modc, 0, 4, prow("b_ada"))
            own(dve.scalar_tensor_tensor(out=scl[:, 0:8], in0=modc[:, 8:16], scalar=1.0, in1=prow("g_mix"),
                                         op0=ALU.add, op1=ALU.mult))
            norm_dve(dve, own, "x", lambda c: xT[:, c, :], KD, lambda c: hT[:, c, :], lambda c: scl[:, c:c + 1])
            fence(dve, "dve")
            for n in range(4, 12):
                ada_sum(dve, own, n, lambda k: prow("c", k, k + 1))
            ada_bias(dve, own, modc, 4, 12, prow("b_ada"))
            fence(dve, "dve")
            norm_dve(dve, own, "cq", lambda c: zT[:, 8 + c, :], 3, lambda c: cqT[:, c, :], lambda c: prow("g_cq", c, c + 1))
            norm_dve(dve, own, "ckv", lambda c: zT[:, 11 + c, :], 2, lambda c: ckvT[:, c, :], lambda c: prow("g_ckv", c, c + 1))
            fence(dve, "dve")
            rope_k, rope_s = slice(64, 96), slice(96, 128)

            def rotate(src, dst):
                own(dve.tensor_tensor(rt[rope_k, 0, :], src[rope_k, :], const("rope", rope_k), ALU.mult))
                own(dve.tensor_tensor(rt[rope_k, 1, :], src[rope_s, :], const("rope", rope_s), ALU.mult))
                return dve.tensor_tensor(dst, rt[rope_k, 0, :], rt[rope_k, 1, :], ALU.add)

            own(rotate(zT[:, 13, :], km[rope_k, 0, :]))
            own(dve.tensor_copy(km[rope_k, 1:8, :], km[rope_k, 0:1, :].to_broadcast([32, 7, S])))
            for j in range(16):
                dve.wait_ge(mm_done, MM0["uq"] + j + 1)
                b = bank(j % 2)
                if j < 8:
                    own(dve.tensor_copy(qm[0:64, j, :], b[0:64, :]))
                    ins = rotate(b, qm[rope_k, j, :])
                elif j < 12:
                    own(dve.tensor_copy(km[0:64, 2 * (j - 8), :], b[0:64, :]))
                    ins = dve.tensor_copy(km[0:64, 2 * (j - 8) + 1, :], b[64:128, :])
                else:
                    ins = dve.tensor_copy(vm[:, j - 12, :], b)
                ins.then_inc(evac, 1)
            fence(dve, "dve")
            for r in range(2):
                src = zT[:, 6 + r, :]
                for g in range(NG):
                    dve.tensor_copy(stk[r][0:64, g, :], src[g * DH:(g + 1) * DH, :]).then_inc(c_stk, 1)
                    dve.tensor_copy(stk[r][64:128, g, 0:S - 1], src[g * DH:(g + 1) * DH, 1:S]).then_inc(c_stk, 1)
                own(dve.memset(stk[r][:, 2, :], 0.0))
                dve.tensor_copy(stk[r][:, 2, 0:32:2], prow("pek" if r == 0 else "pev")).then_inc(c_stk, 1)
            for r in range(2):
                dve.wait_ge(mm_done, MM0["ck"] + r + 1)
                if r:
                    dve.wait_ge(c_hid, 2)
                dve.tensor_copy(hb, PS[:, 2 * r:2 * r + 2, 2 * NC]).then_inc(c_pe, 1)
                dve.wait_ge(c_mm, r + 1)
                if r == 0:
                    own(dve.tensor_copy(kcT, PS[:, 0, 128:128 + NC]))
                else:
                    own(dve.tensor_copy(vcm[0:NC, :], PS[0:NC, 1, 128:256]))
            fence(dve, "dve")
            dve.wait_ge(tables, 32)
            nsa.dve(dve, own)
            fence(dve, "dve")
            mla.dve(dve, own)
            fence(dve, "dve")
            dve.wait_ge(silu_c, 1)
            for n in range(12, 24):
                ada_sum(dve, own, n, lambda k: scl[:, 8 + k:9 + k])
            ada_bias(dve, own, modc2, 12, 24, prow("ada_b2"))
            fence(dve, "dve")
            for j in range(16):
                dve.wait_ge(mm_done, MM0["on"] + j + 1)
                if j < 8:
                    dve.tensor_tensor(yT[:, j, :], gT[:, j, :], bank(j % 2), ALU.mult).then_inc(evac, 1)
                else:
                    if j == 8:
                        dve.wait_ge(evac, EV0["on"] + 8)
                    if j >= 10:
                        dve.wait_ge(y_tmp, j - 9)
                    dve.tensor_tensor(ytmp[:, j % 2, :], gT[:, j, :], bank(j % 2), ALU.mult).then_inc(evac, 1)
                    dve.wait_ge(evac, EV0["on"] + j + 1)
                    dve.tensor_tensor(yT[:, j - 8, :], yT[:, j - 8, :], ytmp[:, j % 2, :], ALU.add).then_inc(y_tmp, 1)
            fence(dve, "dve")

            def residual(name, mod, gcol):
                for j in range(8):
                    dve.wait_ge(mm_done, MM0[name] + j + 1)
                    dve.scalar_tensor_tensor(out=xT[:, j, :], in0=bank(j % 2), scalar=mod[:, gcol + j:gcol + j + 1],
                                             in1=xT[:, j, :], op0=ALU.mult, op1=ALU.add).then_inc(evac, 1)

            residual("out1", modc, 16)
            fence(dve, "dve")
            own(dve.scalar_tensor_tensor(out=scl[:, 0:8], in0=modc[:, 32:40], scalar=1.0, in1=prow("g_mlp"),
                                         op0=ALU.add, op1=ALU.mult))
            norm_dve(dve, own, "mid", lambda c: xT[:, c, :], KD, lambda c: hT[:, c, :], lambda c: scl[:, c:c + 1])
            fence(dve, "dve")
            for j in range(2):
                dve.memset(rbuf[:, j, :], 0.0).then_inc(fc_sq, 1)
            dve.wait_ge(fc_sq, 2)
            with dve.Fori(0, 4) as i:
                for j in range(8):
                    dve.wait_ge(mm_done, i * 8 + (MM0["fc1"] + j + 1))
                    dve.wait_ge(fc_sq, i * 8 + (j + 1))
                    dve.tensor_scalar(rbuf[:, j % 2, :], bank(j % 2), 0.0, None, ALU.max).then_inc(evac, 1)
            fence(dve, "dve")
            residual("fc2", modc, 40)
            fence(dve, "dve")
            norm_dve(dve, own, "fin", lambda c: xT[:, c, :], KD, lambda c: xT[:, c, :], lambda c: prow("g_final", c, c + 1))
            fence(dve, "dve")
            own(dve.scalar_tensor_tensor(out=scl[:, 0:8], in0=modc2[:, 8:16], scalar=1.0, in1=prow("n1g"),
                                         op0=ALU.add, op1=ALU.mult))
            norm_dve(dve, own, "n1", lambda c: xT[:, c, :], KD, lambda c: hT[:, c, :], lambda c: scl[:, c:c + 1])
            fence(dve, "dve")
            own(dve.memset(uT[:, :, 0:3], 0.0))
            for c in range(8):
                dve.wait_ge(evac, EV0["in2"] + c + 1)
                for j in range(4):
                    wj = prow("convw", 4 * c + j, 4 * c + j + 1)
                    src = uT[:, c, j:j + S]
                    if j == 0:
                        own(dve.tensor_scalar(qk2[:, c, :], src, wj, None, ALU.mult))
                    else:
                        ins = dve.scalar_tensor_tensor(out=qk2[:, c, :], in0=src, scalar=wj, in1=qk2[:, c, :],
                                                       op0=ALU.mult, op1=ALU.add)
                        if j < 3:
                            own(ins)
                ins.then_inc(cv_sum, 1)
            fence(dve, "dve")
            f = slice(32, 36)
            own(dve.tensor_scalar(grow[f, 0, :], zG[f, :], prow("gb_f", rows=f), None, ALU.add))
            own(dve.tensor_scalar(grow[f, 1, :], grow[f, 0, :], -1.0, None, ALU.mult))
            own(dve.tensor_scalar(grow[f, 2, :], grow[f, 0, :], 0.0, None, ALU.min))
            dve.tensor_tensor(grow[f, 1, :], grow[f, 1, :], grow[f, 0, :], ALU.min).then_inc(gr_x, 1)
            dve.wait_ge(gr_act, 1)
            r4 = slice(0, 4)
            own(dve.tensor_tensor(grow[r4, 0, :], grow[f, 2, :], grow[f, 1, :], ALU.subtract))
            own(dve.memset(grow[r4, 1, :], 1.0))
            own(dve.tensor_tensor_scan(grow[r4, 2, :], grow[r4, 1, :], grow[r4, 0, :], 0.0, ALU.mult, ALU.add))
            own(dve.scalar_tensor_tensor(out=grow[r4, 4, :], in0=zG[r4, :], scalar=prow("gb_i", rows=r4), in1=grow[r4, 2, :],
                                         op0=ALU.add, op1=ALU.subtract))
            own(dve.memset(grow[r4, 1, :], 0.0))
            own(dve.tensor_tensor_scan(grow[r4, 5, :], grow[r4, 4, :], grow[r4, 1, :], 0.0, ALU.max, ALU.add))
            dve.tensor_tensor(grow[r4, 3, :], grow[r4, 2, :], grow[r4, 5, :], ALU.add).then_inc(gr, 1)
            for a in range(2):
                own(dve.tensor_tensor_reduce(otmp[:, 0:64], prow("lam", 128 * a, 128 * a + 64), prow("lam", 128 * a + 64, 128 * a + 128),
                                             1.0, 0.0, ALU.mult, ALU.add, lamc[:, a:a + 1]))
            dve.tensor_scalar(lamc[:, 5:6], lamc[:, 0:1], 1.0, None, ALU.mult).then_inc(lam_s, 1)
            dve.wait_ge(lam_e, 1)
            own(dve.tensor_tensor(lamc[:, 6:7], lamc[:, 2:3], lamc[:, 3:4], ALU.subtract))
            own(dve.tensor_scalar(lamc[:, 4:5], lamc[:, 6:7], 0.2, None, ALU.add))
            dve.wait_ge(gr_act, 4)
            for h in range(MH):
                own(dve.tensor_tensor(abcm[:, h, :].rearrange("p (t s) -> p t s", t=T), abc[:, h, :].rearrange("p (t s) -> p t s", t=T),
                                      mask[:, 3 * P:].unsqueeze(1).to_broadcast([P, T, P]), ALU.add))
            fence(dve, "dve")
            mls.dve(dve, own)
            fence(dve, "dve")
            dif.dve(dve, own)
            fence(dve, "dve")
            residual("out2", modc2, 16)
            fence(dve, "dve")
            own(dve.scalar_tensor_tensor(out=scl[:, 0:8], in0=modc2[:, 32:40], scalar=1.0, in1=prow("n2g"),
                                         op0=ALU.add, op1=ALU.mult))
            norm_dve(dve, own, "n2", lambda c: xT[:, c, :], KD, lambda c: hT[:, c, :], lambda c: scl[:, c:c + 1])
            fence(dve, "dve")
            dve.memset(zeros, 0.0).then_inc(zero_ok, 1)

            def top16(src, val, idx):
                own(dve.max(val[:, 0:8], src))
                own(dve.max_index(idx[:, 0:8], val[:, 0:8], src))
                own(dve.match_replace(src, val[:, 0:8], src, -3e38))
                own(dve.max(val[:, 8:16], src))
                own(dve.max_index(idx[:, 8:16], val[:, 8:16], src))

            def pick_head(t, h):
                dve.wait_ge(pk_ev, h + 1 if t == 0 else PH + t)
                for c in (2 * h, 2 * h + 1):
                    top16(sc[:, c, :], tkv[:, c, :], tki[:, c, :])
                own(dve.tensor_tensor(cand[:, h, :].rearrange("p (a b) -> p a b", a=PK),
                                      tkv[:, 2 * h, :].unsqueeze(2).to_broadcast([P, PK, PK]),
                                      tkv[:, 2 * h + 1, :].unsqueeze(1).to_broadcast([P, PK, PK]), ALU.add))
                top16(cand[:, h, :], fval[:, PK * h:PK * h + PK], fpos[:, PK * h:PK * h + PK])

            def pick_half(t, half):
                if half == 0:
                    dve.tensor_copy(tkf, tki).then_inc(pk_top, 1)
                    dve.wait_ge(pk_top, t + 1)
                    own(dve.tensor_scalar(fpi, fpos, 4, None, ALU.logical_shift_right))
                else:
                    own(dve.tensor_scalar(fpi, fpos, 15, None, ALU.bitwise_and))
                own(dve.tensor_copy(fpf, fpi))
                own(dve.tensor_tensor(oneh, fpf.unsqueeze(2).to_broadcast([P, NSLOT, PK]),
                                      const("iota").unsqueeze(1).to_broadcast([P, NSLOT, PK]), ALU.is_equal))
                keys = tkf.rearrange("p (h a) k -> p h a k", a=2)[:, :, half, :]
                for h in range(PH):
                    own(dve.tensor_tensor(oneh[:, PK * h:PK * h + PK, :], oneh[:, PK * h:PK * h + PK, :],
                                          keys[:, h, :].unsqueeze(1).to_broadcast([P, PK, PK]), ALU.mult))
                own(dve.tensor_reduce(selv[:, half, :], oneh, AXX, ALU.add))

            def pick_experts(t):
                own(dve.scalar_tensor_tensor(out=fpf, in0=selv[:, 0, :], scalar=float(NKEY), in1=selv[:, 1, :],
                                             op0=ALU.mult, op1=ALU.add))
                own(dve.tensor_copy(eidx[:, t, :], fpf))
                f3 = fval.rearrange("p (h k) -> p h k", h=PH)
                g3 = gate[:, t, :].rearrange("p (h k) -> p h k", h=PH)
                dve.tensor_tensor(g3, f3, f3[:, :, 0:1].to_broadcast([P, PH, PK]), ALU.subtract).then_inc(pk_mx, 1)

            def pick_gates(t):
                g3 = gate[:, t, :].rearrange("p (h k) -> p h k", h=PH)
                dve.wait_ge(pk_ex, t + 1)
                own(dve.tensor_reduce(sm8[:, 0, :], g3, AXX, ALU.add))
                own(dve.reciprocal(sm8[:, 1, :], sm8[:, 0, :]))
                dve.tensor_tensor(g3, g3, sm8[:, 1, :].unsqueeze(2).to_broadcast([P, PH, PK]), ALU.mult).then_inc(top_done, 1)
                dve.wait_ge(top_done, t + 1)

            for h in range(PH):
                pick_head(0, h)
            pick_half(0, 0)
            pick_half(0, 1)
            pick_experts(0)
            pick_gates(0)
            NI = NSLOT // GRP
            side = {0: (0,), 2: (1,), 4: (2,), 5: (3,), 6: (4,), 7: (5,), 8: (6,), 9: (7,)}
            dve.sem_inc(u_used, GRP)
            dve.sem_inc(pe_used, GRP)
            dve.sem_inc(dot_cp, 1)
            for t in range(T):
                base = 2 * t * NI
                dve.wait_ge(tt_ev, 4 if t < 2 else 3 + t)
                with dve.Fori(0, NI) as i:
                    for j in range(GRP):
                        dve.wait_ge(u_land[j], i * 16 + 16 * (base + 1))
                        if j == 0:
                            dve.wait_ge(dot_cp, i + (NI * t + 1))
                        dve.tensor_tensor_reduce(ubuf[:, j, :], ubuf[:, j, :], h2tok[:, t % 2, :], 1.0, 0.0,
                                                 ALU.mult, ALU.add, dots8[:, j:j + 1]).then_inc(u_used, 1)
                    dve.wait_ge(u_used, i * GRP + GRP * (base + 2))
                    dve.tensor_copy(dots[:, bass.ds(i * GRP, GRP)], dots8).then_inc(dot_cp, 1)
                if t > 0:
                    dve.wait_ge(stored, 16 * t)
                own(dve.memset(acc, 0.0))
                dve.wait_ge(gl_done, t + 1)
                dve.tensor_tensor(wexp[:, t, :], dots, gate[:, t, :], ALU.mult).then_inc(wexp_ok, 1)
                dve.wait_ge(wexp_ok, t + 1)
                vb = base + NI
                for r in range(NI):
                    for q in range(GRP // 2):
                        dve.wait_ge(u_land[2 * q], 16 * (vb + r + 1))
                        dve.wait_ge(u_used, GRP * (vb + 1 + r) + 2 * (q - 1))
                        e = r * GRP + 2 * q
                        dve.scalar_tensor_tensor(out=acc[:, q % 2, :], in0=ubuf[:, 2 * q, :], scalar=wexp[:, t, e:e + 1],
                                                 in1=acc[:, q % 2, :], op0=ALU.mult, op1=ALU.add).then_inc(u_used, 2)
                    if t < T - 1:
                        for h in side.get(r, ()):
                            pick_head(t + 1, h)
                        if r in (10, 12):
                            pick_half(t + 1, (r - 10) // 2)
                        if r == 13:
                            pick_experts(t + 1)
                        if r == 15:
                            pick_gates(t + 1)
                dve.wait_ge(u_used, GRP * (vb + NI + 1))
                if t == 0:
                    dve.wait_ge(g2_ev, 17)
                a0, a1 = acc[:, 0, :], acc[:, 1, :]
                h0, g2 = a0.rearrange("p (a n) -> p a n", a=2), g2row[:, :, :]
                own(dve.tensor_tensor(a0, a0, a1, ALU.add))
                dve.wait_ge(v_sum, t + 1)
                own(dve.tensor_tensor(h0, h0, PS[:, 6:8, :], ALU.add))
                own(dve.tensor_tensor(h0, h0, g2, ALU.mult))
                dve.wait_ge(x_turned, t + 1)
                dve.tensor_tensor(h0, h0, PS[:, 0:2, :], ALU.add).then_inc(tile_read, 1)
                dve.wait_ge(tile_read, t + 1)
                own(dve.tensor_tensor_reduce(a1, a0, a0, 1.0, 0.0, ALU.mult, ALU.add, ssf[:, 1:2]))
                dve.tensor_scalar(ssf[:, 0:1], ssf[:, 1:2], 1.0 / D, EPS, ALU.mult, ALU.add).then_inc(fin_ms, 1)
                dve.wait_ge(fin_rt, t + 1)
                own(dve.reciprocal(ssf[:, 2:3], ssf[:, 0:1]))
                dve.scalar_tensor_tensor(out=a0, in0=a0, scalar=ssf[:, 2:3], in1=fgrow, op0=ALU.mult, op1=ALU.mult)\
                   .then_inc(fin_ok, 1)

        @block.gpsimd
        def _(pool):
            for n in range(24):
                if n == 12:
                    pool.wait_ge(stage_done, 3 * MLA_FENCE)
                if n >= 2:
                    pool.wait_ge(ada_summed, n - 1)
                pool.dma_start(adaw[n % 2], ap["ada"][n]).then_inc(ada_loaded[n % 2], 16)
            NI = NSLOT // GRP
            for ph in range(2 * T):
                t, table = ph // 2, ap["peer_u"] if ph % 2 == 0 else ap["peer_v"]
                if ph % 2 == 0:
                    pool.wait_ge(top_done, t + 1)
                    pool.wait_ge(pe_used, GRP * (t * NI + 1))
                with pool.Fori(0, NI) as i:
                    for half in range(2):
                        a, b = half * GRP // 2, (half + 1) * GRP // 2
                        if ph % 2 == 1:
                            pool.wait_ge(pe_used, i * GRP + (GRP * NI * t + b))
                            pool.sem_inc(pool_step, 1)
                        pool.wait_ge(u_used, i * GRP + (GRP * NI * ph + b))
                        pool.sem_inc(pool_step, 1)
                        pool.tensor_copy(idx8[:, a:b], eidx[:, t, bass.ds(i * GRP + a, b - a)]).then_inc(idx_cp, 1)
                        pool.wait_ge(idx_cp, i * 2 + (2 * NI * ph + half + 1))
                        pool.sem_inc(pool_step, 1)
                        for j in range(a, b):
                            pool.indirect_dma_start(ubuf[:, j, :], None, table,
                                                    bass.IndirectOffsetOnAxis(ap=idx8[:, j:j + 1], axis=0))\
                                .then_inc(u_land[j], 16)


def lay_out(inp):
    f32 = np.float32
    w = {k: np.asarray(v) for k, v in inp.items()}
    w = {k: (v[0] if k not in ("g_final", "final_g_2") else v) for k, v in w.items()}

    def kparts(m, k):
        return m.reshape(k, P, m.shape[1]).transpose(1, 0, 2)

    def block(m, k):
        b = np.zeros((P, BLK), f32)
        b[:, :k * m.shape[1]] = kparts(m, k).reshape(P, -1)
        return b

    def blocks(m, k, width):
        return [block(m[:, i:i + width], k) for i in range(0, m.shape[1], width)]

    def swap(m):
        return np.concatenate([m[:, 16:32], m[:, 0:16]], axis=1)

    wi = w["w_in"]
    q, kc, vc, ks, vs, kw, vw, zg, qd, kvd, kr, ga, gb = np.split(
        wi, np.cumsum([512, 128, 128, 128, 128, 128, 128, 24, 384, 256, 32, D]).tolist(), axis=1)
    qch = [q[:, h * DH:(h + 1) * DH] for c in range(HG) for h in (c, HG + c)]
    in1 = np.concatenate(qch + [ks, kw, kc, vc, qd, kvd, zg, np.zeros((D, 40), f32), kr, swap(kr), vs, vw], axis=1)
    uq = w["w_uq"]
    uqh = []
    for h in range(8):
        m = uq[:, h * 96:(h + 1) * 96]
        uqh += [m, swap(m[:, 64:96])]
    mq, mk, mv, mo, mi, mf, dq, dk, dv = np.split(
        w["w_in_2"], np.cumsum([512, 512, 512, 512, 4, 4, 512, 512]).tolist(), axis=1)
    gates = np.concatenate([mi, np.zeros((D, 28), f32), mf, np.zeros((D, 476), f32)], axis=1)
    keys = w["peer_sub_keys_2"].transpose(3, 0, 1, 2).reshape(P, 16 * NKEY)
    ada = blocks(w["w_ada"], KD, 512) + blocks(w["ada_w_2"], KD, 512)
    stream = (
        blocks(in1, KD, 512) + [block(np.concatenate(uqh, axis=1), 3)]
        + [block(np.concatenate([w["w_uk"], w["w_uv"]], axis=1), 2)]
        + [block(w["w_ck1"], 16), block(w["w_cv1"], 16)]
        + blocks(np.concatenate([ga, gb], axis=1), KD, 512)
        + [block(w["w_o_nsa"], 4), block(w["w_o_mla"], 4)] + blocks(w["w_out"], KD, 512)
        + blocks(w["w_fc1"], KD, 512) + blocks(w["w_fc2"], 32, P)
        + [block(m, KD) for m in (mq, mk, mo, dq, dk, gates, mv, dv)] + blocks(w["w_out_2"], KD, 512)
        + blocks(w["peer_w_query_2"], KD, 512))
    assert len(stream) == BLOCK0["pqb"]

    def cols(v):
        return v.reshape(-1, P).T

    def rows(v, at):
        a = np.zeros((P, 1), f32)
        a[at:at + len(v), 0] = v
        return a

    lam = np.concatenate([w["lambda_q1_2"], w["lambda_k1_2"], w["lambda_q2_2"], w["lambda_k2_2"]])
    params = dict(
        c=cols(w["c"]), b_ada=cols(w["b_ada"]), g_mix=cols(w["g_mix"]), g_mlp=cols(w["g_mlp"]), g_cq=cols(w["g_cq"]),
        g_ckv=cols(w["g_ckv"]), c2=cols(w["c_2"]), ada_b2=cols(w["ada_b_2"]), n1g=cols(w["norm1_g_2"]),
        n2g=cols(w["norm2_g_2"]), convw=w["conv_w_2"].reshape(4, 8, P).transpose(2, 1, 0).reshape(P, 32),
        convb=cols(w["conv_b_2"]), mng=cols(w["mlstm_norm_g_2"]), dng=cols(w["diff_norm_g_2"]),
        ck2=kparts(w["w_ck2"], 2).reshape(P, 128), cv2=kparts(w["w_cv2"], 2).reshape(P, 128),
        pek=w["pe_ck"].reshape(16, P).T, pev=w["pe_cv"].reshape(16, P).T,
        gb_i=rows(w["mlstm_gate_b_2"][:4], 0), gb_f=rows(w["mlstm_gate_b_2"][4:], 32),
        g_final=cols(w["g_final"]), lam=np.broadcast_to(lam, (P, 256)))
    return {
        "wstream": np.stack(stream), "ada": np.stack(ada), "params": np.concatenate([params[n] for n, _ in PARAMS], axis=1),
        "xT": w["x"].T.reshape(KD, P, S).transpose(1, 0, 2), "fgrow": np.broadcast_to(w["final_g_2"], (P, D)),
        "subkeys": keys.reshape(P, 16, NKEY), "peer_u": w["peer_u_2"], "peer_v": w["peer_v_2"],
    }


def shape_tables():
    f32 = np.float32
    p = np.arange(P)[:, None]
    back = p - (np.arange(S)[None, :] - (S - P))
    mask = np.where(back >= 0, 0.0, -BIG)
    slope = 2.0 ** -(np.arange(NH) + 1.0)
    alibi = np.where(back[:, None, :] >= 0, -8.0 * slope[None, :, None] * back[:, None, :], -BIG)
    t = np.arange(T)[None, :, None] * P + p[:, :, None]
    far = t - (np.arange(NC) * CMP_STRIDE + CMP_END0)[None, None, :]
    biasc = np.where(far[:, :, None, :] >= 0, -8.0 * slope[None, None, :, None] * far[:, :, None, :], -BIG)
    inv = (f32(10000.0) ** (-np.arange(16, dtype=f32) / f32(16))).astype(f32)
    ang = (np.arange(S, dtype=f32)[None, :] * inv[:, None]).astype(f32)
    rope = np.zeros((P, S))
    rope[64:80], rope[80:96] = np.cos(ang), np.cos(ang)
    rope[96:112], rope[112:128] = -np.sin(ang), np.sin(ang)
    sel = np.zeros((P, S))
    for h in range(4):
        sel[h, h * P:(h + 1) * P] = 1.0
    tab = dict(ident=np.eye(P), mask=mask, rope=rope, sel=sel, iota=np.broadcast_to(np.arange(PK), (P, PK)))
    return {"consts": np.concatenate([tab[n] for n, _ in CONSTS], axis=1).astype(f32), "alibi": alibi.astype(f32),
            "biasc": biasc.astype(f32)}


def kernel(**inputs):
    import concourse.bacc as bacc
    from concourse.bass_utils import run_bass_kernel_spmd

    nc = bacc.Bacc("TRN2", target_bir_lowering=False, num_devices=1)
    arrays = {k: np.ascontiguousarray(v) for k, v in {**lay_out(inputs), **shape_tables()}.items()}
    ap = {n: nc.dram_tensor("in_" + n, a.shape, mybir.dt.from_np(a.dtype), kind="ExternalInput").ap() for n, a in arrays.items()}
    out = nc.dram_tensor("result", (S, D), F32, kind="ExternalOutput").ap()
    build(nc, ap, out)
    r = run_bass_kernel_spmd(nc, [{"in_" + n: a for n, a in arrays.items()}], core_ids=[0])
    return r.results[0]["result"].reshape(1, S, D)
```

```python
from contextlib import ExitStack

import numpy as np

import concourse.bass as bass
from concourse import mybir

ALU = mybir.AluOpType
ACT = mybir.ActivationFunctionType
AXX = mybir.AxisListType.X
F32 = mybir.dt.float32
U32 = mybir.dt.uint32

P = 128
D = 1024
S = 512
T = S // P
KD = D // P
FF = 4 * D
EPS = 1e-6
BIG = 1e30
NH, NG, HG, DH = 8, 2, 4, 64
NC = S // 16 - 1
CMP_END0, CMP_STRIDE = 31, 16
MLA_SCALE = 96.0 ** -0.5
NSA_SCALE = 64.0 ** -0.5
MH = 4
PH, PK, NKEY = 8, 16, 128
NEXP = NKEY * NKEY
NSLOT = PH * PK
GRP = 8
V_DVE = ((0, 2), (2, 2), (4, 1), (5, 1), (7, 2))
V_PE = ((1, 2), (3, 2), (6, 4))
BLK = 4096
MIX_FENCE = 6

STREAM = [
    ("in1", [(4, 4)] * 3 + [(6, 6)]), ("ck", [(1, 0)]), ("cv", [(1, 0)]), ("gab", [(4, 4)] * 4),
    ("uq", [(8, 8)]), ("ukv", [(8, 8)]), ("on", [(8, 8)]), ("om", [(8, 8)]), ("out1", [(4, 4)] * 2),
    ("fc1", [(4, 4)] * 8), ("fc2", [(1, 1)] * 8),
    ("in2a", [(4, 4)] * 2 + [(1, 1)] + [(4, 4)] * 2), ("in2b", [(4, 4)] * 3), ("out2", [(12, 12), (4, 4)]),
    ("pqa", [(4, 4)] * 4), ("pqb", [(4, 4)] * 4),
]
BLOCK0, MM0, EV0, MM_THROUGH = {}, {}, {}, []
_b = _m = _e = 0
for _name, _blocks in STREAM:
    BLOCK0[_name], MM0[_name], EV0[_name] = _b, _m, _e
    for _mm, _ev in _blocks:
        _b, _m, _e = _b + 1, _m + _mm, _e + _ev
        MM_THROUGH.append(_m)
NBLK = _b

PARAMS = [("c", 8), ("b_ada", 48), ("g_mix", 8), ("g_mlp", 8), ("g_cq", 3), ("g_ckv", 2), ("c2", 8),
          ("ada_b2", 48), ("n1g", 8), ("n2g", 8), ("convw", 32), ("convb", 8), ("mng", 4), ("dng", 1),
          ("ck2", 128), ("cv2", 128), ("pek", 16), ("pev", 16), ("gb_i", 1), ("gb_f", 1), ("g_final", 8), ("lam", 256)]
PCOL, _o = {}, 0
for _n, _w in PARAMS:
    PCOL[_n] = _o
    _o += _w
NPRM = _o
CONSTS = [("ident", 128), ("mask", 512), ("rope", 512), ("sel", 512), ("iota", 16)]
CCOL, _o = {}, 0
for _n, _w in CONSTS:
    CCOL[_n] = _o
    _o += _w
NCST = _o

NORMS = [("x", 8), ("cq", 3), ("ckv", 2), ("mid", 8), ("fin", 8), ("n1", 8), ("n2", 8)]
SHIFTED = ["x", "mid", "n1", "n2"]
NORM0, _o = {}, 0
for _i, (_n, _w) in enumerate(NORMS):
    NORM0[_n] = (_o, _i)
    _o += _w


def build(nc, ap, out):
    with ExitStack() as ctx:
        def sb(name, shape, dt=F32):
            return ctx.enter_context(nc.sbuf_tensor(name, shape, dt))

        def sem(name):
            return ctx.enter_context(nc.semaphore(name))

        PS = ctx.enter_context(nc.psum_tensor("PS", [P, 8, 512], F32))
        ring = [sb(f"ring{i}", [P, BLK]) for i in range(2)]
        xT = sb("xT", [P, KD, S])
        hT = sb("hT", [P, KD, S])
        prm = sb("prm", [P, NPRM])
        cst = sb("cst", [P, NCST])
        ones = sb("ones", [P, P])
        sq = sb("sq", [P, 2, S])
        rstd = sb("rstd", [P, S])
        modc = sb("modc", [P, 48])
        modc2 = sb("modc2", [P, 48])
        scl = sb("scl", [P, 16])
        smalls = sb("smalls", [P, 512])
        ARENA = 32100
        arena = sb("arena", [P, ARENA])

        def area(kib, *dims, parts=P):
            n = int(np.prod(dims))
            o = int(kib * 256)
            assert o + n <= ARENA, (kib, dims)
            a = arena[0:parts, o:o + n]
            if len(dims) == 2:
                return a.rearrange("p (a b) -> p a b", a=dims[0])
            if len(dims) == 3:
                return a.rearrange("p (a b c) -> p a b c", a=dims[0], b=dims[1])
            return a

        def prow(name, a=0, b=None, rows=slice(0, P)):
            w = dict(PARAMS)[name]
            return prm[rows, PCOL[name] + a:PCOL[name] + (w if b is None else b)]

        def const(name, rows=slice(0, P)):
            return cst[rows, CCOL[name]:CCOL[name] + dict(CONSTS)[name]]

        ident = const("ident")
        mask = const("mask")

        zT = area(0, 14, S)
        vtok = area(28, T, 256)
        qm = area(72, 8, S)
        km = area(0, 8, S)
        vm = area(64, T, S)
        alibi = area(72, 8, S)
        biasc = area(88, T, 8, NC)
        onT = area(92, 4, S)
        omT = area(100, 4, S)
        sneg = area(108, 3, S)
        prob = area(114, 3, S)
        otok = area(120, S)
        otmp = area(122, S)
        probT1 = area(16, 3, S)
        probT2 = area(75, 3, S)
        cqT = area(64, 3, S)
        ckvT = zT[:, 11:13, :]
        rt = area(118, 2, S)
        stk = [area(108, 3, S), area(114, 3, S)]
        adaw = [area(32, BLK), area(48, BLK)]
        adas = area(64, 2, S)
        adaw2 = [area(68, BLK), area(84, BLK)]
        adas2 = area(100, 12, S)
        gT = area(32, 16, S)
        yT = area(0, 8, S)
        ytmp = area(16, 2, S)
        aT = area(0, 32, S)
        rbuf = area(64, 2, S)
        uT = area(0, 8, S + 3)
        qk2 = area(17, 8, S)
        mo = area(33, 4, S)
        dqk = area(41, 8, S)
        mv = area(57, T, S)
        dv = area(65, T, S)
        zG = area(73, S)
        grow = area(75, 8, S)
        abc = area(91, 4, S)
        abcm = area(99, 4, S)
        catT = area(0, 8, S)
        pqt = area(0, 16, S)
        skw = area(32, 16, NKEY)
        sc = area(40, 16, NKEY)
        cand = area(48, PK * PK)
        oneh = area(54, 2, PK, PK)
        h2tok = area(56, 2, D)
        ubuf = area(64, GRP, D)
        acc = area(96, 2, D)
        diag = area(49.5, 9, P)
        fgrow = area(108, D)
        eidx = area(112, T, NSLOT).bitcast(U32)
        gate = area(114, T, NSLOT)
        dots = area(116, NSLOT)
        wexp = area(117, T, NSLOT)
        tkv = area(119, 16, PK)
        tki = area(120, 16, PK).bitcast(U32)
        tkf = area(121, 2, PK)
        fpos = area(122, NSLOT).bitcast(U32)
        fpi = area(122.5, 2, PK).bitcast(U32)
        fpf = area(123, 2, PK)
        exf = area(123.25, PK)
        fval = area(123.5, NSLOT)
        selv = area(124, 2, PK)
        sm8 = area(125, 4, PH)
        g2row = sq
        zeros = rstd[:, 0:P]

        def small(a, n, rows=slice(0, P)):
            return smalls[rows, a:a + n]

        hid = small(0, 124)
        hb = small(124, 2)
        kcT = small(126, NC)
        vcm = small(157, 128)
        gtok = small(285, 96)
        rs = small(381, 48)
        nmx = small(456, 3)
        coef = small(431, 24)
        tok8 = small(0, 32)
        lamc = small(32, 8)
        ss4 = small(40, 16)
        dots8 = small(60, 8)
        idx16 = small(100, 16).bitcast(U32)
        ssf = small(84, 4)

        loaded = sem("loaded")
        ready = sem("constants_ready")
        w_loaded = [sem("w_loaded0"), sem("w_loaded1")]
        mm_done = sem("mm_done")
        evac = sem("evac")
        tables = sem("tables_loaded")
        ada_loaded = [sem("ada_loaded0"), sem("ada_loaded1")]
        ada_summed, ada_taken = sem("ada_summed"), sem("ada_taken")
        stage_done = sem("stage_done")
        act_own = sem("act_own")
        dve_own = sem("dve_own")
        nrm_sq, nrm_mm, nrm_ms, nrm_rt, nrm_h, nrm_sh = (
            sem(n) for n in ("nrm_sq", "nrm_mm", "nrm_ms", "nrm_rt", "nrm_h", "nrm_shifted"))
        stored = sem("stored")

        class Own:

            def __init__(self, eng, s):
                self.eng, self.s, self.n = eng, s, 0

            def __call__(self, ins):
                self.n += 1
                ins.then_inc(self.s, 1)
                self.eng.wait_ge(self.s, self.n)

            def mark(self, ins):
                self.n += 1
                ins.then_inc(self.s, 1)

            def wait(self):
                self.eng.wait_ge(self.s, self.n)

        fences = {}

        def fence(eng, name):
            k = fences[name] = fences.get(name, 0) + 1
            eng.drain().then_inc(stage_done, 1)
            eng.wait_ge(stage_done, 3 * k)

        def tile(i):
            return slice(i * P, (i + 1) * P)

        def bank(b, n=512, rows=slice(0, P)):
            return PS[rows, b, 0:n]

        def block_arrived(pe, n):
            pe.wait_ge(w_loaded[n % 2], 16 * (n // 2 + 1))

        def norm_act(act, name, src, n, dst=None, shift=None, ready=None):
            b, k = NORM0[name]
            for c in range(n):
                if ready is not None:
                    ready(c)
                if b + c >= 2:
                    act.wait_ge(nrm_mm, b + c - 1)
                act.activation(sq[:, c % 2, :], src(c), ACT.Square).then_inc(nrm_sq, 1)
            act.wait_ge(nrm_ms, k + 1)
            act.activation(rstd[:, :], rstd[:, :], ACT.Sqrt).then_inc(nrm_rt, 1)
            if shift is not None:
                for c in range(n):
                    act.wait_ge(nrm_h, b + c + 1)
                    act.activation(dst(c), dst(c), ACT.Identity, bias=shift(c)).then_inc(nrm_sh, 1)

        def norm_pe_chunk(pe, name, c, n):
            b, k = NORM0[name]
            if c == 0 and k:
                pe.wait_ge(nrm_ms, k)
            pe.wait_ge(nrm_sq, b + c + 1)
            pe.matmul(bank(7), ones[:, :], sq[:, c % 2, :], start=(c == 0), stop=(c == n - 1)).then_inc(nrm_mm, 1)

        def norm_pe(pe, name, n):
            for c in range(n):
                norm_pe_chunk(pe, name, c, n)

        def norm_after(pe, name, j):
            if j >= 2:
                norm_pe_chunk(pe, name, j - 2, KD)

        def normed(pe, name, c):
            pe.wait_ge(nrm_sh, KD * SHIFTED.index(name) + c + 1)

        def norm_dve(dve, own, name, src, n, dst, gain):
            b, k = NORM0[name]
            dve.wait_ge(nrm_mm, b + n)
            if b:
                dve.wait_ge(nrm_h, b)
            dve.tensor_scalar(rstd[:, :], bank(7), 1.0 / (n * P), EPS, ALU.mult, ALU.add).then_inc(nrm_ms, 1)
            dve.wait_ge(nrm_rt, k + 1)
            own(dve.reciprocal(rstd[:, :], rstd[:, :]))
            for c in range(n):
                dve.scalar_tensor_tensor(out=dst(c), in0=src(c), scalar=gain(c), in1=rstd[:, :],
                                         op0=ALU.mult, op1=ALU.mult).then_inc(nrm_h, 1)

        def ada_bank(n):
            return 6 if n < 16 else 5

        def ada_total(n):
            return adas[:, n % 2, :] if n < 12 else adas2[:, n - 12, :]

        def ada_sum(dve, own, n, vec):
            dve.wait_ge(ada_loaded[n % 2], 16 * (n // 2 + 1))
            if 2 <= n < 12:
                dve.wait_ge(ada_taken, n - 1)
            w = (adaw if n < 12 else adaw2)[n % 2].rearrange("p (k m) -> p k m", k=KD)
            total = ada_total(n)
            own(dve.tensor_scalar(total, w[:, 0, :], vec(0), None, ALU.mult))
            for k in range(1, KD):
                ins = dve.scalar_tensor_tensor(out=total, in0=w[:, k, :], scalar=vec(k), in1=total,
                                               op0=ALU.mult, op1=ALU.add)
                if k < KD - 1:
                    own(ins)
            ins.then_inc(ada_summed, 1)

        def ada_take(pe, n):
            pe.wait_ge(ada_summed, n + 1)
            for m in range(4):
                ins = pe.matmul(PS[:, ada_bank(n), 4 * n + m:4 * n + m + 1], ada_total(n)[:, tile(m)], ones[:, 0:1],
                                start=True, stop=True)
            ins.then_inc(ada_taken, 1)

        def ada_bias(dve, own, dst, n0, n1, bias):
            dve.wait_ge(ada_taken, n1)
            c = slice(4 * n0 % 48, 4 * n0 % 48 + 4 * (n1 - n0))
            own(dve.tensor_tensor(dst[:, c], PS[:, ada_bank(n0), 4 * n0:4 * n1], bias[:, c], ALU.add))

        def chunk_pe(pe, name, j, lhs, rhs, dst=None, n=512, pre=None):
            if EV0[name] + j >= 2:
                pe.wait_ge(evac, EV0[name] + j - 1)
            o = bank(j % 2, n) if dst is None else dst
            for a, (l, r) in enumerate(zip(lhs, rhs)):
                if pre is not None:
                    pre(a)
                ins = pe.matmul(o, l, r, start=(a == 0), stop=(a == len(lhs) - 1))
            ins.then_inc(mm_done, 1)

        def layer_pe(pe, name, nblk, kc, act_in, pre=None, after=None):
            per = BLK // kc // P
            for n in range(nblk):
                g = BLOCK0[name] + n
                block_arrived(pe, g)
                w = ring[g % 2][:, :].rearrange("p (k m) -> p k m", k=kc)
                for m in range(per):
                    chunk_pe(pe, name, n * per + m, [w[:, k, m * P:(m + 1) * P] for k in range(kc)],
                             [act_in(k) for k in range(kc)], pre=pre if n == m == 0 else None)
                    if after is not None:
                        after(n * per + m)

        def layer_pe_loop(pe, name, nblk, kc, act_in, n=512, pre=None):
            per = BLK // kc // P
            with pe.Fori(0, nblk // 2) as i:
                for s in range(2):
                    pe.wait_ge(w_loaded[s], i * 16 + 16 * (BLOCK0[name] // 2 + 1))
                    w = ring[s][:, :].rearrange("p (k m) -> p k m", k=kc)
                    for m in range(per):
                        j = s * per + m
                        pe.wait_ge(evac, i * (2 * per) + EV0[name] + j - 1)
                        for k in range(kc):
                            if pre is not None and j == 0:
                                pre(k)
                            ins = pe.matmul(bank(j % 2, n), w[:, k, m * P:(m + 1) * P], act_in(k),
                                            start=(k == 0), stop=(k == kc - 1))
                        ins.then_inc(mm_done, 1)

        class Attention:

            def __init__(self, name, units, kind, probT):
                self.units, self.kind, self.name, self.probT = units, kind, name, probT
                self.last = [u for u in range(len(units)) if u + 1 == len(units) or units[u + 1]["tile"] != units[u]["tile"]]
                self.scored = sem(f"{name}_scored")
                self.weighed = sem(f"{name}_weighed")
                self.exped = sem(f"{name}_exped")
                self.turned = sem(f"{name}_turned")
                self.copied = sem(f"{name}_copied")
                self.summed = sem(f"{name}_summed")
                self.banks_free = sem(f"{name}_banks_free")
                self.tok_ready = sem(f"{name}_tok_ready")
                self.tok_turned = sem(f"{name}_tok_turned")
                self.tok_out = sem(f"{name}_tok_out")
                self.ms_ready = sem(f"{name}_ms_ready")
                self.root_ready = sem(f"{name}_root_ready")

            def pe(self, pe):
                U = self.units
                for u in range(len(U) + 10):
                    if u < len(U):
                        if u >= 2:
                            pe.wait_ge(self.weighed, u - 1)
                        for (l, r, o) in U[u]["scores"](u % 2):
                            ins = pe.matmul(o, l, r, start=True, stop=True)
                        ins.then_inc(self.scored, 1)
                    v = u - 2
                    if 0 <= v < len(U):
                        pe.wait_ge(self.weighed if self.kind == "mlstm" else self.exped, v + 1)
                        if v >= 2:
                            pe.wait_ge(self.copied, v - 1)
                        if v - 7 in self.last:
                            pe.wait_ge(self.tok_out, U[v - 7]["tile"] + 1)
                        for (o, i, n) in U[v]["turns"](v % 2, v % 3):
                            ins = pe.transpose(o, i, ident[0:n, 0:n])
                        ins.then_inc(self.turned, 1)
                    if self.fill_pe is not None:
                        self.fill_pe(pe, u)
                    v = u - 4
                    if 0 <= v < len(U):
                        pe.wait_ge(self.copied, v + 1)
                        t = U[v]["tile"]
                        if t > 0 and (v - 1) in self.last:
                            pe.wait_ge(self.banks_free, t)
                        for (o, pairs) in U[v]["values"](v % 3):
                            for a, (l, r) in enumerate(pairs):
                                ins = pe.matmul(o, l, r, start=(a == 0), stop=(a == len(pairs) - 1))
                        ins.then_inc(self.summed, 1)
                    v = u - 8
                    if v in self.last:
                        t = U[v]["tile"]
                        pe.wait_ge(self.tok_ready, t + 1)
                        pe.wait_ge(self.copied, min(u - 2, len(U)))
                        for c in range(4):
                            ins = pe.transpose(PS[:, 2 + (u - 1) % 2, tile(c)], otok[:, tile(c)], ident)
                        ins.then_inc(self.tok_turned, 1)

            def act(self, act):
                U = self.units
                for u in range(len(U) + 10):
                    if u - 9 in self.last and self.out_act is not None:
                        t = U[u - 9]["tile"]
                        act.wait_ge(self.tok_turned, t + 1)
                        act.activation(self.out_act[:, :, tile(t)], bank(2 + u % 2).rearrange("p (c t) -> p c t", c=4),
                                       ACT.Copy).then_inc(self.tok_out, 1)
                    if u < len(U):
                        if self.kind == "mlstm":
                            if u >= 3:
                                act.wait_ge(self.weighed, u - 2)
                        else:
                            act.wait_ge(self.weighed, u + 1)
                            if u >= 3:
                                act.wait_ge(self.turned, u - 2)
                        U[u]["exp"](act, u % 3).then_inc(self.exped, 1)
                    v = u - 2
                    if 0 <= v < len(U):
                        act.wait_ge(self.turned, v + 1)
                        if v >= 3:
                            act.wait_ge(self.summed, v - 2)
                        n, r = U[v]["tcols"], U[v]["trows"]
                        act.activation(self.probT[0:r, v % 3, 0:n], PS[0:r, 2 + v % 2, 0:n], ACT.Copy).then_inc(self.copied, 1)
                    if u - 6 in self.last and self.root is not None:
                        t = U[u - 6]["tile"]
                        act.wait_ge(self.ms_ready, t + 1)
                        act.activation(self.root, self.root, ACT.Sqrt).then_inc(self.root_ready, 1)

            def dve(self, dve, own):
                U = self.units
                for u in range(len(U) + 10):
                    if u - 9 in self.last and self.out_dve is not None:
                        t = U[u - 9]["tile"]
                        dve.wait_ge(self.tok_turned, t + 1)
                        self.out_dve(dve, own, t, 2 + u % 2).then_inc(self.tok_out, 1)
                    if self.fill_dve is not None:
                        self.fill_dve(dve, u)
                    if u - 5 in self.last:
                        t = U[u - 5]["tile"]
                        dve.wait_ge(self.summed, u - 4)
                        if t > 0:
                            dve.wait_ge(self.tok_turned, t)
                        self.finish_a(dve, own, t)
                    if u < len(U):
                        dve.wait_ge(self.scored, u + 1)
                        if self.kind == "mlstm":
                            dve.wait_ge(self.exped, u + 1)
                            if u >= 3:
                                dve.wait_ge(self.turned, u - 2)
                        elif u >= 3:
                            dve.wait_ge(self.exped, u - 2)
                        U[u]["weigh"](dve, own, u % 2, u % 3).then_inc(self.weighed, 1)
                    if 0 <= u - 1 < len(U) and U[u - 1].get("rowsum"):
                        dve.wait_ge(self.exped, u)
                        U[u - 1]["rowsum"](dve, own, (u - 1) % 3)
                    if u - 7 in self.last and self.finish_b is not None:
                        t = U[u - 7]["tile"]
                        dve.wait_ge(self.root_ready, t + 1)
                        self.finish_b(dve, own, t)

            root = out_act = finish_b = out_dve = fill_pe = fill_dve = None

        def softmax_unit(t, q, k, bias, scale, v, o, rsum, probT):
            n = (t + 1) * P
            return dict(
                tile=t, tcols=n, trows=P,
                scores=lambda b: [(q, k, PS[:, b, 0:n])],
                weigh=lambda dve, own, b, m: dve.tensor_tensor_reduce(
                    sneg[:, m, 0:n], PS[:, b, 0:n], bias, -scale, BIG, ALU.add, ALU.min, nmx[:, m:m + 1]),
                exp=lambda act, b: act.activation(prob[:, b, 0:n], sneg[:, b, 0:n], ACT.Exp, scale=-1.0,
                                                  bias=nmx[:, b:b + 1], accum_out=rsum),
                turns=lambda b, m: [(PS[:, 2 + b, tile(kb)], prob[:, m, tile(kb)], P) for kb in range(t + 1)],
                values=lambda b: [(o, [(probT[:, b, tile(kb)], v(kb)) for kb in range(t + 1)])])

        def nsa_units():
            U = []
            for t in range(T):
                def q(h):
                    g = h // HG
                    return zT[g * DH:(g + 1) * DH, h % HG, tile(t)]
                for g in range(NG):
                    kc = kcT[g * DH:(g + 1) * DH, :]

                    def weigh(dve, own, b, m, g=g, t=t):
                        s3 = sneg[:, m, 0:P].rearrange("p (h j) -> p h j", h=HG)[:, :, 0:NC]
                        p3 = PS[:, b, 0:P].rearrange("p (h j) -> p h j", h=HG)[:, :, 0:NC]
                        own(dve.tensor_tensor(s3, p3, biasc[:, t, g * HG:(g + 1) * HG, :], ALU.add))
                        own(dve.tensor_reduce(ssf, s3, AXX, ALU.max))
                        own(dve.tensor_scalar(ssf, ssf, -1e20, None, ALU.max))
                        return dve.tensor_tensor(s3, s3, ssf.unsqueeze(2).to_broadcast([P, HG, NC]), ALU.subtract)

                    U.append(dict(
                        tile=t, tcols=512, trows=NC,
                        scores=lambda b, g=g, kc=kc, t=t: [
                            (zT[g * DH:(g + 1) * DH, a, tile(t)], kc, PS[:, b, 32 * a:32 * a + NC]) for a in range(HG)],
                        weigh=weigh,
                        exp=lambda act, b: act.activation(
                            prob[:, b, 0:P].rearrange("p (h j) -> p h j", h=HG)[:, :, 0:NC],
                            sneg[:, b, 0:P].rearrange("p (h j) -> p h j", h=HG)[:, :, 0:NC], ACT.Exp, scale=NSA_SCALE),
                        rowsum=lambda dve, own, b, g=g, t=t: own(dve.tensor_reduce(
                            rs[:, 24 * (t % 2) + g * HG:24 * (t % 2) + (g + 1) * HG],
                            prob[:, b, 0:P].rearrange("p (h j) -> p h j", h=HG)[:, :, 0:NC], AXX, ALU.add)),
                        turns=lambda b, m: [(PS[0:NC, 2 + b, tile(a)], prob[:, m, 32 * a:32 * a + NC], P) for a in range(HG)],
                        values=lambda b, g=g: [(PS[:, 4, (g * HG + a) * DH:(g * HG + a + 1) * DH],
                                                [(probT1[0:NC, b, tile(a)], vcm[0:NC, g * DH:(g + 1) * DH])])
                                               for a in range(HG)]))
                for br in range(2):
                    for h in range(NH):
                        g = h // HG
                        r = 24 * (t % 2) + 8 * (br + 1) + h
                        U.append(softmax_unit(
                            t, q(h), zT[g * DH:(g + 1) * DH, 4 + br, 0:(t + 1) * P],
                            alibi[:, h, (T - 1 - t) * P:S], NSA_SCALE,
                            lambda kb, br=br, g=g: vtok[:, kb, br * P + g * DH:br * P + (g + 1) * DH],
                            PS[:, 5 + br, h * DH:(h + 1) * DH], rs[:, r:r + 1], probT1))
            return U

        def mla_units():
            U = []
            for t in range(T):
                for h in range(NH):
                    r = 24 * (t % 2) + h
                    U.append(softmax_unit(
                        t, qm[0:96, h, tile(t)], km[0:96, h, 0:(t + 1) * P], mask[:, (T - 1 - t) * P:S], MLA_SCALE,
                        lambda kb, h=h: vm[:, kb, h * DH:(h + 1) * DH],
                        PS[:, 4, h * DH:(h + 1) * DH], rs[:, r:r + 1], probT1))
            return U

        def diff_units():
            U = []
            for t in range(T):
                for p in range(2):
                    for h in range(MH):
                        r = 24 * (t % 2) + MH * p + h
                        U.append(softmax_unit(
                            t, dqk[p * DH:(p + 1) * DH, h, tile(t)], dqk[p * DH:(p + 1) * DH, 4 + h, 0:(t + 1) * P],
                            mask[:, (T - 1 - t) * P:S], NSA_SCALE,
                            lambda kb, h=h: dv[:, kb, tile(h)],
                            PS[:, 4 + p, tile(h)], rs[:, r:r + 1], probT2))
            return U

        def mlstm_units():
            U = []
            for t in range(T):
                for h in range(MH):
                    n = (t + 1) * P
                    r = 24 * (t % 2) + h

                    def decay(act, b, h=h, t=t):
                        nm = tok8[:, 8 * t + h:8 * t + h + 1]
                        if t > 0:
                            act.activation(sneg[:, b, 0:t * P], abc[:, h, 0:t * P], ACT.Exp, bias=nm)
                        return act.activation(sneg[:, b, tile(t)], abcm[:, h, tile(t)], ACT.Exp, bias=nm)

                    U.append(dict(
                        tile=t, tcols=n, trows=P,
                        scores=lambda b, h=h, t=t, n=n: [(qk2[:, h, tile(t)], qk2[:, 4 + h, 0:n], PS[:, b, 0:n])],
                        exp=decay,
                        weigh=lambda dve, own, b, m, n=n, r=r: dve.tensor_tensor_reduce(
                            prob[:, m, 0:n], PS[:, b, 0:n], sneg[:, m, 0:n], float(P) ** -0.5, 0.0,
                            ALU.mult, ALU.add, rs[:, r:r + 1]),
                        turns=lambda b, m, t=t: [(PS[:, 2 + b, tile(kb)], prob[:, m, tile(kb)], P) for kb in range(t + 1)],
                        values=lambda b, h=h, t=t: [(PS[:, 4, tile(h)],
                                                     [(probT2[:, b, tile(kb)], mv[:, kb, tile(h)]) for kb in range(t + 1)])]))
            return U

        def per_head(a, n, w):
            return a.unsqueeze(2).to_broadcast([P, n, w])

        def heads(a, n):
            return a.rearrange("p (h d) -> p h d", h=n)

        nsa = Attention("nsa", nsa_units(), "softmax", probT1)
        mla = Attention("mla", mla_units(), "softmax", probT1)
        mls = Attention("mls", mlstm_units(), "mlstm", probT2)
        dif = Attention("dif", diff_units(), "softmax", probT2)

        def nsa_finish(dve, own, t):
            r = rs[:, 24 * (t % 2):24 * (t % 2) + 24]
            own(dve.tensor_scalar(coef, r, 1e-30, None, ALU.max))
            own(dve.reciprocal(coef, coef))
            own(dve.tensor_tensor(coef, coef, gtok[:, 24 * t:24 * t + 24], ALU.mult))
            own(dve.tensor_tensor(heads(otok, NH), heads(bank(4), NH), per_head(coef[:, 0:8], NH, DH), ALU.mult))
            own(dve.tensor_tensor(heads(otmp, NH), heads(bank(5), NH), per_head(coef[:, 8:16], NH, DH), ALU.mult))
            own(dve.tensor_tensor(otok, otok, otmp, ALU.add))
            ins = dve.tensor_tensor(heads(otmp, NH), heads(bank(6), NH), per_head(coef[:, 16:24], NH, DH), ALU.mult)
            ins.then_inc(nsa.banks_free, 1)
            dve.wait_ge(nsa.banks_free, t + 1)
            dve.tensor_tensor(otok, otok, otmp, ALU.add).then_inc(nsa.tok_ready, 1)

        def mla_finish(dve, own, t):
            r = rs[:, 24 * (t % 2):24 * (t % 2) + 8]
            own(dve.tensor_scalar(coef[:, 0:8], r, 1e-30, None, ALU.max))
            own(dve.reciprocal(coef[:, 0:8], coef[:, 0:8]))
            ins = dve.tensor_tensor(heads(otok, NH), heads(bank(4), NH), per_head(coef[:, 0:8], NH, DH), ALU.mult)
            ins.then_inc(mla.banks_free, 1)

        def head_ms(dve, own, att):
            own(dve.tensor_tensor(otmp, otok, otok, ALU.mult))
            own(dve.tensor_reduce(ss4[:, 0:4], heads(otmp, MH), AXX, ALU.add))
            dve.tensor_scalar(ss4[:, 0:4], ss4[:, 0:4], 1.0 / P, EPS, ALU.mult, ALU.add).then_inc(att.ms_ready, 1)

        def mls_finish(dve, own, t):
            den = rs[:, 24 * (t % 2):24 * (t % 2) + 4]
            own(dve.tensor_scalar(coef[:, 0:4], den, -1.0, None, ALU.mult))
            own(dve.tensor_tensor(coef[:, 0:4], coef[:, 0:4], den, ALU.max))
            own(dve.tensor_tensor(coef[:, 0:4], coef[:, 0:4], tok8[:, 8 * t + 4:8 * t + 8], ALU.max))
            own(dve.reciprocal(coef[:, 0:4], coef[:, 0:4]))
            ins = dve.tensor_tensor(heads(otok, MH), heads(bank(4), MH), per_head(coef[:, 0:4], MH, P), ALU.mult)
            ins.then_inc(mls.banks_free, 1)
            dve.wait_ge(mls.banks_free, t + 1)
            head_ms(dve, own, mls)

        def dif_finish(dve, own, t):
            r = rs[:, 24 * (t % 2):24 * (t % 2) + 8]
            own(dve.reciprocal(coef[:, 0:8], r))
            own(dve.tensor_scalar(coef[:, 4:8], coef[:, 4:8], lamc[:, 4:5], None, ALU.mult))
            own(dve.tensor_tensor(heads(otok, MH), heads(bank(4), MH), per_head(coef[:, 0:4], MH, P), ALU.mult))
            ins = dve.tensor_tensor(heads(otmp, MH), heads(bank(5), MH), per_head(coef[:, 4:8], MH, P), ALU.mult)
            ins.then_inc(dif.banks_free, 1)
            dve.wait_ge(dif.banks_free, t + 1)
            own(dve.tensor_tensor(otok, otok, otmp, ALU.subtract))
            head_ms(dve, own, dif)

        def head_norm(att):
            def finish(dve, own, t):
                own(dve.reciprocal(ss4[:, 0:4], ss4[:, 0:4]))
                dve.tensor_tensor(heads(otok, MH), heads(otok, MH), per_head(ss4[:, 0:4], MH, P), ALU.mult)\
                   .then_inc(att.tok_ready, 1)
            return finish

        def mls_out(dve, own, t, b):
            for h in range(MH):
                ins = dve.scalar_tensor_tensor(out=catT[:, h, tile(t)], in0=PS[:, b, tile(h)], scalar=prow("mng", h, h + 1),
                                               in1=mo[:, h, tile(t)], op0=ALU.mult, op1=ALU.mult)
            return ins

        def dif_out(dve, own, t, b):
            return dve.tensor_scalar(catT[:, MH:2 * MH, tile(t)], bank(b).rearrange("p (c t) -> p c t", c=4),
                                     prow("dng"), 1.0 - 0.2, ALU.mult, ALU.mult)

        nsa.finish_a, nsa.out_act = nsa_finish, onT
        mla.finish_a, mla.out_act = mla_finish, omT
        mla.tok_ready = mla.banks_free
        mls.finish_a, mls.finish_b, mls.root, mls.out_dve = mls_finish, head_norm(mls), ss4[:, 0:4], mls_out
        dif.finish_a, dif.finish_b, dif.root, dif.out_dve = dif_finish, head_norm(dif), ss4[:, 0:4], dif_out

        def gab_pe(pe, u):
            j, part = u // 5, u % 5
            if j >= 16 or part == 4:
                return
            g = BLOCK0["gab"] + j // 4
            if part == 0:
                if j % 4 == 0:
                    block_arrived(pe, g)
                if j > 0:
                    pe.wait_ge(evac, EV0["gab"] + j)
            w = ring[g % 2][:, :].rearrange("p (k m) -> p k m", k=KD)
            for k in (2 * part, 2 * part + 1):
                ins = pe.matmul(bank(7), w[:, k, tile(j % 4)], hT[:, k, :], start=(k == 0), stop=(k == KD - 1))
            if part == 3:
                ins.then_inc(mm_done, 1)

        def gab_dve(dve, u):
            j = u // 5
            if j < 16 and u % 5 == 4:
                dve.wait_ge(mm_done, MM0["gab"] + j + 1)
                dve.tensor_copy(gT[:, j, :], bank(7)).then_inc(evac, 1)

        def in2b_pe(pe, u):
            j, part = u // 2, u % 2
            if j >= 12:
                return
            g = BLOCK0["in2b"] + j // 4
            if part == 0:
                if j % 4 == 0:
                    block_arrived(pe, g)
                if j >= 2:
                    pe.wait_ge(evac, EV0["in2b"] + j - 1)
            w = ring[g % 2][:, :].rearrange("p (k m) -> p k m", k=KD)
            for k in range(4 * part, 4 * part + 4):
                lhs, rhs = (w[:, k, tile(j % 4)], hT[:, k, :]) if j < 8 else (hT[:, k, tile(j - 8)], w[:, k, :])
                ins = pe.matmul(bank(5 + j % 2), lhs, rhs, start=(k == 0), stop=(k == KD - 1))
            if part == 1:
                ins.then_inc(mm_done, 1)

        def in2b_dve(dve, u):
            j = u // 2 - 1
            if 0 <= j < 12 and u % 2 == 0:
                dve.wait_ge(mm_done, MM0["in2b"] + j + 1)
                dve.tensor_copy(dqk[:, j, :] if j < 8 else dv[:, j - 8, :], bank(5 + j % 2)).then_inc(evac, 1)

        def half_layer(name, banks, per, kc, act_in, take):
            def on_pe(pe, u):
                j, k = u // 4, u % 4
                if j >= 8:
                    return
                g = BLOCK0[name] + j // per
                if k == 0:
                    if j % per == 0:
                        block_arrived(pe, g)
                    if j >= 2:
                        pe.wait_ge(evac, EV0[name] + j - 1)
                w = ring[g % 2][:, :].rearrange("p (k m) -> p k m", k=kc)
                ins = pe.matmul(bank(banks + j % 2), w[:, k, tile(j % per)], act_in[:, k, :], start=(k == 0), stop=(k == 3))
                if k == 3:
                    ins.then_inc(mm_done, 1)

            def on_dve(dve, u):
                j = u // 4 - 1
                if 0 <= j < 8 and u % 4 == 0:
                    dve.wait_ge(mm_done, MM0[name] + j + 1)
                    take(dve, j, bank(banks + j % 2)).then_inc(evac, 1)

            return on_pe, on_dve

        def take_on(dve, j, products):
            if j == 0:
                dve.wait_ge(gt_sig, 16)
            return dve.tensor_tensor(gT[:, j, :], gT[:, j, :], products, ALU.mult)

        def take_out2(dve, j, products):
            return dve.scalar_tensor_tensor(out=xT[:, j, :], in0=products, scalar=modc2[:, 16 + j:17 + j],
                                            in1=xT[:, j, :], op0=ALU.mult, op1=ALU.add)

        mla.fill_pe, mla.fill_dve = half_layer("on", 5, 8, 4, onT, take_on)
        dif.fill_pe, dif.fill_dve = half_layer("out2", 6, 4, KD, catT, take_out2)
        nsa.fill_pe, nsa.fill_dve = gab_pe, gab_dve
        mls.fill_pe, mls.fill_dve = in2b_pe, in2b_dve

        gt_sig = sem("mix_gates_sigmoid")
        g_sig, g_turn = sem("gates_sigmoid"), sem("gates_turned")
        c_stk, c_mm, c_pe, c_hid, c_out = (sem(n) for n in ("cmp_stacked", "cmp_hidden", "cmp_bias", "cmp_silu", "cmp_out"))
        y_tmp = sem("y_tmp")
        fc_sq = sem("fc_squared")
        cv_sum = sem("conv_summed")
        gr, gr_x = sem("gate_rows"), sem("gate_rows_abs")
        dot_cp = sem("dots_copied")
        sk_loaded, sk_done = sem("subkeys_loaded"), sem("subkey_scores")
        wexp_ok, diag_ok, pe_used = sem("expert_weights"), sem("diagonals"), sem("slots_used_pe")
        v_sum, x_turned, tile_read = sem("v_summed"), sem("x_turned"), sem("tile_read")
        zero_ok = sem("zeros_ready")
        gr_act = sem("gate_rows_act")
        gr_pe = sem("gate_rows_pe")
        lam_s, lam_e = sem("lam_sums"), sem("lam_exps")
        silu_c = sem("silu_c")
        tt_pe, tt_ev = sem("token_turned"), sem("token_copied")
        pk_ev, pk_top = sem("peer_scores_copied"), sem("peer_scores_used")
        pk_mx, pk_ex = sem("peer_gate_max"), sem("peer_gate_exp")
        u_land = [sem(f"landed{j}") for j in range(GRP)]
        u_used = sem("slots_used")
        idx_cp, pool_step = sem("idx_copied"), sem("pool_step")
        top_done, experts_ok = sem("top_done"), sem("experts_ok")
        gl_done, fin_ms, fin_rt, fin_ok = (sem(n) for n in (
            "gelu_done", "final_ms", "final_root", "final_ready"))
        g2_pe, g2_ev = sem("g2_pe"), sem("g2_ev")

        block = ctx.enter_context(nc.Block())

        @block.sync
        def _(sp):
            sp.wait_ge(ada_loaded[1], 32)
            for n in range(NBLK):
                if n >= 2:
                    sp.wait_ge(mm_done, MM_THROUGH[n - 2])
                src = n if n < BLOCK0["pqb"] else n - 4
                sp.dma_start(ring[n % 2][:, :], ap["wstream"][src]).then_inc(w_loaded[n % 2], 16)
            for t in range(T):
                sp.wait_ge(fin_ok, t + 1)
                sp.dma_start(out[t * P:(t + 1) * P, :], acc[:, 0, :]).then_inc(stored, 16)
            sp.wait_ge(stored, 16 * T)

        @block.tensor
        def _(pe):
            pe.wait_ge(loaded, 48)
            pe.wait_ge(ready, 1)
            norm_pe(pe, "x", KD)
            for n in range(4):
                ada_take(pe, n)
            name = "in1"
            for n in range(4):
                g = BLOCK0[name] + n
                block_arrived(pe, g)
                w = ring[g % 2][:, :].rearrange("p (k m) -> p k m", k=KD)
                for m in range(4 if n < 3 else 2):
                    chunk_pe(pe, name, 4 * n + m, [w[:, k, tile(m)] for k in range(KD)], [hT[:, k, :] for k in range(KD)],
                             pre=(lambda k: normed(pe, "x", k)) if n == m == 0 else None)
                    if 4 * n + m >= 6:
                        ada_take(pe, 4 + 4 * n + m - 6)
            for t in range(T):
                chunk_pe(pe, name, 14 + t, [hT[:, k, tile(t)] for k in range(KD)],
                         [w[:, k, 256:512] for k in range(KD)], n=256)
                if t == 0:
                    norm_pe(pe, "cq", 3)
                if t == 1:
                    norm_pe(pe, "ckv", 2)
                if t == 2:
                    pe.wait_ge(g_sig, 1)
                    for q in range(T):
                        ins = pe.transpose(PS[:, 6, 24 * q:24 * q + 24], sq[0:24, 0, tile(q)], ident[0:24, 0:24])
                    ins.then_inc(g_turn, 1)
            fence(pe, "pe")
            for r in range(2):
                n = BLOCK0["ck"] + r
                block_arrived(pe, n)
                w = ring[n % 2][:, :].rearrange("p (l m) -> p l m", l=16)
                if r == 0:
                    pe.wait_ge(c_stk, 10)
                for hc in range(2):
                    for l in range(16):
                        rhs = stk[r][:, :, 2 * l:2 * l + 16 * (NC - 1) + 1:16]
                        ins = pe.matmul(PS[:, 2 * r + hc, 0:3 * NC].rearrange("p (g j) -> p g j", g=3), w[:, l, tile(hc)],
                                        rhs, start=(l == 0), stop=(l == 15))
                ins.then_inc(mm_done, 1)
                pe.wait_ge(c_hid, 2 * r + 2)
                if r == 0:
                    for g in range(NG):
                        for hc in range(2):
                            ins = pe.matmul(PS[g * DH:(g + 1) * DH, 0, 128:128 + NC], prow("ck2", hc * DH, (hc + 1) * DH),
                                            hid[:, hc * 62 + g * NC:hc * 62 + (g + 1) * NC], start=(hc == 0), stop=(hc == 1))
                    ins.then_inc(c_mm, 1)
                else:
                    for g in range(NG):
                        for hc in range(2):
                            ins = pe.matmul(PS[0:NC, 1, 128 + g * DH:128 + (g + 1) * DH],
                                            hid[:, hc * 62 + g * NC:hc * 62 + (g + 1) * NC],
                                            prow("cv2", hc * DH, (hc + 1) * DH), start=(hc == 0), stop=(hc == 1))
                    ins.then_inc(c_mm, 1)
            fence(pe, "pe")
            nsa.pe(pe)
            fence(pe, "pe")
            block_arrived(pe, BLOCK0["uq"])
            w = ring[BLOCK0["uq"] % 2][:, 0:3 * D].rearrange("p (k m) -> p k m", k=3)
            for h in range(NH):
                chunk_pe(pe, "uq", h, [w[:, k, tile(h)] for k in range(3)], [cqT[:, k, :] for k in range(3)])
            block_arrived(pe, BLOCK0["ukv"])
            w = ring[BLOCK0["ukv"] % 2][:, 0:2 * D].rearrange("p (k m) -> p k m", k=2)
            for c in range(4):
                chunk_pe(pe, "uq", 8 + c, [w[:, k, tile(c)] for k in range(2)], [ckvT[:, k, :] for k in range(2)])
            for t in range(T):
                chunk_pe(pe, "uq", 12 + t, [ckvT[:, k, tile(t)] for k in range(2)], [w[:, k, 512:1024] for k in range(2)])
            fence(pe, "pe")
            mla.pe(pe)
            fence(pe, "pe")
            block_arrived(pe, BLOCK0["om"])
            w = ring[BLOCK0["om"] % 2][:, :].rearrange("p (k m) -> p k m", k=4)
            for m in range(8):
                chunk_pe(pe, "on", 8 + m, [w[:, k, tile(m)] for k in range(4)], [omT[:, k, :] for k in range(4)])
            layer_pe(pe, "out1", 2, KD, lambda k: yT[:, k, :], pre=lambda k: pe.wait_ge(y_tmp, k + 1),
                     after=lambda j: norm_after(pe, "mid", j))
            norm_after(pe, "mid", 8)
            norm_after(pe, "mid", 9)
            layer_pe_loop(pe, "fc1", 8, KD, lambda k: hT[:, k, :], pre=lambda k: normed(pe, "mid", k))
            fence(pe, "pe")
            layer_pe(pe, "fc2", 8, 32, lambda k: aT[:, k, :], after=lambda j: norm_after(pe, "fin", j))
            norm_after(pe, "fin", 8)
            norm_after(pe, "fin", 9)
            for n in range(12, 18):
                ada_take(pe, n)
            norm_pe(pe, "n1", KD)
            for n in range(18, 24):
                ada_take(pe, n)
            name = "in2a"
            for n in range(5):
                g = BLOCK0[name] + n
                block_arrived(pe, g)
                w = ring[g % 2][:, :].rearrange("p (k m) -> p k m", k=KD)
                for m in range(1 if n == 2 else 4):
                    j = 4 * n + m - (3 if n > 2 else 0)
                    if n == 3:
                        chunk_pe(pe, name, j, [hT[:, k, tile(m)] for k in range(KD)], [w[:, k, :] for k in range(KD)])
                    else:
                        chunk_pe(pe, name, j, [w[:, k, tile(m)] for k in range(KD)], [hT[:, k, :] for k in range(KD)],
                                 pre=(lambda k: normed(pe, "n1", k)) if j == 0 else None)
                    if j == 14:
                        pe.wait_ge(gr, 1)
                        for h in range(MH):
                            ins = pe.matmul(PS[:, 2 + h, :], const("sel", slice(0, 4))[:, tile(h)], grow[0:4, 4, :],
                                            start=True, stop=True)
                        ins.then_inc(gr_pe, 1)
                    if j == 15:
                        pe.wait_ge(gr_act, 3)
                        for t in range(T):
                            pe.transpose(PS[:, 6, 8 * t:8 * t + 4], grow[0:4, 6, tile(t)], ident[0:4, 0:4])
                            ins = pe.transpose(PS[:, 6, 8 * t + 4:8 * t + 8], grow[0:4, 7, tile(t)], ident[0:4, 0:4])
                        ins.then_inc(gr_pe, 1)
            fence(pe, "pe")
            mls.pe(pe)
            fence(pe, "pe")
            dif.pe(pe)
            fence(pe, "pe")
            for j in range(8):
                w = ring[(BLOCK0["out2"] + j // 4) % 2][:, :].rearrange("p (k m) -> p k m", k=KD)
                chunk_pe(pe, "out2", 8 + j, [w[:, k, tile(j % 4)] for k in range(4, KD)], [catT[:, k, :] for k in range(4, KD)])
                norm_after(pe, "n2", j)
            norm_after(pe, "n2", 8)
            norm_after(pe, "n2", 9)
            normed(pe, "n2", KD - 1)
            pe.wait_ge(sk_loaded, 16)

            def sub_scores(t, c):
                h = c // 2
                o = PS[:, 2 + h % 4, tile(2 * (h // 4) + c % 2)]
                return pe.matmul(o, pqt[:, c, tile(t)], skw[:, c, :], start=True, stop=True)

            def turn(src, t, half, b):
                for c in range(4):
                    ins = pe.transpose(PS[:, b, tile(c)], src[:, 4 * half + c, tile(t)], ident)
                return ins

            def turn_h2(b):
                if b >= 2:
                    pe.wait_ge(tt_ev, b - 1)
                turn(hT, b // 2, b % 2, 6 + b % 2).then_inc(tt_pe, 1)

            turn_h2(0)
            turn_h2(1)
            for j in range(20):
                n, m = j // 4, j % 4
                if j < 16:
                    g = BLOCK0["pqa"] + n
                    if m == 0:
                        block_arrived(pe, g)
                        w = ring[g % 2][:, :].rearrange("p (k m) -> p k m", k=KD)
                    chunk_pe(pe, "pqa", j, [w[:, k, tile(m)] for k in range(KD)], [hT[:, k, 0:256] for k in range(KD)], n=256)
                if 3 <= j < 19 and j % 2 == 1:
                    pe.wait_ge(evac, EV0["pqa"] + j - 1)
                    sub_scores(0, j - 3)
                    sub_scores(0, j - 2).then_inc(sk_done, 1)
            turn_h2(2)
            turn_h2(3)
            pe.wait_ge(tt_ev, 4)
            for k in range(KD):
                ins = pe.matmul(PS[:, 6 + k // 4, tile(k % 4)], modc2[:, 40 + k:41 + k].to_broadcast([P, P]), ident,
                                start=True, stop=True)
            ins.then_inc(g2_pe, 1)

            def scores_of(t):
                pe.wait_ge(pk_ev, PH - 1 + t)
                for c in range(16):
                    ins = sub_scores(t, c)
                ins.then_inc(sk_done, 1)

            scores_of(1)
            layer_pe_loop(pe, "pqb", 4, KD, lambda k: hT[:, k, 256:512], n=256)
            pe.wait_ge(evac, EV0["pqb"] + 16)
            scores_of(2)
            for t in range(T):
                if t > 0:
                    pe.wait_ge(tile_read, t)
                    if t + 1 < T:
                        for half in range(2):
                            ins = turn(hT, t + 1, half, half)
                        ins.then_inc(tt_pe, 1)
                        pe.wait_ge(tt_ev, 4 + t)
                for half in range(2):
                    ins = turn(xT, t, half, half)
                ins.then_inc(x_turned, 1)
                if t == 0:
                    pe.wait_ge(g2_ev, 1)
                    pe.wait_ge(zero_ok, 1)
                for b in range(2):
                    pe.matmul(bank(6 + b), zeros, xT[:, b, :], start=True, stop=False)
                for r in range(NSLOT // GRP):
                    for q, (slot, worth) in enumerate(V_PE):
                        n = (t * (NSLOT // GRP) + r) * len(V_PE) + q
                        pe.wait_ge(diag_ok, n + 1)
                        pe.wait_ge(u_land[slot], 16 * ((2 * t + 1) * (NSLOT // GRP) + r + 1))
                        for b in range(2):
                            ins = pe.matmul(bank(6 + b), diag[:, n % 9, :], ubuf[:, slot, b * 512:(b + 1) * 512],
                                            start=False, stop=False)
                        ins.then_inc(pe_used, worth)
                for b in range(2):
                    ins = pe.matmul(bank(6 + b), zeros, xT[:, b, :], start=False, stop=True)
                ins.then_inc(v_sum, 1)
                if t == 0:
                    scores_of(3)

        @block.scalar
        def _(act):
            own = Own(act, act_own)
            for dst, src in ((prm[:, :], ap["params"]), (xT[:, :, :], ap["xT"]), (cst[:, :], ap["consts"])):
                act.dma_start(dst, src).then_inc(loaded, 16)
            act.wait_ge(loaded, 48)
            act.activation(scl[:, 8:16], prow("c2"), ACT.Silu).then_inc(silu_c, 1)
            norm_act(act, "x", lambda c: xT[:, c, :], KD, lambda c: hT[:, c, :], lambda c: modc[:, c:c + 1])
            for dst, src in ((alibi, ap["alibi"]), (biasc, ap["biasc"])):
                act.dma_start(dst, src).then_inc(tables, 16)
            n = "in1"
            for j in range(18):
                act.wait_ge(mm_done, MM0[n] + j + 1)
                if j < 14:
                    act.activation(zT[:, j, :], bank(j % 2), ACT.Copy).then_inc(evac, 1)
                else:
                    act.activation(vtok[:, j - 14, :], bank(j % 2, 256), ACT.Copy).then_inc(evac, 1)
                if j == 13:
                    norm_act(act, "cq", lambda c: zT[:, 8 + c, :], 3)
                if j == 14:
                    norm_act(act, "ckv", lambda c: zT[:, 11 + c, :], 2)
                if j == 15:
                    act.wait_ge(nrm_mm, NORM0["mid"][0])
                    act.activation(sq[0:24, 0, :], zT[0:24, 13, :], ACT.Sigmoid).then_inc(g_sig, 1)
                if j == 16:
                    act.wait_ge(g_turn, 1)
                    act.activation(gtok, PS[:, 6, 0:96], ACT.Copy)
            fence(act, "act")
            for r in range(2):
                act.wait_ge(c_pe, 1 + r)
                act.wait_ge(c_mm, r) if r else None
                for hc in range(2):
                    act.activation(hid[:, hc * 62:(hc + 1) * 62], PS[:, 2 * r + hc, 0:2 * NC], ACT.Silu,
                                   bias=hb[:, hc:hc + 1]).then_inc(c_hid, 1)
            fence(act, "act")
            nsa.act(act)
            fence(act, "act")
            with act.Fori(0, 2) as i:
                for j in range(8):
                    g = gT[:, bass.ds(i * 8 + j, 1), :].rearrange("p a n -> p (a n)")
                    act.activation(g, g, ACT.Sigmoid).then_inc(gt_sig, 1)
            fence(act, "act")
            mla.act(act)
            fence(act, "act")
            norm_act(act, "mid", lambda c: xT[:, c, :], KD, lambda c: hT[:, c, :], lambda c: modc[:, 24 + c:25 + c],
                     ready=lambda c: act.wait_ge(evac, EV0["out1"] + c + 1))
            with act.Fori(0, 4) as i:
                for j in range(8):
                    act.wait_ge(evac, i * 8 + (EV0["fc1"] + j + 1))
                    act.activation(aT[:, bass.ds(i * 8 + j, 1), :].rearrange("p a n -> p (a n)"), rbuf[:, j % 2, :],
                                   ACT.Square).then_inc(fc_sq, 1)
            fence(act, "act")
            norm_act(act, "fin", lambda c: xT[:, c, :], KD, ready=lambda c: act.wait_ge(evac, EV0["fc2"] + c + 1))
            norm_act(act, "n1", lambda c: xT[:, c, :], KD, lambda c: hT[:, c, :], lambda c: modc2[:, c:c + 1],
                     ready=lambda c: act.wait_ge(nrm_h, NORM0["fin"][0] + c + 1))
            n = "in2a"
            for j in range(17):
                act.wait_ge(mm_done, MM0[n] + j + 1)
                if j < 8:
                    ins = act.activation(uT[:, j, 3:S + 3], bank(j % 2), ACT.Copy)
                elif j == 8:
                    ins = act.activation(zG, bank(j % 2), ACT.Copy)
                elif j < 13:
                    ins = act.activation(mv[:, j - 9, :], bank(j % 2), ACT.Copy)
                else:
                    ins = act.activation(mo[:, j - 13, :], bank(j % 2), ACT.Sigmoid)
                ins.then_inc(evac, 1)
                if 3 <= j < 11:
                    c = j - 3
                    act.wait_ge(cv_sum, c + 1)
                    act.activation(qk2[:, c, :], qk2[:, c, :], ACT.Silu, bias=prow("convb", c, c + 1))
                if j == 11:
                    act.wait_ge(gr_x, 1)
                    own(act.activation(grow[32:36, 1, :], grow[32:36, 1, :], ACT.Exp))
                    act.activation(grow[32:36, 1, :], grow[32:36, 1, :], ACT.Ln, bias=1.0).then_inc(gr_act, 1)
                if j == 12:
                    act.wait_ge(gr, 1)
                    act.activation(grow[0:4, 6, :], grow[0:4, 5, :], ACT.Copy, scale=-1.0).then_inc(gr_act, 1)
                    act.activation(grow[0:4, 7, :], grow[0:4, 3, :], ACT.Exp, scale=-1.0).then_inc(gr_act, 1)
                    act.wait_ge(lam_s, 1)
                    act.activation(lamc[:, 2:4], lamc[:, 0:2], ACT.Exp).then_inc(lam_e, 1)
                if j == 15:
                    act.wait_ge(gr_pe, 1)
                    act.activation(abc, PS[:, 2:6, :], ACT.Copy).then_inc(gr_act, 1)
                    act.wait_ge(gr_pe, 2)
                    act.activation(tok8, PS[:, 6, 0:32], ACT.Copy)
            fence(act, "act")
            mls.act(act)
            fence(act, "act")
            dif.act(act)
            fence(act, "act")
            act.dma_start(skw, ap["subkeys"]).then_inc(sk_loaded, 16)
            act.dma_start(fgrow, ap["fgrow"]).then_inc(g2_ev, 16)
            norm_act(act, "n2", lambda c: xT[:, c, :], KD, lambda c: hT[:, c, :], lambda c: modc2[:, 24 + c:25 + c],
                     ready=lambda c: act.wait_ge(evac, EV0["out2"] + 8 + c + 1))
            def copy_h2(b):
                act.wait_ge(tt_pe, b + 1)
                act.activation(h2tok[:, b // 2, (b % 2) * 512:(b % 2 + 1) * 512], bank(6 + b % 2), ACT.Copy).then_inc(tt_ev, 1)

            copy_h2(0)
            copy_h2(1)
            for j in range(20):
                if j < 16:
                    act.wait_ge(mm_done, MM0["pqa"] + j + 1)
                    act.activation(pqt[:, j, 0:256], bank(j % 2, 256), ACT.Copy).then_inc(evac, 1)
                if j >= 4 and j % 2 == 0:
                    h = (j - 4) // 2
                    act.wait_ge(sk_done, h + 1)
                    act.activation(sc[:, 2 * h:2 * h + 2, :].rearrange("p a n -> p (a n)"),
                                   PS[:, 2 + h % 4, (h // 4) * 256:(h // 4 + 1) * 256], ACT.Copy).then_inc(pk_ev, 1)
            copy_h2(2)
            copy_h2(3)
            act.wait_ge(g2_pe, 1)
            act.activation(g2row[:, :, :], PS[:, 6:8, :], ACT.Copy).then_inc(g2_ev, 1)

            def copy_scores(t):
                act.wait_ge(sk_done, PH + t)
                act.wait_ge(pk_top, t)
                act.activation(sc.rearrange("p (a b c) n -> p b a (c n)", a=2, b=4),
                               PS[:, 2:6, :].rearrange("p b (a n) -> p b a n", a=2), ACT.Copy).then_inc(pk_ev, 1)

            with act.Fori(0, 2) as i:
                for j in range(8):
                    act.wait_ge(mm_done, i * 8 + (MM0["pqb"] + j + 1))
                    act.activation(pqt[:, bass.ds(i * 8 + j, 1), 256:512].rearrange("p a n -> p (a n)"), bank(j % 2, 256),
                                   ACT.Copy).then_inc(evac, 1)
            copy_scores(1)
            act.wait_ge(pk_mx, 1)
            act.activation(gate[:, 0, :], gate[:, 0, :], ACT.Exp).then_inc(pk_ex, 1)
            for t in range(T):
                if 0 < t < T - 1:
                    act.wait_ge(tt_pe, 4 + t)
                    act.activation(h2tok[:, (t + 1) % 2, :].rearrange("p (a n) -> p a n", a=2), PS[:, 0:2, :],
                                   ACT.Copy).then_inc(tt_ev, 1)
                act.wait_ge(dot_cp, NSLOT // GRP * (t + 1) + 1)
                act.activation(dots, dots, ACT.Gelu).then_inc(gl_done, 1)
                act.wait_ge(wexp_ok, t + 1)
                for r in range(NSLOT // GRP):
                    for q, (slot, worth) in enumerate(V_PE):
                        rnd = t * (NSLOT // GRP) + r
                        n = rnd * len(V_PE) + q
                        if rnd >= 3:
                            act.wait_ge(pe_used, GRP * (rnd - 2) + sum(w for _, w in V_PE[:q + 1]))
                        e = r * GRP + slot
                        act.activation(diag[:, n % 9, :], ident, ACT.Copy, scale=wexp[:, t, e:e + 1]).then_inc(diag_ok, 1)
                    if r == 14 and t < T - 2:
                        copy_scores(t + 2)
                if t < T - 1:
                    act.wait_ge(pk_mx, t + 2)
                    act.activation(gate[:, t + 1, :], gate[:, t + 1, :], ACT.Exp).then_inc(pk_ex, 1)
                act.wait_ge(fin_ms, t + 1)
                act.activation(ssf[:, 0:1], ssf[:, 0:1], ACT.Sqrt).then_inc(fin_rt, 1)

        @block.vector
        def _(dve):
            own = Own(dve, dve_own)
            dve.memset(ones[:, :], 1.0).then_inc(ready, 1)
            dve.wait_ge(loaded, 48)
            for n in range(4):
                ada_sum(dve, own, n, lambda k: prow("c", k, k + 1))
            ada_bias(dve, own, modc, 0, 4, prow("b_ada"))
            own(dve.scalar_tensor_tensor(out=scl[:, 0:8], in0=modc[:, 8:16], scalar=1.0, in1=prow("g_mix"),
                                         op0=ALU.add, op1=ALU.mult))
            norm_dve(dve, own, "x", lambda c: xT[:, c, :], KD, lambda c: hT[:, c, :], lambda c: scl[:, c:c + 1])
            for n in range(4, 12):
                ada_sum(dve, own, n, lambda k: prow("c", k, k + 1))
            ada_bias(dve, own, modc, 4, 12, prow("b_ada"))
            dve.wait_ge(evac, EV0["in1"] + 8)
            for r in range(2):
                src = zT[:, 6 + r, :]
                for g in range(NG):
                    dve.tensor_copy(stk[r][0:64, g, :], src[g * DH:(g + 1) * DH, :]).then_inc(c_stk, 1)
                    dve.tensor_copy(stk[r][64:128, g, 0:S - 1], src[g * DH:(g + 1) * DH, 1:S]).then_inc(c_stk, 1)
                own(dve.memset(stk[r][:, 2, :], 0.0))
                dve.tensor_copy(stk[r][:, 2, 0:32:2], prow("pek" if r == 0 else "pev")).then_inc(c_stk, 1)
            norm_dve(dve, own, "cq", lambda c: zT[:, 8 + c, :], 3, lambda c: cqT[:, c, :], lambda c: prow("g_cq", c, c + 1))
            norm_dve(dve, own, "ckv", lambda c: zT[:, 11 + c, :], 2, lambda c: ckvT[:, c, :], lambda c: prow("g_ckv", c, c + 1))
            fence(dve, "dve")
            for r in range(2):
                dve.wait_ge(mm_done, MM0["ck"] + r + 1)
                if r:
                    dve.wait_ge(c_hid, 2)
                dve.tensor_copy(hb, PS[:, 2 * r:2 * r + 2, 2 * NC]).then_inc(c_pe, 1)
                dve.wait_ge(c_mm, r + 1)
                if r == 0:
                    own(dve.tensor_copy(kcT, PS[:, 0, 128:128 + NC]))
                else:
                    own(dve.tensor_copy(vcm[0:NC, :], PS[0:NC, 1, 128:256]))
            fence(dve, "dve")
            dve.wait_ge(tables, 32)
            nsa.dve(dve, own)
            fence(dve, "dve")
            rope_k, rope_s = slice(64, 96), slice(96, 128)

            def rotate(src, dst):
                own(dve.tensor_tensor(rt[rope_k, 0, :], src[rope_k, :], const("rope", rope_k), ALU.mult))
                own(dve.tensor_tensor(rt[rope_k, 1, :], src[rope_s, :], const("rope", rope_s), ALU.mult))
                return dve.tensor_tensor(dst, rt[rope_k, 0, :], rt[rope_k, 1, :], ALU.add)

            own(rotate(zT[:, 13, :], km[rope_k, 0, :]))
            own(dve.tensor_copy(km[rope_k, 1:8, :], km[rope_k, 0:1, :].to_broadcast([32, 7, S])))
            for j in range(16):
                dve.wait_ge(mm_done, MM0["uq"] + j + 1)
                b = bank(j % 2)
                if j < 8:
                    own(dve.tensor_copy(qm[0:64, j, :], b[0:64, :]))
                    ins = rotate(b, qm[rope_k, j, :])
                elif j < 12:
                    own(dve.tensor_copy(km[0:64, 2 * (j - 8), :], b[0:64, :]))
                    ins = dve.tensor_copy(km[0:64, 2 * (j - 8) + 1, :], b[64:128, :])
                else:
                    ins = dve.tensor_copy(vm[:, j - 12, :], b)
                ins.then_inc(evac, 1)
            fence(dve, "dve")
            mla.dve(dve, own)
            fence(dve, "dve")
            for j in range(8, 16):
                dve.wait_ge(mm_done, MM0["on"] + j + 1)
                if j >= 10:
                    dve.wait_ge(y_tmp, j - 9)
                dve.tensor_tensor(ytmp[:, j % 2, :], gT[:, j, :], bank(j % 2), ALU.mult).then_inc(evac, 1)
                dve.wait_ge(evac, EV0["on"] + j + 1)
                dve.tensor_tensor(yT[:, j - 8, :], gT[:, j - 8, :], ytmp[:, j % 2, :], ALU.add).then_inc(y_tmp, 1)

            def residual(name, mod, gcol, before=None, done=0):
                for j in range(8):
                    if before is not None:
                        before(j)
                    dve.wait_ge(mm_done, MM0[name] + done + j + 1)
                    dve.scalar_tensor_tensor(out=xT[:, j, :], in0=bank(j % 2), scalar=mod[:, gcol + j:gcol + j + 1],
                                             in1=xT[:, j, :], op0=ALU.mult, op1=ALU.add).then_inc(evac, 1)

            residual("out1", modc, 16)
            own(dve.scalar_tensor_tensor(out=scl[:, 0:8], in0=modc[:, 32:40], scalar=1.0, in1=prow("g_mlp"),
                                         op0=ALU.add, op1=ALU.mult))
            norm_dve(dve, own, "mid", lambda c: xT[:, c, :], KD, lambda c: hT[:, c, :], lambda c: scl[:, c:c + 1])
            for j in range(2):
                dve.memset(rbuf[:, j, :], 0.0).then_inc(fc_sq, 1)
            dve.wait_ge(fc_sq, 2)
            with dve.Fori(0, 4) as i:
                for j in range(8):
                    dve.wait_ge(mm_done, i * 8 + (MM0["fc1"] + j + 1))
                    dve.wait_ge(fc_sq, i * 8 + (j + 1))
                    dve.tensor_scalar(rbuf[:, j % 2, :], bank(j % 2), 0.0, None, ALU.max).then_inc(evac, 1)
            fence(dve, "dve")
            def second_ada(j):
                for n in ((12 + 2 * j, 13 + 2 * j) if j < 4 else (16 + j,)):
                    ada_sum(dve, own, n, lambda k: scl[:, 8 + k:9 + k])

            dve.wait_ge(silu_c, 1)
            residual("fc2", modc, 40, second_ada)
            norm_dve(dve, own, "fin", lambda c: xT[:, c, :], KD, lambda c: xT[:, c, :], lambda c: prow("g_final", c, c + 1))
            ada_bias(dve, own, modc2, 12, 16, prow("ada_b2"))
            own(dve.scalar_tensor_tensor(out=scl[:, 0:8], in0=modc2[:, 8:16], scalar=1.0, in1=prow("n1g"),
                                         op0=ALU.add, op1=ALU.mult))
            norm_dve(dve, own, "n1", lambda c: xT[:, c, :], KD, lambda c: hT[:, c, :], lambda c: scl[:, c:c + 1])
            ada_bias(dve, own, modc2, 16, 24, prow("ada_b2"))
            own(dve.memset(uT[:, :, 0:3], 0.0))
            for c in range(8):
                dve.wait_ge(evac, EV0["in2a"] + c + 1)
                for j in range(4):
                    wj = prow("convw", 4 * c + j, 4 * c + j + 1)
                    src = uT[:, c, j:j + S]
                    if j == 0:
                        own(dve.tensor_scalar(qk2[:, c, :], src, wj, None, ALU.mult))
                    else:
                        ins = dve.scalar_tensor_tensor(out=qk2[:, c, :], in0=src, scalar=wj, in1=qk2[:, c, :],
                                                       op0=ALU.mult, op1=ALU.add)
                        if j < 3:
                            own(ins)
                ins.then_inc(cv_sum, 1)
            dve.wait_ge(evac, EV0["in2a"] + 9)
            f = slice(32, 36)
            own(dve.tensor_scalar(grow[f, 0, :], zG[f, :], prow("gb_f", rows=f), None, ALU.add))
            own(dve.tensor_scalar(grow[f, 1, :], grow[f, 0, :], -1.0, None, ALU.mult))
            own(dve.tensor_scalar(grow[f, 2, :], grow[f, 0, :], 0.0, None, ALU.min))
            dve.tensor_tensor(grow[f, 1, :], grow[f, 1, :], grow[f, 0, :], ALU.min).then_inc(gr_x, 1)
            dve.wait_ge(gr_act, 1)
            r4 = slice(0, 4)
            own(dve.tensor_tensor(grow[r4, 0, :], grow[f, 2, :], grow[f, 1, :], ALU.subtract))
            own(dve.memset(grow[r4, 1, :], 1.0))
            own(dve.tensor_tensor_scan(grow[r4, 2, :], grow[r4, 1, :], grow[r4, 0, :], 0.0, ALU.mult, ALU.add))
            own(dve.scalar_tensor_tensor(out=grow[r4, 4, :], in0=zG[r4, :], scalar=prow("gb_i", rows=r4), in1=grow[r4, 2, :],
                                         op0=ALU.add, op1=ALU.subtract))
            own(dve.memset(grow[r4, 1, :], 0.0))
            own(dve.tensor_tensor_scan(grow[r4, 5, :], grow[r4, 4, :], grow[r4, 1, :], 0.0, ALU.max, ALU.add))
            dve.tensor_tensor(grow[r4, 3, :], grow[r4, 2, :], grow[r4, 5, :], ALU.add).then_inc(gr, 1)
            for a in range(2):
                own(dve.tensor_tensor_reduce(otmp[:, 0:64], prow("lam", 128 * a, 128 * a + 64), prow("lam", 128 * a + 64, 128 * a + 128),
                                             1.0, 0.0, ALU.mult, ALU.add, lamc[:, a:a + 1]))
            dve.tensor_scalar(lamc[:, 5:6], lamc[:, 0:1], 1.0, None, ALU.mult).then_inc(lam_s, 1)
            dve.wait_ge(lam_e, 1)
            own(dve.tensor_tensor(lamc[:, 6:7], lamc[:, 2:3], lamc[:, 3:4], ALU.subtract))
            own(dve.tensor_scalar(lamc[:, 4:5], lamc[:, 6:7], 0.2, None, ALU.add))
            dve.wait_ge(gr_act, 4)
            for h in range(MH):
                own(dve.tensor_tensor(abcm[:, h, :].rearrange("p (t s) -> p t s", t=T), abc[:, h, :].rearrange("p (t s) -> p t s", t=T),
                                      mask[:, 3 * P:].unsqueeze(1).to_broadcast([P, T, P]), ALU.add))
            fence(dve, "dve")
            mls.dve(dve, own)
            fence(dve, "dve")
            dif.dve(dve, own)
            fence(dve, "dve")
            residual("out2", modc2, 16, done=8)
            own(dve.scalar_tensor_tensor(out=scl[:, 0:8], in0=modc2[:, 32:40], scalar=1.0, in1=prow("n2g"),
                                         op0=ALU.add, op1=ALU.mult))
            norm_dve(dve, own, "n2", lambda c: xT[:, c, :], KD, lambda c: hT[:, c, :], lambda c: scl[:, c:c + 1])
            dve.wait_ge(nrm_h, NORM0["n2"][0] + KD)
            dve.memset(zeros, 0.0).then_inc(zero_ok, 1)

            def top16(src, val, idx):
                own(dve.max(val[:, 0:8], src))
                own(dve.max_index(idx[:, 0:8], val[:, 0:8], src))
                own(dve.match_replace(src, val[:, 0:8], src, -3e38))
                own(dve.max(val[:, 8:16], src))
                own(dve.max_index(idx[:, 8:16], val[:, 8:16], src))


            def pick_keys(t, h):
                dve.wait_ge(pk_ev, h + 1 if t == 0 else PH + t)
                c0, c1 = 2 * h, 2 * h + 1
                for c in (c0, c1):
                    own.mark(dve.max(tkv[:, c, 0:8], sc[:, c, :]))
                dve.wait_ge(dve_own, own.n - 1)
                for c in (c0, c1):
                    own.mark(dve.max_index(tki[:, c, 0:8], tkv[:, c, 0:8], sc[:, c, :]))
                    dve.wait_ge(dve_own, own.n - 1)
                for c in (c0, c1):
                    own.mark(dve.match_replace(sc[:, c, :], tkv[:, c, 0:8], sc[:, c, :], -3e38))
                    dve.wait_ge(dve_own, own.n - 1)
                for c in (c0, c1):
                    own.mark(dve.max(tkv[:, c, 8:16], sc[:, c, :]))
                    dve.wait_ge(dve_own, own.n - 1)
                for c in (c0, c1):
                    own.mark(dve.max_index(tki[:, c, 8:16], tkv[:, c, 8:16], sc[:, c, :]))
                    dve.wait_ge(dve_own, own.n - (1 if c == c0 else 0))
                if h == PH - 1:
                    dve.sem_inc(pk_top, 1)

            def pick_pairs(t, h):
                own(dve.tensor_tensor(cand.rearrange("p (a b) -> p a b", a=PK),
                                      tkv[:, 2 * h, :].unsqueeze(2).to_broadcast([P, PK, PK]),
                                      tkv[:, 2 * h + 1, :].unsqueeze(1).to_broadcast([P, PK, PK]), ALU.add))
                top16(cand, fval[:, PK * h:PK * h + PK], fpos[:, PK * h:PK * h + PK])

            def pick_experts(t, h):
                s16 = slice(PK * h, PK * h + PK)
                own.mark(dve.tensor_scalar(fpi[:, 0, :], fpos[:, s16], 4, None, ALU.logical_shift_right))
                own(dve.tensor_scalar(fpi[:, 1, :], fpos[:, s16], 15, None, ALU.bitwise_and))
                own.mark(dve.tensor_copy(fpf, fpi))
                own(dve.tensor_copy(tkf, tki[:, 2 * h:2 * h + 2, :]))
                own(dve.tensor_tensor(oneh, fpf.unsqueeze(3).to_broadcast([P, 2, PK, PK]),
                                      const("iota").unsqueeze(1).unsqueeze(1).to_broadcast([P, 2, PK, PK]), ALU.is_equal))
                own(dve.tensor_tensor(oneh, oneh, tkf.unsqueeze(2).to_broadcast([P, 2, PK, PK]), ALU.mult))
                own(dve.tensor_reduce(selv, oneh, AXX, ALU.add))
                own(dve.scalar_tensor_tensor(out=exf, in0=selv[:, 0, :], scalar=float(NKEY), in1=selv[:, 1, :],
                                             op0=ALU.mult, op1=ALU.add))
                dve.tensor_copy(eidx[:, t, s16], exf).then_inc(experts_ok, 1)
                dve.wait_ge(experts_ok, PH * t + h + 1)

            def gate_scores(t):
                f3 = fval.rearrange("p (h k) -> p h k", h=PH)
                g3 = gate[:, t, :].rearrange("p (h k) -> p h k", h=PH)
                dve.tensor_tensor(g3, f3, f3[:, :, 0:1].to_broadcast([P, PH, PK]), ALU.subtract).then_inc(pk_mx, 1)

            def pick_gates(t):
                g3 = gate[:, t, :].rearrange("p (h k) -> p h k", h=PH)
                dve.wait_ge(pk_ex, t + 1)
                own(dve.tensor_reduce(sm8[:, 0, :], g3, AXX, ALU.add))
                own(dve.reciprocal(sm8[:, 1, :], sm8[:, 0, :]))
                dve.tensor_tensor(g3, g3, sm8[:, 1, :].unsqueeze(2).to_broadcast([P, PH, PK]), ALU.mult).then_inc(top_done, 1)
                dve.wait_ge(top_done, t + 1)

            NI = NSLOT // GRP

            def pick(t, piece):
                if piece < 3 * PH:
                    (pick_keys, pick_pairs, pick_experts)[piece % 3](t, piece // 3)
                elif piece == 3 * PH:
                    gate_scores(t)

            dve.sem_inc(u_used, GRP)
            dve.sem_inc(pe_used, GRP)
            dve.sem_inc(dot_cp, 1)

            def dot_round(t, i, between=None):
                base = 2 * t * NI
                for j in range(GRP):
                    dve.wait_ge(u_land[j], i * 16 + 16 * (base + 1))
                    if j == 0 and between is None:
                        dve.wait_ge(dot_cp, i + (NI * t + 1))
                    dot = dots8[:, j:j + 1] if between is None else dots[:, i * GRP + j:i * GRP + j + 1]
                    dve.tensor_tensor_reduce(ubuf[:, j, :], ubuf[:, j, :], h2tok[:, t % 2, :], 1.0, 0.0,
                                             ALU.mult, ALU.add, dot).then_inc(u_used, 1)
                    if between is not None and j % 4 == 2:
                        between(j // 4)
                if between is None:
                    dve.wait_ge(u_used, i * GRP + GRP * (base + 2))
                    dve.tensor_copy(dots[:, bass.ds(i * GRP, GRP)], dots8).then_inc(dot_cp, 1)

            for t in range(T):
                base = 2 * t * NI
                dve.wait_ge(tt_ev, (2, 4, 5, 6)[t])
                if t == 0:
                    for piece in range(3):
                        pick(0, piece)
                    for i in range(NI):
                        def next_head(half, i=i):
                            if (2 * i + half) % 4 < 3:
                                pick(0, 3 * (1 + i // 2) + (2 * i + half) % 4)
                        dot_round(0, i, next_head)
                    dve.wait_ge(u_used, GRP * (NI + 1))
                    dve.sem_inc(dot_cp, NI)
                    pick_gates(0)
                else:
                    with dve.Fori(0, NI) as i:
                        dot_round(t, i)
                if t > 0:
                    dve.wait_ge(stored, 16 * t)
                own(dve.memset(acc, 0.0))
                dve.wait_ge(gl_done, t + 1)
                dve.tensor_tensor(wexp[:, t, :], dots, gate[:, t, :], ALU.mult).then_inc(wexp_ok, 1)
                dve.wait_ge(wexp_ok, t + 1)
                vb = base + NI
                for r in range(NI):
                    for q, (slot, worth) in enumerate(V_DVE):
                        dve.wait_ge(u_land[slot], 16 * (vb + r + 1))
                        dve.wait_ge(u_used, GRP * (vb + 1 + r) + (sum(w for _, w in V_DVE[:q - 1]) if q else -V_DVE[-1][1]))
                        e, k = r * GRP + slot, (r * len(V_DVE) + q) % 2
                        dve.scalar_tensor_tensor(out=acc[:, k, :], in0=ubuf[:, slot, :], scalar=wexp[:, t, e:e + 1],
                                                 in1=acc[:, k, :], op0=ALU.mult, op1=ALU.add).then_inc(u_used, worth)
                        if t < T - 1 and q in (1, 3):
                            pick(t + 1, 2 * r + q // 2)
                    if t < T - 1:
                        if r == 15:
                            pick_gates(t + 1)
                dve.wait_ge(u_used, GRP * (vb + NI + 1))
                if t == 0:
                    dve.wait_ge(g2_ev, 17)
                a0, a1 = acc[:, 0, :], acc[:, 1, :]
                h0, g2 = a0.rearrange("p (a n) -> p a n", a=2), g2row[:, :, :]
                own(dve.tensor_tensor(a0, a0, a1, ALU.add))
                dve.wait_ge(v_sum, t + 1)
                own(dve.tensor_tensor(h0, h0, PS[:, 6:8, :], ALU.add))
                own(dve.tensor_tensor(h0, h0, g2, ALU.mult))
                dve.wait_ge(x_turned, t + 1)
                dve.tensor_tensor(h0, h0, PS[:, 0:2, :], ALU.add).then_inc(tile_read, 1)
                dve.wait_ge(tile_read, t + 1)
                own(dve.tensor_tensor_reduce(a1, a0, a0, 1.0, 0.0, ALU.mult, ALU.add, ssf[:, 1:2]))
                dve.tensor_scalar(ssf[:, 0:1], ssf[:, 1:2], 1.0 / D, EPS, ALU.mult, ALU.add).then_inc(fin_ms, 1)
                dve.wait_ge(fin_rt, t + 1)
                own(dve.reciprocal(ssf[:, 2:3], ssf[:, 0:1]))
                dve.scalar_tensor_tensor(out=a0, in0=a0, scalar=ssf[:, 2:3], in1=fgrow, op0=ALU.mult, op1=ALU.mult)\
                   .then_inc(fin_ok, 1)

        @block.gpsimd
        def _(pool):
            for n in range(24):
                if n == 12:
                    pool.wait_ge(stage_done, 3 * MIX_FENCE)
                if n >= 2:
                    pool.wait_ge(ada_summed, n - 1)
                pool.dma_start((adaw if n < 12 else adaw2)[n % 2], ap["ada"][n]).then_inc(ada_loaded[n % 2], 16)
            NI = NSLOT // GRP
            for ph in range(2 * T):
                t, table = ph // 2, ap["peer_u"] if ph % 2 == 0 else ap["peer_v"]
                if ph % 2 == 0:
                    pool.wait_ge(pe_used, GRP * (t * NI + 1))
                with pool.Fori(0, PH) as i:
                    if ph % 2 == 0:
                        pool.wait_ge(experts_ok, i + (PH * t + 1))
                        pool.sem_inc(pool_step, 1)
                    for rnd in range(2):
                        pool.tensor_copy(idx16[:, rnd * GRP:(rnd + 1) * GRP],
                                         eidx[:, t, bass.ds(i * (2 * GRP) + rnd * GRP, GRP)]).then_inc(idx_cp, 1)
                        pool.wait_ge(idx_cp, i * 2 + (NI * ph + rnd + 1))
                        pool.sem_inc(pool_step, 1)
                        for a in range(0, GRP, 2):
                            if ph % 2 == 1 and a != 4:
                                pool.wait_ge(pe_used, i * (2 * GRP) + (GRP * (NI * t + rnd) + a + 2))
                                pool.sem_inc(pool_step, 1)
                            pool.wait_ge(u_used, i * (2 * GRP) + (GRP * (NI * ph + rnd) + a + 2))
                            pool.sem_inc(pool_step, 1)
                            for j in (a, a + 1):
                                pool.indirect_dma_start(
                                    ubuf[:, j, :], None, table,
                                    bass.IndirectOffsetOnAxis(ap=idx16[:, rnd * GRP + j:rnd * GRP + j + 1], axis=0))\
                                    .then_inc(u_land[j], 16)


def lay_out(inp):
    f32 = np.float32
    w = {k: np.asarray(v) for k, v in inp.items()}
    w = {k: (v[0] if k not in ("g_final", "final_g_2") else v) for k, v in w.items()}

    def kparts(m, k):
        return m.reshape(k, P, m.shape[1]).transpose(1, 0, 2)

    def block(m, k):
        b = np.zeros((P, BLK), f32)
        b[:, :k * m.shape[1]] = kparts(m, k).reshape(P, -1)
        return b

    def blocks(m, k, width):
        return [block(m[:, i:i + width], k) for i in range(0, m.shape[1], width)]

    def swap(m):
        return np.concatenate([m[:, 16:32], m[:, 0:16]], axis=1)

    wi = w["w_in"]
    q, kc, vc, ks, vs, kw, vw, zg, qd, kvd, kr, ga, gb = np.split(
        wi, np.cumsum([512, 128, 128, 128, 128, 128, 128, 24, 384, 256, 32, D]).tolist(), axis=1)
    qch = [q[:, h * DH:(h + 1) * DH] for c in range(HG) for h in (c, HG + c)]
    in1 = np.concatenate(qch + [ks, kw, kc, vc, qd, kvd, zg, np.zeros((D, 40), f32), kr, swap(kr), vs, vw], axis=1)
    uq = w["w_uq"]
    uqh = []
    for h in range(8):
        m = uq[:, h * 96:(h + 1) * 96]
        uqh += [m, swap(m[:, 64:96])]
    mq, mk, mv, mo, mi, mf, dq, dk, dv = np.split(
        w["w_in_2"], np.cumsum([512, 512, 512, 512, 4, 4, 512, 512]).tolist(), axis=1)
    gates = np.concatenate([mi, np.zeros((D, 28), f32), mf, np.zeros((D, 476), f32)], axis=1)
    keys = w["peer_sub_keys_2"].transpose(3, 0, 1, 2).reshape(P, 16 * NKEY)
    ada = blocks(w["w_ada"], KD, 512) + blocks(w["ada_w_2"], KD, 512)
    stream = (
        blocks(in1, KD, 512) + [block(w["w_ck1"], 16), block(w["w_cv1"], 16)]
        + blocks(np.concatenate([ga, gb], axis=1), KD, 512)
        + [block(np.concatenate(uqh, axis=1), 3), block(np.concatenate([w["w_uk"], w["w_uv"]], axis=1), 2)]
        + [block(w["w_o_nsa"], 4), block(w["w_o_mla"], 4)] + blocks(w["w_out"], KD, 512)
        + blocks(w["w_fc1"], KD, 512) + blocks(w["w_fc2"], 32, P)
        + [block(m, KD) for m in (mq, mk, gates, mv, mo, dq, dk, dv)] + blocks(w["w_out_2"], KD, 512)
        + blocks(w["peer_w_query_2"], KD, 512))
    assert len(stream) == BLOCK0["pqb"]

    def cols(v):
        return v.reshape(-1, P).T

    def rows(v, at):
        a = np.zeros((P, 1), f32)
        a[at:at + len(v), 0] = v
        return a

    lam = np.concatenate([w["lambda_q1_2"], w["lambda_k1_2"], w["lambda_q2_2"], w["lambda_k2_2"]])
    params = dict(
        c=cols(w["c"]), b_ada=cols(w["b_ada"]), g_mix=cols(w["g_mix"]), g_mlp=cols(w["g_mlp"]), g_cq=cols(w["g_cq"]),
        g_ckv=cols(w["g_ckv"]), c2=cols(w["c_2"]), ada_b2=cols(w["ada_b_2"]), n1g=cols(w["norm1_g_2"]),
        n2g=cols(w["norm2_g_2"]), convw=w["conv_w_2"].reshape(4, 8, P).transpose(2, 1, 0).reshape(P, 32),
        convb=cols(w["conv_b_2"]), mng=cols(w["mlstm_norm_g_2"]), dng=cols(w["diff_norm_g_2"]),
        ck2=kparts(w["w_ck2"], 2).reshape(P, 128), cv2=kparts(w["w_cv2"], 2).reshape(P, 128),
        pek=w["pe_ck"].reshape(16, P).T, pev=w["pe_cv"].reshape(16, P).T,
        gb_i=rows(w["mlstm_gate_b_2"][:4], 0), gb_f=rows(w["mlstm_gate_b_2"][4:], 32),
        g_final=cols(w["g_final"]), lam=np.broadcast_to(lam, (P, 256)))
    return {
        "wstream": np.stack(stream), "ada": np.stack(ada), "params": np.concatenate([params[n] for n, _ in PARAMS], axis=1),
        "xT": w["x"].T.reshape(KD, P, S).transpose(1, 0, 2), "fgrow": np.broadcast_to(w["final_g_2"], (P, D)),
        "subkeys": keys.reshape(P, 16, NKEY), "peer_u": w["peer_u_2"], "peer_v": w["peer_v_2"],
    }


def shape_tables():
    f32 = np.float32
    p = np.arange(P)[:, None]
    back = p - (np.arange(S)[None, :] - (S - P))
    mask = np.where(back >= 0, 0.0, -BIG)
    slope = 2.0 ** -(np.arange(NH) + 1.0)
    alibi = np.where(back[:, None, :] >= 0, -8.0 * slope[None, :, None] * back[:, None, :], -BIG)
    t = np.arange(T)[None, :, None] * P + p[:, :, None]
    far = t - (np.arange(NC) * CMP_STRIDE + CMP_END0)[None, None, :]
    biasc = np.where(far[:, :, None, :] >= 0, -8.0 * slope[None, None, :, None] * far[:, :, None, :], -BIG)
    inv = (f32(10000.0) ** (-np.arange(16, dtype=f32) / f32(16))).astype(f32)
    ang = (np.arange(S, dtype=f32)[None, :] * inv[:, None]).astype(f32)
    rope = np.zeros((P, S))
    rope[64:80], rope[80:96] = np.cos(ang), np.cos(ang)
    rope[96:112], rope[112:128] = -np.sin(ang), np.sin(ang)
    sel = np.zeros((P, S))
    for h in range(4):
        sel[h, h * P:(h + 1) * P] = 1.0
    tab = dict(ident=np.eye(P), mask=mask, rope=rope, sel=sel, iota=np.broadcast_to(np.arange(PK), (P, PK)))
    return {"consts": np.concatenate([tab[n] for n, _ in CONSTS], axis=1).astype(f32), "alibi": alibi.astype(f32),
            "biasc": biasc.astype(f32)}


def kernel(**inputs):
    import concourse.bacc as bacc
    from concourse.bass_utils import run_bass_kernel_spmd

    nc = bacc.Bacc("TRN2", target_bir_lowering=False, num_devices=1)
    arrays = {k: np.ascontiguousarray(v) for k, v in {**lay_out(inputs), **shape_tables()}.items()}
    ap = {n: nc.dram_tensor("in_" + n, a.shape, mybir.dt.from_np(a.dtype), kind="ExternalInput").ap() for n, a in arrays.items()}
    out = nc.dram_tensor("result", (S, D), F32, kind="ExternalOutput").ap()
    build(nc, ap, out)
    r = run_bass_kernel_spmd(nc, [{"in_" + n: a for n, a in arrays.items()}], core_ids=[0])
    return r.results[0]["result"].reshape(1, S, D)
```
